# Optimizing a Trainium2 kernel written in Bass

```python
import math
import jax, jax.numpy as jnp
from jax import lax
import numpy as np

D_MODEL = 1024
BATCH = 1
SEQ = 256
DEPTH = 2

LRU_WIDTH = D_MODEL // 2
LRU_HEADS = 8
LRU_HEAD_DIM = LRU_WIDTH // LRU_HEADS
CONV_WIDTH = 4
LRU_C = 8.0
RWKV_WIDTH = D_MODEL // 2
RWKV_HEAD_DIM = 64
RWKV_HEADS = RWKV_WIDTH // RWKV_HEAD_DIM
DECAY_LORA = 64
AAA_LORA = 64
GATE_LORA = 128
RWKV_IN = 3 * RWKV_WIDTH + DECAY_LORA + AAA_LORA + GATE_LORA
EVEN_IN = 2 * LRU_WIDTH + RWKV_IN
GN_EPS = 64e-5
DIFF_HEAD_DIM = 64
DIFF_HEADS = D_MODEL // (2 * DIFF_HEAD_DIM)
DIFF_V_DIM = 2 * DIFF_HEAD_DIM
QKV_DIM = 2 * DIFF_HEADS * 2 * DIFF_HEAD_DIM + DIFF_HEADS * DIFF_V_DIM
ROPE_DIM = DIFF_HEAD_DIM // 4
ROPE_THETA = 500000.0
Q_BLOCK = 128
FFN_DIM = 2816
N_EXPERTS = 8
TOP_K = 2
EXPERT_DIM = 3584
RMS_EPS = 1e-6


F32 = jnp.float32

def rms_norm(x, g, eps=RMS_EPS):
    xf = x.astype(F32)
    y = xf * lax.rsqrt(jnp.mean(jnp.square(xf), axis=-1, keepdims=True) + eps)
    return (y * g.astype(F32)).astype(x.dtype)

def token_shift(x):
    return jnp.pad(x, ((0, 0), (1, 0), (0, 0)))[:, :-1]

def swiglu(x, wg, wu, wd):
    return (jax.nn.silu(x @ wg) * (x @ wu)) @ wd

def causal_dwconv(x, w, b):
    y = lax.conv_general_dilated(x, w[:, None, :].astype(x.dtype), window_strides=(1,),
                                 padding=[(CONV_WIDTH - 1, 0)],
                                 dimension_numbers=('NWC', 'WIO', 'NWC'),
                                 feature_group_count=x.shape[-1])
    return y + b

def rg_lru(x, wa, ba, wx, bx, lam):
    B, T, _ = x.shape
    xf = x.astype(F32)
    xh = xf.reshape(B, T, LRU_HEADS, LRU_HEAD_DIM)
    gate_a = jnp.einsum('bthi,hij->bthj', xh, wa.astype(F32)).reshape(B, T, LRU_WIDTH) + ba
    gate_x = jnp.einsum('bthi,hij->bthj', xh, wx.astype(F32)).reshape(B, T, LRU_WIDTH) + bx
    log_a = -LRU_C * jax.nn.sigmoid(gate_a) * jax.nn.softplus(-lam.astype(F32))
    a = jnp.exp(log_a)
    u = jnp.sqrt(-jnp.expm1(2.0 * log_a)) * jax.nn.sigmoid(gate_x) * xf

    def combine(l, r):
        return (l[0] * r[0], r[0] * l[1] + r[1])

    _, h = lax.associative_scan(combine, (a, u), axis=1)
    return h.astype(x.dtype)

def rwkv7_scan(r, w, k, v, kk, a):
    B, T, H, N = r.shape

    def step(S, inp):
        r_t, w_t, k_t, v_t, kk_t, a_t = inp
        sa = jnp.einsum('bhvk,bhk->bhv', S, -kk_t)
        S = S * w_t[:, :, None, :] + sa[..., None] * (kk_t * a_t)[:, :, None, :] \
            + v_t[..., None] * k_t[:, :, None, :]
        o = jnp.einsum('bhvk,bhk->bhv', S, r_t)
        return S, o

    xs = tuple(jnp.moveaxis(t, 1, 0) for t in (r, w, k, v, kk, a))
    S0 = jnp.zeros((B, H, N, N), F32)
    _, o = lax.scan(step, S0, xs)
    return jnp.moveaxis(o, 0, 1)

def rwkv7_mixer(p, mu, w0, w2, a0, a2, g2, k_k, k_a, r_k, gn_w, gn_b):
    B, T, _ = p.shape
    pf = p.astype(F32)
    ps = pf + (token_shift(pf) - pf) * mu
    idx = np.cumsum([RWKV_WIDTH, RWKV_WIDTH, RWKV_WIDTH, DECAY_LORA, AAA_LORA]).tolist()
    r, k, v, xw, xa, xg = jnp.split(ps, idx, axis=-1)
    wlog = -jax.nn.softplus(-(w0 + jnp.tanh(xw) @ w2)) - 0.5
    decay = jnp.exp(-jnp.exp(wlog))
    a = jax.nn.sigmoid(a0 + xa @ a2)
    g = jax.nn.sigmoid(xg) @ g2

    def hs(t):
        return t.reshape(B, T, RWKV_HEADS, RWKV_HEAD_DIM)

    kk = hs(k * k_k)
    kk = kk / jnp.maximum(jnp.linalg.norm(kk, axis=-1, keepdims=True), 1e-12)
    k = k * (1.0 + (a - 1.0) * k_a)
    rh, kh, vh = hs(r), hs(k), hs(v)
    o = rwkv7_scan(rh, hs(decay), kh, vh, kk, hs(a))
    mean = jnp.mean(o, axis=-1, keepdims=True)
    var = jnp.mean(jnp.square(o - mean), axis=-1, keepdims=True)
    on = ((o - mean) * lax.rsqrt(var + GN_EPS)).reshape(B, T, RWKV_WIDTH) * gn_w + gn_b
    bonus = (jnp.sum(rh * kh * r_k, axis=-1, keepdims=True) * vh).reshape(B, T, RWKV_WIDTH)
    return (on + bonus) * g

def even_mixer(xn, w_in, conv_w, conv_b, gate_a_w, gate_a_b, gate_x_w, gate_x_b, lru_lambda,
               shift_mu, w0, w2, a0, a2, g2, k_k, k_a, r_k, gn_w, gn_b, w_out):
    proj = xn @ w_in
    lru_x, lru_g, rw = jnp.split(proj, [LRU_WIDTH, 2 * LRU_WIDTH], axis=-1)
    h = rg_lru(causal_dwconv(lru_x, conv_w, conv_b), gate_a_w, gate_a_b, gate_x_w, gate_x_b, lru_lambda)
    y_lru = jax.nn.gelu(lru_g) * h
    y_rwkv = rwkv7_mixer(rw, shift_mu, w0, w2, a0, a2, g2, k_k, k_a, r_k, gn_w, gn_b)
    y = jnp.concatenate([y_lru, y_rwkv.astype(y_lru.dtype)], axis=-1)
    return y @ w_out

def partial_rope(x, positions):
    half = ROPE_DIM // 2
    inv_freq = ROPE_THETA ** (-jnp.arange(0, ROPE_DIM, 2, dtype=F32) / ROPE_DIM)
    ang = positions.astype(F32)[:, :, None] * inv_freq
    cos = jnp.cos(ang)[:, :, None, None, :]
    sin = jnp.sin(ang)[:, :, None, None, :]
    xf = x.astype(F32)
    x1 = xf[..., :half]
    x2 = xf[..., half:ROPE_DIM]
    out = jnp.concatenate([x1 * cos - x2 * sin, x2 * cos + x1 * sin, xf[..., ROPE_DIM:]], axis=-1)
    return out.astype(x.dtype)

def diff_attention(xn, positions, w_qkv, q_norm, k_norm, lq1, lk1, lq2, lk2, subln, w_o, lambda_init):
    B, T, _ = xn.shape
    qkv = xn @ w_qkv
    qd = DIFF_HEADS * 2 * DIFF_HEAD_DIM
    q, k, v = jnp.split(qkv, [qd, 2 * qd], axis=-1)
    q = q.reshape(B, T, DIFF_HEADS, 2, DIFF_HEAD_DIM)
    k = k.reshape(B, T, DIFF_HEADS, 2, DIFF_HEAD_DIM)
    v = v.reshape(B, T, DIFF_HEADS, DIFF_V_DIM).astype(F32)
    q = partial_rope(rms_norm(q, q_norm), positions)
    k = partial_rope(rms_norm(k, k_norm), positions)
    lam = jnp.exp(jnp.sum(lq1.astype(F32) * lk1.astype(F32))) \
        - jnp.exp(jnp.sum(lq2.astype(F32) * lk2.astype(F32))) + lambda_init
    n_blk = T // Q_BLOCK
    qb = jnp.moveaxis(q.reshape(B, n_blk, Q_BLOCK, DIFF_HEADS, 2, DIFF_HEAD_DIM), 1, 0)
    kpos = jnp.arange(T)
    scale = DIFF_HEAD_DIM ** -0.5

    def block(args):
        q_blk, bi = args
        s = jnp.einsum('bqhcd,bkhcd->bhcqk', q_blk, k, preferred_element_type=F32) * scale
        qpos = bi * Q_BLOCK + jnp.arange(Q_BLOCK)
        s = jnp.where(kpos[None, :] <= qpos[:, None], s, -jnp.inf)
        p = jax.nn.softmax(s, axis=-1)
        attn = p[:, :, 0] - lam * p[:, :, 1]
        return jnp.einsum('bhqk,bkhe->bqhe', attn, v)

    o = lax.map(block, (qb, jnp.arange(n_blk)))
    o = jnp.moveaxis(o, 0, 1).reshape(B, T, DIFF_HEADS, DIFF_V_DIM)
    o = rms_norm(o, subln) * (1.0 - lambda_init)
    return o.reshape(B, T, DIFF_HEADS * DIFF_V_DIM).astype(xn.dtype) @ w_o

def moe_swiglu(xn, router, wg, wu, wd):
    B, T, D = xn.shape
    xt = xn.reshape(B * T, D)
    logits = (xt @ router).astype(F32)
    topv, topi = lax.top_k(logits, TOP_K)
    gates = jax.nn.softmax(topv, axis=-1)
    combine = jnp.sum(jax.nn.one_hot(topi, N_EXPERTS, dtype=F32) * gates[..., None], axis=1)
    y = jnp.zeros((B * T, D), F32)
    for e in range(N_EXPERTS):
        y = y + combine[:, e:e + 1] * swiglu(xt, wg[e], wu[e], wd[e]).astype(F32)
    return y.reshape(B, T, D).astype(xn.dtype)

def first_inputs(seed: int = 0) -> dict:
    key = jax.random.key(seed)
    keys = jax.random.split(key, 64)
    counter = [0]

    def nk():
        kk = keys[counter[0]]
        counter[0] += 1
        return kk

    def nrm(shape, scale):
        return jax.random.normal(nk(), shape, F32) * scale

    def gain(shape):
        return 1.0 + nrm(shape, 0.02)

    ne = (DEPTH + 1) // 2
    no = DEPTH // 2
    D = D_MODEL
    x = jax.random.normal(nk(), (BATCH, SEQ, D), F32)
    positions = jnp.broadcast_to(jnp.arange(SEQ, dtype=jnp.int32), (BATCH, SEQ))
    u = jax.random.uniform(nk(), (ne, LRU_WIDTH), F32, 0.9, 0.999)
    s = u ** (1.0 / LRU_C)
    return {
        'x': x,
        'positions': positions,
        'e_ln_mix': gain((ne, D)),
        'e_w_in': nrm((ne, D, EVEN_IN), D ** -0.5),
        'e_conv_w': nrm((ne, CONV_WIDTH, LRU_WIDTH), CONV_WIDTH ** -0.5),
        'e_conv_b': nrm((ne, LRU_WIDTH), 0.01),
        'e_gate_a_w': nrm((ne, LRU_HEADS, LRU_HEAD_DIM, LRU_HEAD_DIM), LRU_HEAD_DIM ** -0.5),
        'e_gate_a_b': nrm((ne, LRU_WIDTH), 0.01),
        'e_gate_x_w': nrm((ne, LRU_HEADS, LRU_HEAD_DIM, LRU_HEAD_DIM), LRU_HEAD_DIM ** -0.5),
        'e_gate_x_b': nrm((ne, LRU_WIDTH), 0.01),
        'e_lru_lambda': jnp.log(s) - jnp.log1p(-s),
        'e_shift_mu': jax.random.uniform(nk(), (ne, RWKV_IN), F32),
        'e_w0': jax.random.uniform(nk(), (ne, RWKV_WIDTH), F32, -6.0, 1.0),
        'e_w2': nrm((ne, DECAY_LORA, RWKV_WIDTH), 0.1),
        'e_a0': nrm((ne, RWKV_WIDTH), 0.1),
        'e_a2': nrm((ne, AAA_LORA, RWKV_WIDTH), 0.1),
        'e_g2': nrm((ne, GATE_LORA, RWKV_WIDTH), GATE_LORA ** -0.5),
        'e_k_k': 0.85 + nrm((ne, RWKV_WIDTH), 0.02),
        'e_k_a': gain((ne, RWKV_WIDTH)),
        'e_r_k': nrm((ne, RWKV_HEADS, RWKV_HEAD_DIM), 0.1),
        'e_gn_w': gain((ne, RWKV_WIDTH)),
        'e_gn_b': nrm((ne, RWKV_WIDTH), 0.01),
        'e_w_out': nrm((ne, D, D), D ** -0.5),
        'e_ln_ffn': gain((ne, D)),
        'e_ffn_gate': nrm((ne, D, FFN_DIM), D ** -0.5),
        'e_ffn_up': nrm((ne, D, FFN_DIM), D ** -0.5),
        'e_ffn_down': nrm((ne, FFN_DIM, D), FFN_DIM ** -0.5),
        'o_ln_mix': gain((no, D)),
        'o_w_qkv': nrm((no, D, QKV_DIM), D ** -0.5),
        'o_q_norm': gain((no, DIFF_HEAD_DIM)),
        'o_k_norm': gain((no, DIFF_HEAD_DIM)),
        'o_lambda_q1': nrm((no, DIFF_HEAD_DIM), 0.1),
        'o_lambda_k1': nrm((no, DIFF_HEAD_DIM), 0.1),
        'o_lambda_q2': nrm((no, DIFF_HEAD_DIM), 0.1),
        'o_lambda_k2': nrm((no, DIFF_HEAD_DIM), 0.1),
        'o_subln': gain((no, DIFF_V_DIM)),
        'o_w_o': nrm((no, DIFF_HEADS * DIFF_V_DIM, D), D ** -0.5),
        'o_ln_ffn': gain((no, D)),
        'o_router': nrm((no, D, N_EXPERTS), D ** -0.5),
        'o_moe_gate': nrm((no, N_EXPERTS, D, EXPERT_DIM), D ** -0.5),
        'o_moe_up': nrm((no, N_EXPERTS, D, EXPERT_DIM), D ** -0.5),
        'o_moe_down': nrm((no, N_EXPERTS, EXPERT_DIM, D), EXPERT_DIM ** -0.5),
    }

def first_block(x, positions, e_ln_mix, e_w_in, e_conv_w, e_conv_b, e_gate_a_w, e_gate_a_b,
              e_gate_x_w, e_gate_x_b, e_lru_lambda, e_shift_mu, e_w0, e_w2, e_a0, e_a2, e_g2,
              e_k_k, e_k_a, e_r_k, e_gn_w, e_gn_b, e_w_out, e_ln_ffn, e_ffn_gate, e_ffn_up,
              e_ffn_down, o_ln_mix, o_w_qkv, o_q_norm, o_k_norm, o_lambda_q1, o_lambda_k1,
              o_lambda_q2, o_lambda_k2, o_subln, o_w_o, o_ln_ffn, o_router, o_moe_gate,
              o_moe_up, o_moe_down):
    for i in range(DEPTH):
        j = i // 2
        if i % 2 == 0:
            h = rms_norm(x, e_ln_mix[j])
            x = x + even_mixer(h, e_w_in[j], e_conv_w[j], e_conv_b[j], e_gate_a_w[j], e_gate_a_b[j],
                               e_gate_x_w[j], e_gate_x_b[j], e_lru_lambda[j], e_shift_mu[j], e_w0[j],
                               e_w2[j], e_a0[j], e_a2[j], e_g2[j], e_k_k[j], e_k_a[j], e_r_k[j],
                               e_gn_w[j], e_gn_b[j], e_w_out[j])
            h = rms_norm(x, e_ln_ffn[j])
            x = x + swiglu(h, e_ffn_gate[j], e_ffn_up[j], e_ffn_down[j])
        else:
            lambda_init = 0.8 - 0.6 * math.exp(-0.3 * i)
            h = rms_norm(x, o_ln_mix[j])
            x = x + diff_attention(h, positions, o_w_qkv[j], o_q_norm[j], o_k_norm[j],
                                   o_lambda_q1[j], o_lambda_k1[j], o_lambda_q2[j], o_lambda_k2[j],
                                   o_subln[j], o_w_o[j], lambda_init)
            h = rms_norm(x, o_ln_ffn[j])
            x = x + moe_swiglu(h, o_router[j], o_moe_gate[j], o_moe_up[j], o_moe_down[j])
    return x


HEAD_DIM = 64
H_MLA = 8
H_MOBA = 8
MLA_WIDTH = H_MLA * HEAD_DIM
MOBA_WIDTH = H_MOBA * HEAD_DIM
D_MIX = MLA_WIDTH + MOBA_WIDTH
Q_LORA = 256
KV_LORA = 128
NOPE_DIM = 64
ROPE_DIM_2 = 32
V_DIM = HEAD_DIM
QK_DIM = NOPE_DIM + ROPE_DIM_2
ROPE_THETA_2 = 10000.0
MOBA_BLOCK = 256
MOBA_TOPK = 3
MOBA_Q_CHUNK = 64
N_BUCKETS = 32
REL_MAX_DIST = 4096
EPS = 1e-6

IN_SPLITS = (Q_LORA, KV_LORA, ROPE_DIM_2, MLA_WIDTH, MOBA_WIDTH, MOBA_WIDTH, MOBA_WIDTH, MOBA_WIDTH)
IN_OFFSETS = (Q_LORA,
              Q_LORA + KV_LORA,
              Q_LORA + KV_LORA + ROPE_DIM_2,
              Q_LORA + KV_LORA + ROPE_DIM_2 + MLA_WIDTH,
              Q_LORA + KV_LORA + ROPE_DIM_2 + MLA_WIDTH + MOBA_WIDTH,
              Q_LORA + KV_LORA + ROPE_DIM_2 + MLA_WIDTH + 2 * MOBA_WIDTH,
              Q_LORA + KV_LORA + ROPE_DIM_2 + MLA_WIDTH + 3 * MOBA_WIDTH)
D_IN = Q_LORA + KV_LORA + ROPE_DIM_2 + MLA_WIDTH + 4 * MOBA_WIDTH


def rms_norm_2(x, g):
    xf = x.astype(jnp.float32)
    y = xf * lax.rsqrt(jnp.mean(xf * xf, axis=-1, keepdims=True) + EPS)
    return (y * g.astype(jnp.float32)).astype(x.dtype)

def apply_rope(x, positions):
    half = ROPE_DIM_2 // 2
    inv_freq = ROPE_THETA_2 ** (-jnp.arange(0, half, dtype=jnp.float32) / half)
    ang = positions.astype(jnp.float32)[..., None] * inv_freq
    cos = jnp.cos(ang)[:, :, None, :]
    sin = jnp.sin(ang)[:, :, None, :]
    xf = x.astype(jnp.float32)
    x1, x2 = xf[..., :half], xf[..., half:]
    out = jnp.concatenate([x1 * cos - x2 * sin, x1 * sin + x2 * cos], axis=-1)
    return out.astype(x.dtype)

def rel_bucket(dist):
    n = jnp.maximum(dist, 0)
    max_exact = N_BUCKETS // 2
    nf = jnp.maximum(n, 1).astype(jnp.float32)
    large = max_exact + (jnp.log(nf / max_exact) / math.log(REL_MAX_DIST / max_exact)
                         * (N_BUCKETS - max_exact)).astype(jnp.int32)
    large = jnp.minimum(large, N_BUCKETS - 1)
    return jnp.where(n < max_exact, n, large)

def mla_attention(c_q, c_kv, k_rope, positions, q_norm_g, w_uq, kv_norm_g, w_ukv, q_g, k_g):
    B, S, _ = c_q.shape
    q = (rms_norm_2(c_q, q_norm_g) @ w_uq).reshape(B, S, H_MLA, QK_DIM)
    kv = (rms_norm_2(c_kv, kv_norm_g) @ w_ukv).reshape(B, S, H_MLA, NOPE_DIM + V_DIM)
    k_nope, v = kv[..., :NOPE_DIM], kv[..., NOPE_DIM:]
    k = jnp.concatenate(
        [k_nope, jnp.broadcast_to(k_rope[:, :, None, :], (B, S, H_MLA, ROPE_DIM_2))], axis=-1)
    q = rms_norm_2(q, q_g)
    k = rms_norm_2(k, k_g)
    q = jnp.concatenate([q[..., :NOPE_DIM], apply_rope(q[..., NOPE_DIM:], positions)], axis=-1)
    k = jnp.concatenate([k[..., :NOPE_DIM], apply_rope(k[..., NOPE_DIM:], positions)], axis=-1)
    n_qb = S // Q_BLOCK
    qb = q.reshape(B, n_qb, Q_BLOCK, H_MLA, QK_DIM).transpose(1, 0, 2, 3, 4)
    kpos = jnp.arange(S)
    scale = QK_DIM ** -0.5

    def block(args):
        q_blk, i = args
        s = jnp.einsum('bqhd,bkhd->bhqk', q_blk, k,
                       preferred_element_type=jnp.float32) * scale
        qpos = i * Q_BLOCK + jnp.arange(Q_BLOCK)
        s = jnp.where(kpos[None, :] <= qpos[:, None], s, -jnp.inf)
        p = jax.nn.softmax(s, axis=-1)
        return jnp.einsum('bhqk,bkhd->bqhd', p.astype(v.dtype), v)

    o = lax.map(block, (qb, jnp.arange(n_qb)))
    return o.transpose(1, 0, 2, 3, 4).reshape(B, S, MLA_WIDTH)

def moba_attention(q, k, v, q_g, k_g, rel_bias):
    B, S, _ = q.shape
    q = rms_norm_2(q.reshape(B, S, H_MOBA, HEAD_DIM), q_g).transpose(0, 2, 1, 3)
    k = rms_norm_2(k.reshape(B, S, H_MOBA, HEAD_DIM), k_g).transpose(0, 2, 1, 3)
    v = v.reshape(B, S, H_MOBA, HEAD_DIM).transpose(0, 2, 1, 3)
    nb = -(-S // MOBA_BLOCK)
    pad = nb * MOBA_BLOCK - S
    kp = jnp.pad(k, ((0, 0), (0, 0), (0, pad), (0, 0))).reshape(B, H_MOBA, nb, MOBA_BLOCK, HEAD_DIM)
    vp = jnp.pad(v, ((0, 0), (0, 0), (0, pad), (0, 0))).reshape(B, H_MOBA, nb, MOBA_BLOCK, HEAD_DIM)
    blk_ids = jnp.arange(nb)
    counts = jnp.minimum(S - blk_ids * MOBA_BLOCK, MOBA_BLOCK).astype(jnp.float32)
    k_mean = kp.astype(jnp.float32).sum(axis=3) / counts[None, None, :, None]
    topk = min(MOBA_TOPK, nb)
    n_qc = S // MOBA_Q_CHUNK
    qc = q.reshape(B, H_MOBA, n_qc, MOBA_Q_CHUNK, HEAD_DIM).transpose(2, 0, 1, 3, 4)
    scale = HEAD_DIM ** -0.5
    bias_t = rel_bias.astype(jnp.float32).T
    head_idx = jnp.arange(H_MOBA)[None, :, None, None, None]
    gather_blocks = jax.vmap(jax.vmap(lambda blocks, idx: blocks[idx]))

    def chunk(args):
        q_c, i = args
        q0 = i * MOBA_Q_CHUNK
        own = q0 // MOBA_BLOCK
        qpos = q0 + jnp.arange(MOBA_Q_CHUNK)
        g = jnp.einsum('bhqd,bhnd->bhqn', q_c.astype(jnp.float32), k_mean)
        g = jnp.where(blk_ids < own, g, -jnp.inf)
        _, sel = lax.top_k(g, topk)
        valid = (jnp.arange(topk) < own)[:, None]
        k_sel = gather_blocks(kp, sel)
        v_sel = gather_blocks(vp, sel)
        s_sel = jnp.einsum('bhqd,bhqtkd->bhqtk', q_c, k_sel,
                           preferred_element_type=jnp.float32) * scale
        kpos_sel = sel[..., None] * MOBA_BLOCK + jnp.arange(MOBA_BLOCK)
        bias_sel = bias_t[head_idx, rel_bucket(qpos[:, None, None] - kpos_sel)]
        s_sel = jnp.where(valid, s_sel + bias_sel, -jnp.inf)
        k_own = lax.dynamic_slice_in_dim(kp, own, 1, axis=2)[:, :, 0]
        v_own = lax.dynamic_slice_in_dim(vp, own, 1, axis=2)[:, :, 0]
        s_own = jnp.einsum('bhqd,bhkd->bhqk', q_c, k_own,
                           preferred_element_type=jnp.float32) * scale
        kpos_own = own * MOBA_BLOCK + jnp.arange(MOBA_BLOCK)
        dist_own = qpos[:, None] - kpos_own[None, :]
        bias_own = bias_t[:, rel_bucket(dist_own)]
        s_own = jnp.where(dist_own >= 0, s_own + bias_own[None], -jnp.inf)
        s_all = jnp.concatenate(
            [s_sel.reshape(B, H_MOBA, MOBA_Q_CHUNK, topk * MOBA_BLOCK), s_own], axis=-1)
        p = jax.nn.softmax(s_all, axis=-1).astype(v.dtype)
        p_sel = p[..., :topk * MOBA_BLOCK].reshape(B, H_MOBA, MOBA_Q_CHUNK, topk, MOBA_BLOCK)
        p_own = p[..., topk * MOBA_BLOCK:]
        return (jnp.einsum('bhqtk,bhqtkd->bhqd', p_sel, v_sel)
                + jnp.einsum('bhqk,bhkd->bhqd', p_own, v_own))

    o = lax.map(chunk, (qc, jnp.arange(n_qc)))
    o = o.transpose(1, 2, 0, 3, 4).reshape(B, H_MOBA, S, HEAD_DIM)
    return o.transpose(0, 2, 1, 3).reshape(B, S, MOBA_WIDTH)

def hybrid_layer(x, c, positions, norm_g, w_ada, b_ada, w_in, mla_q_norm_g, mla_w_uq,
                 mla_kv_norm_g, mla_w_ukv, mla_q_g, mla_k_g, moba_q_g, moba_k_g, w_out, rel_bias):
    mod = jax.nn.silu(c) @ w_ada + b_ada
    shift, scale, gate = jnp.split(mod[:, None, :], 3, axis=-1)
    h = rms_norm_2(x, norm_g) * (1 + scale) + shift
    z = h @ w_in
    c_q, c_kv, k_rope, g_mla, q_b, k_b, v_b, g_moba = jnp.split(z, list(IN_OFFSETS), axis=-1)
    o_mla = mla_attention(c_q, c_kv, k_rope, positions, mla_q_norm_g, mla_w_uq,
                          mla_kv_norm_g, mla_w_ukv, mla_q_g, mla_k_g)
    o_moba = moba_attention(q_b, k_b, v_b, moba_q_g, moba_k_g, rel_bias)
    y = jnp.concatenate([jax.nn.silu(g_mla) * o_mla, jax.nn.silu(g_moba) * o_moba], axis=-1) @ w_out
    return x + gate * y

def second_inputs(seed: int = 0) -> dict:
    key = jax.random.key(seed)
    ks = jax.random.split(key, 20)
    f32 = jnp.float32
    nrm = lambda k, shape, s: jax.random.normal(k, shape, f32) * s
    return {
        "x": nrm(ks[0], (BATCH, SEQ, D_MODEL), 1.0),
        "c": nrm(ks[1], (BATCH, D_MODEL), 1.0),
        "positions": jnp.broadcast_to(jnp.arange(SEQ, dtype=jnp.int32), (BATCH, SEQ)),
        "norm_g": 1.0 + nrm(ks[2], (DEPTH, D_MODEL), 0.05),
        "w_ada": nrm(ks[3], (DEPTH, D_MODEL, 3 * D_MODEL), 0.5 * D_MODEL ** -0.5),
        "b_ada": nrm(ks[4], (DEPTH, 3 * D_MODEL), 0.01),
        "w_in": nrm(ks[5], (DEPTH, D_MODEL, D_IN), D_MODEL ** -0.5),
        "mla_q_norm_g": 1.0 + nrm(ks[6], (DEPTH, Q_LORA), 0.05),
        "mla_w_uq": nrm(ks[7], (DEPTH, Q_LORA, H_MLA * QK_DIM), Q_LORA ** -0.5),
        "mla_kv_norm_g": 1.0 + nrm(ks[8], (DEPTH, KV_LORA), 0.05),
        "mla_w_ukv": nrm(ks[9], (DEPTH, KV_LORA, H_MLA * (NOPE_DIM + V_DIM)), KV_LORA ** -0.5),
        "mla_q_g": 1.0 + nrm(ks[10], (DEPTH, QK_DIM), 0.05),
        "mla_k_g": 1.0 + nrm(ks[11], (DEPTH, QK_DIM), 0.05),
        "moba_q_g": 1.0 + nrm(ks[12], (DEPTH, HEAD_DIM), 0.05),
        "moba_k_g": 1.0 + nrm(ks[13], (DEPTH, HEAD_DIM), 0.05),
        "w_out": nrm(ks[14], (DEPTH, D_MIX, D_MODEL), D_MIX ** -0.5),
        "rel_bias": nrm(ks[15], (N_BUCKETS, H_MOBA), 0.5),
    }

def second_block(x, c, positions, norm_g, w_ada, b_ada, w_in, mla_q_norm_g, mla_w_uq,
              mla_kv_norm_g, mla_w_ukv, mla_q_g, mla_k_g, moba_q_g, moba_k_g, w_out, rel_bias):
    for l in range(DEPTH):
        x = hybrid_layer(x, c, positions, norm_g[l], w_ada[l], b_ada[l], w_in[l],
                         mla_q_norm_g[l], mla_w_uq[l], mla_kv_norm_g[l], mla_w_ukv[l],
                         mla_q_g[l], mla_k_g[l], moba_q_g[l], moba_k_g[l], w_out[l], rel_bias)
    return x


def setup_inputs(seed=0):
    out = dict(first_inputs(seed))
    for name, value in second_inputs(seed + 1).items():
        if name != "x":
            out[name + "_2"] = value
    return out


def reference(
    x, positions, e_ln_mix, e_w_in, e_conv_w, e_conv_b, e_gate_a_w, e_gate_a_b, e_gate_x_w,
    e_gate_x_b, e_lru_lambda, e_shift_mu, e_w0, e_w2, e_a0, e_a2, e_g2, e_k_k, e_k_a, e_r_k,
    e_gn_w, e_gn_b, e_w_out, e_ln_ffn, e_ffn_gate, e_ffn_up, e_ffn_down, o_ln_mix, o_w_qkv,
    o_q_norm, o_k_norm, o_lambda_q1, o_lambda_k1, o_lambda_q2, o_lambda_k2, o_subln, o_w_o,
    o_ln_ffn, o_router, o_moe_gate, o_moe_up, o_moe_down, c_2, positions_2, norm_g_2, w_ada_2,
    b_ada_2, w_in_2, mla_q_norm_g_2, mla_w_uq_2, mla_kv_norm_g_2, mla_w_ukv_2, mla_q_g_2,
    mla_k_g_2, moba_q_g_2, moba_k_g_2, w_out_2, rel_bias_2,
):
    x = first_block(
        x, positions, e_ln_mix, e_w_in, e_conv_w, e_conv_b, e_gate_a_w, e_gate_a_b, e_gate_x_w,
        e_gate_x_b, e_lru_lambda, e_shift_mu, e_w0, e_w2, e_a0, e_a2, e_g2, e_k_k, e_k_a, e_r_k,
        e_gn_w, e_gn_b, e_w_out, e_ln_ffn, e_ffn_gate, e_ffn_up, e_ffn_down, o_ln_mix, o_w_qkv,
        o_q_norm, o_k_norm, o_lambda_q1, o_lambda_k1, o_lambda_q2, o_lambda_k2, o_subln, o_w_o,
        o_ln_ffn, o_router, o_moe_gate, o_moe_up, o_moe_down,
    )
    return second_block(
        x, c_2, positions_2, norm_g_2, w_ada_2, b_ada_2, w_in_2, mla_q_norm_g_2, mla_w_uq_2,
        mla_kv_norm_g_2, mla_w_ukv_2, mla_q_g_2, mla_k_g_2, moba_q_g_2, moba_k_g_2, w_out_2,
        rel_bias_2,
    )


_drawn_inputs = setup_inputs


def setup_inputs(seed=0):
    import zlib

    import numpy as np

    out = dict(_drawn_inputs(seed))
    spreads = {}
    factors = {'e_gate_a_b': 8.0,
     'e_gate_x_b': 8.0,
     'e_k_k': 5.003,
     'e_k_a': 2.867,
     'e_gn_w': 3.784,
     'e_gn_b': 3.861,
     'o_k_norm': 3.204,
     'o_lambda_q1': 2.719,
     'o_subln': 4.035,
     'norm_g_2': 8.0,
     'b_ada_2': 8.0,
     'mla_q_norm_g_2': 8.0,
     'mla_w_uq_2': 2.847,
     'mla_kv_norm_g_2': 8.0,
     'mla_q_g_2': 8.0,
     'mla_k_g_2': 8.0,
     'moba_q_g_2': 8.0,
     'moba_k_g_2': 8.0,
     'rel_bias_2': 4.944}
    for name, (base, spread) in spreads.items():
        noise = np.random.default_rng([zlib.crc32(name.encode()), seed]).standard_normal(out[name].shape)
        drawn = base * np.exp(spread * noise) if base else spread * noise
        out[name] = __import__('jax').numpy.asarray(drawn.astype(out[name].dtype))
    for name, factor in factors.items():
        out[name] = (out[name] * factor).astype(out[name].dtype)
    return out
```

```python
import math
from contextlib import ExitStack

import numpy as np

import concourse.bass as bass
from concourse import mybir

F32 = mybir.dt.float32
F32R = mybir.dt.float32r
I32 = mybir.dt.int32
U32 = mybir.dt.uint32
ALU = mybir.AluOpType
ACT = mybir.ActivationFunctionType
AX = mybir.AxisListType.X

P = 128
T = 256
TT = T // P
D = 1024
KD = D // P
BANK = 512
W = 512
NC4 = W // P
HALF = 64
EVEN_IN = 2816
CT_IN = EVEN_IN // P
CT_RW = CT_IN - 2 * NC4
FFN = 2816
NE = 8
EF = 3584
EC = EF // BANK
ITEMS = NE + 3
QKV = 3072
DIN2 = 2976
HEAD0 = 416
CONV = 4
SLOTS = 7
SLOT = 4096
E_SLOTS = 7
E_SPLITS = 4
E_HALF = SLOT // 2
MIX_SLOTS = 3
LAMBDA_INIT = 0.8 - 0.6 * math.exp(-0.3)
MASKED = -1e30
TWO_PI = 2.0 * math.pi
DEPTH2 = 2


def const_tables():
    j = np.arange(P)[:, None]
    t = np.arange(P)[None, :]
    same = (j // HALF) == (t // HALF)
    parts = {
        "ident": (j == t),
        "same_head": same,
        "before_same": same & (j < t),
        "until_same": same & (j <= t),
        "after_same": same & (j > t),
        "before": (j < t),
        "ones": np.ones((P, P)),
    }
    for s in (1, 2, 4, 8, 16, 32):
        parts[f"join{s}"] = (j // (2 * s) == t // (2 * s)) & (j % (2 * s) >= s) & (t % (2 * s) < s)
    parts["join1_up"] = parts["join1"].T
    parts["future"] = np.concatenate([np.zeros((P, P)), np.where(t > j, MASKED, 0.0)], 1)
    parts["restart"] = np.broadcast_to((np.arange(T) % HALF != 0)[None, :], (P, T))
    parts["count128"] = np.broadcast_to(t, (P, P))
    parts["count8"] = np.broadcast_to(np.arange(8)[None, :], (P, 8))
    f1 = 500000.0 ** (-np.arange(0, 16, 2, dtype=np.float32) / np.float32(16))
    f2 = 10000.0 ** (-np.arange(0, 16, dtype=np.float32) / np.float32(16))
    parts["freq1"] = np.broadcast_to(f1[None, :], (P, 8))
    parts["freq2"] = np.broadcast_to(f2[None, :], (P, 16))
    at, where = 0, {}
    for name, a in parts.items():
        where[name] = (at, a.shape[1])
        at += a.shape[1]
    table = np.concatenate([np.asarray(a, np.float32) for a in parts.values()], 1)
    return np.ascontiguousarray(table), where


BIAS_ROW = 384


def bucket_table():
    dist = np.arange(T)
    nf = np.maximum(dist, 1).astype(np.float32)
    large = 16 + (np.log(nf / np.float32(16)) / np.float32(math.log(4096 / 16))
                  * np.float32(16)).astype(np.int32)
    bucket = np.where(dist < 16, dist, np.minimum(large, 31))
    out = np.zeros((32, BIAS_ROW), np.float32)
    for i in range(BIAS_ROW):
        d = 255 - i
        if d >= 0:
            out[bucket[d], i] = 1.0
    return out


CONSTS, WHERE = const_tables()
NCONST = CONSTS.shape[1]


class Plan:

    def __init__(self):
        self.by = []
        self.index = {}

    def add(self, name, who):
        self.index[name] = len(self.by)
        self.by.append(who)

    def emptied_before(self, i):
        if i < 8:
            return None
        who = self.by[i - 8]
        return who, sum(w == who for w in self.by[:i - 7])

    def filled(self, name):
        return self.index[name] + 1


def attention_fills(plan, tag, steps):
    plan.add((tag, "scores", 0), "v")
    plan.add((tag, "scores", 1), "v")
    for i in range(steps):
        plan.add((tag, "weightsT", i), "a")
        if i + 2 < steps:
            plan.add((tag, "scores", i + 2), "v")
        plan.add((tag, "values", i), "a")


FFN_CHUNKS = [(c, min(BANK, FFN - c * BANK)) for c in range(-(-FFN // BANK))]
FFN_STEPS = [(c, w, m) for c, w in FFN_CHUNKS for m in range(TT)]
LEVELS = (2, 4, 8, 16, 32)


MOD_AT = {"gate_g": (0, 3), "key_norm": (3, 6), "bonus": (6, 8), 0: (8, 9), 1: (9, 10), 2: (10, 11), 3: (11, 12)}


def make_plan():
    plan = Plan()
    add = plan.add

    def norm(tag):
        for u in range(4):
            add((tag, "xT", u), "av"[u % 2])

    def rows(tag, n):
        for c in range(n):
            for m in range(TT):
                add((tag, c, m), "v")

    def mods(first, end):
        for i in range(first, end):
            add(("mod", i), "a")

    add("params", "v")
    norm("mix0")
    for u in range(CT_IN // 2):
        add(("w_in", u), "a" if u < 4 or u % 2 else "v")
    for u in range(4):
        add(("lru_gate", u), "a")
    for u in range(4):
        add(("lora", u), "a")
    for u in range(2):
        add(("gate_g", u), "v")
    mods(*MOD_AT["gate_g"])
    for u in range(2):
        add(("key_norm", u), "a")
    mods(*MOD_AT["key_norm"])
    for u in range(2):
        add(("bonus", u), "v")
    mods(*MOD_AT["bonus"])
    for u in range(6):
        add(("by_token", u), "av"[u % 2])
    for u in range(8):
        add(("AB", u), "v")
        add(("CB", u), "v")
    for u in range(4):
        add(("A", u), "v")
    for s in LEVELS:
        for g in range(4):
            add(("U", s, g), "a")
        for g in range(4):
            add(("dY", s, g), "v")
            if s < LEVELS[-1]:
                add(("dX", s, g), "v")
    for h in range(NE):
        add(("bias", h), "a")
    for c in range(4):
        add(("Z", c), "v")
        add(("SA", c), "v")
        if c < 3:
            add(("dS", c), "v")
        add(("O", c), "a")
        mods(*MOD_AT[c])
    for u in range(2):
        add(("OT", u), "v")
    rows("w_out", 2)
    norm("ffn")
    for i, (c, w, m) in enumerate(FFN_STEPS + [(None, 0, 0)]):
        if c is not None:
            add(("G", c, m), "a")
            add(("Up", c, m), "v")
        if i:
            pc, pw, pm = FFN_STEPS[i - 1]
            add(("hT", pc, pm), "a")
            add(("Dn", pc, pm, 0), "v")
            add(("Dn", pc, pm, 1), "v")
    norm("mix1")
    for c in range(QKV // BANK):
        for m in range(TT):
            add(("qkv", c, m), "av"[m])
    for u in range(8):
        add(("qkT", u), "av"[u % 2])
    attention_fills(plan, "diff", 16)
    for u in range(4):
        add(("oT", u), "av"[u % 2])
    rows("w_o", 2)
    norm("moe")
    add("router", "v")
    add("places", "v")
    for l in range(DEPTH2):
        for u in range(2):
            add(("mod_gate", l, u), "v")
        for u in range(4):
            add((("h", l), "xT", u), "av"[u % 2])
        for c in range(6):
            for m in range(TT):
                add(("z", l, c, m), "av"[m])
        for u in range(2):
            add(("cT", l, u), "a")
        for c in range(4):
            for m in range(TT):
                add(("up", l, c, m), "av"[m])
        for u in range(8):
            add(("mlaT", l, u), "av"[u % 2])
        attention_fills(plan, ("mla", l), 8)
        for u in range(4):
            add(("mobaT", l, u), "av"[u % 2])
        attention_fills(plan, ("moba", l), 8)
        for u in range(4):
            add(("yT", l, u), "av"[u % 2])
        for c in range(2):
            for m in range(TT):
                add(("w_out", l, c, m), "v")
    return plan


PLAN = make_plan()


class Tiles:

    def __init__(self):
        self.rows = []
        self.by_name = {}
        self.signals = [0] * SLOTS
        self.last_use = [None] * SLOTS
        self.turn = 0

    def add(self, name, slots, loads, last_use, after=()):
        slot = self.turn % slots
        self.turn = (slot + 1) % slots
        self.signals[slot] += 16 * len(loads)
        row = {"slot": slot, "loads": loads, "free": self.last_use[slot],
               "ready": self.signals[slot], "after": list(after)}
        self.rows.append((name, row))
        self.by_name[name] = row
        self.last_use[slot] = last_use

    def restart(self):
        self.turn = 0


def columns(w, c0, n):
    k = w.shape[0] // P
    return (0, [k, n], w[:, c0:c0 + n].rearrange("(k p) n -> p k n", p=P))


def row_tiles(w, r0, n):
    return (0, [n // P, D], w[r0:r0 + n, :].rearrange("(k p) n -> p k n", p=P))


def make_tiles(I):
    tiles = Tiles()
    w_in = I["e_w_in"][0]
    for c in range(6):
        n = min(BANK, EVEN_IN - c * BANK)
        tiles.add(("w_in", c), MIX_SLOTS, [columns(w_in, c * BANK, n)],
                  ("w_in", (c * BANK + n) // 256 - 1))
    for i in range(12):
        tiles.add(("ada", i), MIX_SLOTS, [columns(I["w_ada_2"][i // 6], i % 6 * BANK, BANK)], ("mod", i))
    for c in range(2):
        tiles.add(("w_out", c), MIX_SLOTS, [columns(I["e_w_out"][0], c * BANK, BANK)],
                  ("w_out", c, TT - 1))
    tiles.turn = 2
    for i, (c, w) in enumerate(FFN_CHUNKS + [(None, 0)]):
        if c is not None:
            for kind, src in (("G", "e_ffn_gate"), ("Up", "e_ffn_up")):
                slot = tiles.turn % SLOTS
                tiles.add((kind, c), SLOTS, [columns(I[src][0], c * BANK, w)], (kind, c, TT - 1),
                          ["scratch0"] if MIX_SLOTS <= slot and tiles.last_use[slot] is None else [])
        if i:
            pc, pw = FFN_CHUNKS[i - 1]
            slot = tiles.turn % SLOTS
            tiles.add(("Dn", pc), SLOTS, [row_tiles(I["e_ffn_down"][0], pc * BANK, pw)],
                      ("Dn", pc, TT - 1, 1), ["scratch0"] if MIX_SLOTS <= slot and tiles.last_use[slot] is None else [])
    tiles.restart()
    for c in range(QKV // BANK):
        tiles.add(("qkv", c), MIX_SLOTS, [columns(I["o_w_qkv"][0], c * BANK, BANK)],
                  ("qkv", c, TT - 1))
    for c in range(2):
        tiles.add(("w_o", c), MIX_SLOTS, [columns(I["o_w_o"][0], c * BANK, BANK)],
                  ("w_o", c, TT - 1))
    tiles.rows.append(("experts", None))
    tiles.restart()
    for l in range(DEPTH2):
        for c in range(6):
            c0, n = (0, HEAD0) if c == 0 else (HEAD0 + (c - 1) * BANK, BANK)
            tiles.add(("z", l, c), MIX_SLOTS, [columns(I["w_in_2"][l], c0, n)],
                      ("z", l, c, TT - 1))
        tiles.add(("up", l), MIX_SLOTS,
                  [(0, [2, 768], I["mla_w_uq_2"][l].rearrange("(k p) n -> p k n", p=P)),
                   (1536, [1, 1024], I["mla_w_ukv_2"][l].rearrange("(k p) n -> p k n", p=P))],
                  ("up", l, 3, TT - 1))
        for c in range(2):
            tiles.add(("wo2", l, c), MIX_SLOTS, [columns(I["w_out_2"][l], c * BANK, BANK)],
                      ("w_out", l, c, TT - 1))
    return tiles


PARAM_ROWS = [("e_ln_mix", 8), ("e_ln_ffn", 8), ("o_ln_mix", 8), ("o_ln_ffn", 8), ("e_conv_w", 16),
              ("e_conv_b", 4), ("e_gate_a_b", 4), ("e_gate_x_b", 4), ("e_lru_lambda", 4),
              ("e_shift_mu", CT_RW), ("e_w0", 4), ("e_a0", 4), ("e_k_k", 4), ("e_k_a", 4),
              ("e_r_k", 4), ("e_gn_w", 4), ("e_gn_b", 4), ("o_subln", 1), ("norm_g_2", 16),
              ("mla_q_norm_g_2", 4)]
PARAM_ROWS_2 = [("mla_kv_norm_g_2", 2), ("c_2", 8), ("b_ada_2", 48)]
PARAM_AT = {}
for _half, _rows in enumerate((PARAM_ROWS, PARAM_ROWS_2)):
    _at = 0
    for _name, _n in _rows:
        PARAM_AT[_name] = _half * P + _at
        _at += _n
NROWS = [sum(n for _, n in r) for r in (PARAM_ROWS, PARAM_ROWS_2)]
NPARAM = P + NROWS[1]

NAMES = ["x", "positions", "e_ln_mix", "e_w_in", "e_conv_w", "e_conv_b", "e_gate_a_w", "e_gate_a_b",
         "e_gate_x_w", "e_gate_x_b", "e_lru_lambda", "e_shift_mu", "e_w0", "e_w2", "e_a0", "e_a2",
         "e_g2", "e_k_k", "e_k_a", "e_r_k", "e_gn_w", "e_gn_b", "e_w_out", "e_ln_ffn", "e_ffn_gate",
         "e_ffn_up", "e_ffn_down", "o_ln_mix", "o_w_qkv", "o_q_norm", "o_k_norm", "o_lambda_q1",
         "o_lambda_k1", "o_lambda_q2", "o_lambda_k2", "o_subln", "o_w_o", "o_ln_ffn", "o_router",
         "o_moe_gate", "o_moe_up", "o_moe_down", "c_2", "positions_2", "norm_g_2", "w_ada_2",
         "b_ada_2", "w_in_2", "mla_q_norm_g_2", "mla_w_uq_2", "mla_kv_norm_g_2", "mla_w_ukv_2",
         "mla_q_g_2", "mla_k_g_2", "moba_q_g_2", "moba_k_g_2", "w_out_2", "rel_bias_2"]


N_SMALL = 7
DIFF_STEPS = [(h, m) for h in range(8) for m in range(TT)]
PAIR_STEPS = [(g, m) for g in range(4) for m in range(TT)]
ZC, ZR, ZG = 256, 384, HEAD0
ZQ = HEAD0 + 512
ZV = ZQ + 1024
ZGB = ZV + 512


class Chain:

    def __init__(self, eng, own):
        self.eng, self.own, self.made = eng, own, {}

    def __call__(self, instruction, to=None):
        sem = self.own if to is None else to
        self.made[sem.num] = self.made.get(sem.num, 0) + 1
        instruction.then_inc(sem, 1)
        self.eng.wait_ge(sem, self.made[sem.num])


def build(nc, I, consts, buckets, out):
    tiles = make_tiles(I)
    scratch = nc.dram_tensor("bias_rows", (P, W * NE), F32, kind="Internal").ap()
    ctx = ExitStack()
    with ctx:
        def sb(name, shape, dt=F32):
            return ctx.enter_context(nc.sbuf_tensor(name, shape, dt))

        def sem(name):
            return ctx.enter_context(nc.semaphore(name))

        X = sb("X", [P, TT, D])
        XN = sb("XN", [P, TT, D])
        XT = sb("XT", [P, KD, T])
        YT = sb("YT", [P, KD, T])
        CST = sb("CST", [P, NCONST])
        BIAS = sb("BIAS", [P, NE, T])
        big_base = -(-nc.sbuf_base // 32) * 32
        BIG = sb("BIG", [P, 12288 + 25930])

        PRM = sb("PRM", [P, NPARAM])
        GAINS = sb("GAINS", [P, 1024])
        ROUTER = sb("ROUTER", [P, KD, NE])
        POS = sb("POS", [P, 2 * TT], I32)
        SM = sb("SM", [P, 720])
        IX = sb("IX", [P, TT, 8], U32)
        ITEM = sb("ITEM", [1, 16], I32)
        banks = [ctx.enter_context(nc.psum_tensor(f"bank{i}", [P, BANK], F32)) for i in range(8)]

        def slot(s):
            return BIG[:, s * SLOT:(s + 1) * SLOT]

        def R(at, n):
            assert at + n <= 25930
            return BIG[:, 12288 + at:12288 + at + n]

        def cst(name):
            at, n = WHERE[name]
            return CST[:, at:at + n]

        def prm(name, i=0):
            at = PARAM_AT[name] + i
            return PRM[:, at:at + 1]

        small_at = [0]

        def small(n):
            small_at[0] += n
            assert small_at[0] <= 720
            return SM[:, small_at[0] - n:small_at[0]]

        IDENT = cst("ident")

        filled = sem("bank_filled")
        emptied = {"a": sem("bank_emptied_by_scalar"), "v": sem("bank_emptied_by_vector")}
        slot_loaded = [sem(f"slot{i}_loaded") for i in range(SLOTS)]
        row_tile = sem("row_tile_done")
        v_done = sem("vector_done")
        a_done = sem("scalar_done")
        x_loaded = sem("x_loaded")
        const_loaded = sem("consts_loaded")
        rows_loaded = sem("param_rows_loaded")
        rows_cleared = sem("rows_cleared")
        lru_w_cleared = sem("lru_gate_weights_cleared")
        lru_w_loaded = sem("lru_gate_weights_loaded")
        small_loaded = sem("small_inputs_loaded")
        bias_saved = sem("bias_rows_saved")
        bias_loaded = sem("bias_loaded")
        bias_ready = sem("bias_rows_ready")
        moe_gain_loaded = sem("moe_gain_loaded")
        squares = sem("squares_ready")
        mean_square = sem("mean_square_ready")
        inverse_rms = sem("inverse_rms_ready")
        xn_ready = sem("xn_ready")
        x_ready = sem("x_ready")
        conv_ready = sem("conv_ready")
        lru_done = sem("lru_done")
        qk_built = sem("mla_keys_built")
        lam_abs = sem("lambda_abs_ready")
        lam_exp = sem("lambda_exp_ready")
        gates_ready = sem("lru_gates_ready")
        decay_arg = sem("lru_decay_arg_ready")
        decay_ready = sem("lru_decay_ready")
        root_arg = sem("lru_root_arg_ready")
        root_ready = sem("lru_root_ready")
        shifted = sem("shifted_ready")
        lora_in = sem("lora_inputs_ready")
        lora_out = sem("lora_gates_ready")
        cum_ready = sem("cumulated_decay_ready")
        exps_ready = sem("decay_exps_ready")
        key_squares = sem("key_squares_ready")
        key_norms = sem("key_norms_ready")
        chunk_ops = sem("chunk_operands_ready")
        inverse_in = sem("inverse_operands_ready")
        state_ready = sem("state_ready")
        gn_ready = sem("group_norm_ready")
        gn_var = sem("group_variance_ready")
        gn_root = sem("group_root_ready")
        yT_ready = sem("mixer_result_ready")
        angles = sem("angles_ready")
        sines = sem("sines_ready")
        lam_dots = sem("lambda_dots_ready")
        lam_exps = sem("lambda_exps_ready")
        qk_sums = sem("qk_sums_ready")
        qk_squares = sem("qk_squares_ready")
        qk_roots = sem("qk_roots_ready")
        qk_ready = sem("qk_ready")
        maxima = sem("score_maxima_ready")
        exps = sem("score_exps_ready")
        weights = sem("weights_ready")
        o_squares = sem("o_squares_ready")
        o_sums = sem("o_sums_ready")
        o_roots = sem("o_roots_ready")
        o_ready = sem("o_ready")
        moe_in = sem("moe_input_ready")
        gap_ready = sem("router_gap_ready")
        gap_exp = sem("router_exp_ready")
        choices = sem("choices_ready")
        items_ready = sem("items_ready")
        m_filled = sem("expert_bank_filled")
        m_emptied = {"a": sem("expert_bank_emptied_by_scalar"),
                     "v": sem("expert_bank_emptied_by_vector")}
        m_places = sem("expert_places_ready")
        m_combs = sem("expert_weights_ready")
        v_ended = sem("vector_past_experts")
        m_loaded = [sem(f"expert_slot{i}_loaded") for i in range(E_SLOTS)]
        w_high = sem("expert_weights_high_ready")
        w_low = sem("expert_weights_low_ready")
        xg_high = sem("expert_x_high_ready")
        c_silu = sem("condition_silu_ready")
        mod_ready = sem("modulation_ready")
        gate_silu = sem("output_gates_ready")
        out_saved = sem("out_saved")

        block = ctx.enter_context(nc.Block())

        def fill(pe, name):
            i = PLAN.index[name]
            before = PLAN.emptied_before(i)
            if before is not None:
                pe.wait_ge(emptied[before[0]], before[1])
            return banks[i % 8][:, :]

        def take(eng, name):
            eng.wait_ge(filled, PLAN.filled(name))
            return banks[PLAN.index[name] % 8][:, :]

        def wait_taken(eng, name):
            i = PLAN.index[name]
            who = PLAN.by[i]
            eng.wait_ge(emptied[who], sum(w == who for w in PLAN.by[:i + 1]))

        def wait_tile(pe, name):
            row = tiles.by_name[name]
            pe.wait_ge(slot_loaded[row["slot"]], row["ready"])
            return slot(row["slot"])

        def at_head(tt, h):
            return tt * 8 + h % 2 * 4 + h // 2

        def v3(ap, n):
            return ap.rearrange("p (a b) -> p a b", a=n)

        PS = v3(R(0, CT_RW * T), CT_RW)
        GG = v3(R(3584, 1024), 4)
        BON = v3(R(4608, 1024), 4)
        KB = v3(R(5632, 1024), 4)
        KT = v3(R(6656, 1024), 4)
        QR = R(7680, 2048).rearrange("p (c w t) -> p c w t", c=4, w=2)
        TMK = v3(R(9728, 1024), TT)
        TMT = v3(R(10752, 1024), TT)
        TMV = v3(R(11776, 1024), TT)
        CW = v3(R(12800, 1024), 4)
        KK = v3(R(13824, 1024), 4)
        EP = v3(R(14848, 1024), 4)
        EPX = v3(R(15872, 1024), 4)
        EN = v3(R(16896, 1024), 4)
        TMP = v3(R(17920, 1024), 4)
        WLA = R(18944, 512)
        WG2 = R(19456, 512)
        RW = v3(R(20000, CT_RW * (T + 1)), CT_RW)
        TWX = R(23600, 256)
        SXG = R(23856, 256)
        GAW = v3(R(24112, 512), 4)
        GXW = v3(R(24624, 512), 4)
        LX = v3(R(7680, 4 * (T + CONV - 1)), 4)
        LG = v3(R(4608, 1024), 4)
        XC = v3(R(5632, 1024), 4)
        GA = v3(R(9728, 1024), 4)
        GX = v3(R(10752, 1024), 4)
        T1 = v3(R(11776, 1024), 4)
        T2 = v3(R(12800, 1024), 4)
        B1T = v3(R(12800, 2048), 16)
        CB2 = v3(R(14848, 4096), 16)
        AL = v3(R(18944, 2048), 16)
        YI = v3(R(20992, 2048), 16)
        XI = v3(R(23040, 2048), 16)
        AM = v3(R(0, 2048), 16)
        UU = XN[:, :, :].rearrange("p a b -> p (a b)").rearrange("p (a b) -> p a b", a=16)
        ST = [v3(R(2048, 512), 4), v3(R(5632, 512), 4)]
        ZS = R(2560, 512)
        SAN = R(3072, 512)
        OO = v3(R(6656, 1024), TT)
        GSQ = v3(R(9728, 1024), TT)
        DS = v3(R(6144, 512), 4)
        ROWB = [v3(R(18944, 4 * BIAS_ROW), 4), v3(R(23040, 4 * BIAS_ROW), 4)]
        BUCK = R(25500, BIAS_ROW)
        ROWS = R(3968, 2 * P)
        SIL = v3(R(18432, 1024), 2)
        HH = v3(R(19456, 1024), 2)
        HT = R(20480, 1024).rearrange("p (b k s) -> p b k s", b=2, k=4)
        PSEL = v3(R(23552, 256), TT)
        PCMB = v3(R(23808, 256), TT)
        PCT = v3(R(24064, 256), TT)
        YE = R(24320, 1024)

        def split_part(name, at, n):
            return nc.alloc_sbuf_tensor_at(name, [P, n], F32R, offset=big_base + 4 * at)[:, :]

        XGH = v3(split_part("expert_x_high", 12288 + 21504, 1024), KD)
        XGL = v3(split_part("expert_x_low", 12288 + 22528, 1024), KD)
        WH, WL = ([split_part(f"weights_{part}{i}", E_SLOTS * E_HALF + (2 * i + j) * E_HALF, E_HALF)
                   for i in range(E_SPLITS)] for j, part in enumerate(("high", "low")))
        GMOE = YT[:, 0:4, :].rearrange("p a b -> p (a b)")
        QKVB = v3(R(0, 6144), TT)
        SQ = v3(R(6144, 4096), TT)
        QKT = v3(R(10240, 4096), 16)
        SS = R(14336, 1024).rearrange("p (b c k) -> p b c k", b=2, c=2)
        EE = R(15360, 1024).rearrange("p (b c k) -> p b c k", b=2, c=2)
        AT = R(16384, 512).rearrange("p (b k) -> p b k", b=2)
        PT = R(16896, 1024).rearrange("p (b c k q) -> p b c k q", b=2, c=2, k=2)
        OA = v3(R(17920, 2048), TT)
        ROT = R(19968, 2048).rearrange("p (a b) -> p a b", a=4)
        ZB = v3(R(0, TT * DIN2), TT)
        QK = v3(R(5952, 3072), TT)
        KV = v3(R(9024, 2048), TT)
        SQ2 = v3(R(11072, 3072), TT)
        QKT2 = v3(R(14144, 4096), 16)
        SS2 = R(18240, 1024).rearrange("p (b c k) -> p b c k", b=2, c=2)
        EE2 = R(19264, 1024).rearrange("p (b c k) -> p b c k", b=2, c=2)
        PT2 = R(20288, 1024).rearrange("p (b c k q) -> p b c k q", b=2, c=2, k=2)
        O2 = v3(R(21312, 2048), TT)
        GATE = R(23360, 1024)
        CN = v3(R(14144, 768), TT)
        CT = v3(R(25408, 0 + 512), 2)
        CT3 = XN[:, 0, 0:256]
        ROT2 = SQ2.rearrange("p a b -> p (a b)")[:, 0:2048].rearrange("p (a b) -> p a b", a=4)
        G_QK = GAINS[:, 0:128]
        G_MLA = [GAINS[:, 128 + 192 * l:320 + 192 * l] for l in range(DEPTH2)]
        G_MOBA = [GAINS[:, 512 + 128 * l:640 + 128 * l] for l in range(DEPTH2)]
        G_LAM = GAINS[:, 768:1024]
        s_ss = small(2)
        s_ms = small(2)
        s_rs = small(2)
        s_half = small(4)
        s_l = [small(4) for _ in range(6)]
        s_omka = small(4)
        s_pl = small(16).rearrange("p (c k) -> p c k", c=4)
        s_mean = small(16)
        s_var = small(16)
        s_qk = small(64)
        s_ang = small(96)
        s_turn = small(48)
        s_posf = small(4)
        s_subg = small(1)
        s_rcb = small(4).rearrange("p (b c) -> p b c", b=2)
        s_lg = small(16).rearrange("p (m e) -> p m e", m=TT)
        s_nm = small(4).rearrange("p (b c) -> p b c", b=2)
        s_sm = small(4).rearrange("p (b c) -> p b c", b=2)
        s_lam = small(4)
        s_relb = small(8)
        s_mx = small(16).rearrange("p (m e) -> p m e", m=TT)
        s_ixf = small(16).rearrange("p (m e) -> p m e", m=TT)
        s_w = small(2 * TT)
        s_oh = small(2 * TT * NE).rearrange("p (k m e) -> p k m e", k=2, m=TT)
        s_mask = small(TT * NE).rearrange("p (m e) -> p m e", m=TT)
        s_comb = small(TT * ITEMS).rearrange("p (m e) -> p m e", m=TT)
        s_place = small(TT * ITEMS).rearrange("p (m e) -> p m e", m=TT)
        s_cnt = small(NE)
        s_over = small(NE)
        s_rank = small(NE)
        s_pick = small(NE)
        s_junk = small(NE)
        s_item = small(16)
        s_cc = small(KD)
        s_mod = small(48)
        s_gs = small(KD)
        gate_d = I["o_moe_gate"].rearrange("l e (k p) f -> p (l e) k f", p=P)
        up_d = I["o_moe_up"].rearrange("l e (k p) f -> p (l e) k f", p=P)
        down_d = I["o_moe_down"].rearrange("l e (k p) d -> p (l e) k d", p=P)
        E_TILES = []
        for c in range(EC + 1):
            for kind, c_ in (("G", c), ("Up", c), ("Dn", c - 1)):
                if 0 <= c_ < EC:
                    E_TILES += [(kind, c_, 0), (kind, c_, 1)]
        TURNS = len(E_TILES) // E_SLOTS
        SPLIT = [n for n in E_TILES if n[0] != "Dn"]
        N_SPLIT = len(SPLIT)
        assert len(E_TILES) % E_SLOTS == 0 and N_SPLIT % E_SPLITS == 0

        E_PLAN = Plan()
        for u in range(2):
            E_PLAN.add(("XG", u), "v")
        E_PLAN.add("PCT", "a")
        for c in range(EC + 1):
            if c < EC:
                E_PLAN.add(("G", c), "a")
            if c:
                E_PLAN.add(("hT", c - 1), "a")
            if c < EC:
                E_PLAN.add(("Up", c), "v")
            if c:
                E_PLAN.add(("Dn", c - 1, 0), "v")
                E_PLAN.add(("Dn", c - 1, 1), "v")
        for m in range(TT):
            for n in range(2):
                E_PLAN.add(("Y", m, n), "v")
        E_N = len(E_PLAN.by)
        E_BY = {w: sum(b == w for b in E_PLAN.by) for w in "av"}

        def e_count(it, who, i):
            n = sum(w == who for w in E_PLAN.by[:(i + E_N if i < 0 else i) + 1])
            return it * E_BY[who] + (n if i < 0 else n + E_BY[who])

        def e_fill(pe, it, name):
            i = E_PLAN.index[name]
            k = i - 8 if i >= 8 else max(k for k in range(E_N) if k % 8 == i % 8) - E_N
            who = E_PLAN.by[k if k >= 0 else k + E_N]
            pe.wait_ge(m_emptied[who], e_count(it, who, k))
            return banks[i % 8][:, :]

        def e_take(eng, it, name):
            eng.wait_ge(m_filled, it * E_N + (E_N + E_PLAN.index[name] + 1))
            return banks[E_PLAN.index[name] % 8][:, :]

        def e_wait_taken(eng, it, name):
            i = E_PLAN.index[name]
            eng.wait_ge(m_emptied[E_PLAN.by[i]], e_count(it, E_PLAN.by[i], i))

        def e_split_done(eng, it, g, ahead=1):
            eng.wait_ge(w_low, it * N_SPLIT + (ahead * N_SPLIT + g + 1))

        def expert_loads(sp):
            sp.wait_ge(items_ready, 1)
            with sp.Fori(0, sp.value_load(ITEM[0:1, 12:13], min_val=NE, max_val=ITEMS)) as it:
                expert = sp.value_load(ITEM[0:1, bass.ds(it, 1)], min_val=0, max_val=NE - 1)
                for q, (kind, c, j) in enumerate(E_TILES):
                    before = E_TILES[q - E_SLOTS]
                    ahead = 1 if q >= E_SLOTS else 0
                    if before[0] == "Dn":
                        sp.wait_ge(m_filled, it * E_N + (ahead * E_N + E_PLAN.index[before] + 1))
                    else:
                        e_split_done(sp, it, SPLIT.index(before), ahead)
                    if kind == "Dn":
                        src = down_d[:, bass.ds(expert, 1), 4 * c:4 * c + 4, j * BANK:(j + 1) * BANK]
                    else:
                        w = gate_d if kind == "G" else up_d
                        src = w[:, bass.ds(expert, 1), 4 * j:4 * j + 4, c * BANK:(c + 1) * BANK]
                    dst = half(q % E_SLOTS).rearrange("p (l k n) -> p l k n", l=1, k=4)
                    sp.dma_start(dst, src).then_inc(m_loaded[q % E_SLOTS], 16)

        def half(i):
            return BIG[:, i * E_HALF:(i + 1) * E_HALF]

        def e_tile(eng, it, name):
            q = E_TILES.index(name)
            eng.wait_ge(m_loaded[q % E_SLOTS], it * (16 * TURNS) + 16 * (q // E_SLOTS + 1))
            return half(q % E_SLOTS)

        def wait_x(eng, n):
            if n == 0:
                eng.wait_ge(x_loaded, 16)
            elif n < 4:
                wait_taken(eng, [("w_out", 1, 1), ("Dn", len(FFN_CHUNKS) - 1, 1, 1), ("w_o", 1, 1)][n - 1])
            else:
                eng.wait_ge(x_ready, n - 3)

        @block.sync
        def _(sp):
            sp.dma_start(X[:, :, :], I["x"][0].rearrange("(m p) d -> p m d", p=P)).then_inc(x_loaded, 16)
            sp.dma_start(CST[:, :], consts).then_inc(const_loaded, 16)
            released = False
            for name, row in tiles.rows:
                if name == "experts":
                    expert_loads(sp)
                    continue
                if row["free"] is not None:
                    sp.wait_ge(filled, PLAN.filled(row["free"]))
                if row["after"] and not released:
                    sp.wait_ge(yT_ready, 1)
                    released = True
                if name == ("z", 0, 0):
                    sp.wait_ge(x_ready, 1)
                for at, dims, src in row["loads"]:
                    dst = slot(row["slot"])[:, at:at + dims[0] * dims[1]]
                    sp.dma_start(dst.rearrange("p (k n) -> p k n", k=dims[0]), src)\
                        .then_inc(slot_loaded[row["slot"]], 16)
            wait_x(sp, 6)
            sp.dma_start(out[0].rearrange("(m p) d -> p m d", p=P), X[:, :, :]).then_inc(out_saved, 16)
            sp.wait_ge(out_saved, 16)

        @block.gpsimd
        def _(pool):
            g = nc.gpsimd
            for half, n in enumerate(NROWS):
                pool.dma_start(ROWS[0:n, half * P:half * P + P], I[f"rows{half}"]).then_inc(rows_loaded, 16)
            loads = [(POS[:, 0:2 * TT], I["pos"].rearrange("s m p -> p (s m)")),
                     (GAINS[:, :], I["gains"].partition_broadcast(P)), (WLA, I["lora"]), (WG2, I["e_g2"][0]),
                     (s_relb[0:32, :], I["rel_bias_2"]), (BUCK[0:32, :], buckets),
                     (ROUTER[:, :, :], I["o_router"][0].rearrange("(k p) e -> p k e", p=P))]
            for dst, src in loads:
                pool.dma_start(dst, src, allow_slow_non_contiguous=True).then_inc(small_loaded, 16)
            assert len(loads) == N_SMALL
            g.memset(R(24112, 1024), 0.0).then_inc(lru_w_cleared, 1)
            g.memset(LX[:, :, 0:CONV - 1], 0.0).then_inc(rows_cleared, 1)
            g.memset(RW[:, :, 0:1], 0.0).then_inc(rows_cleared, 1)
            pool.wait_ge(lru_w_cleared, 1)
            for dst, name in ((GAW, "e_gate_a_w"), (GXW, "e_gate_x_w")):
                src = I[name][0].rearrange("(c h) i j -> h i c j", h=2)
                for h in range(2):
                    pool.dma_start(dst[64 * h:64 * h + 64, :, 64 * h:64 * h + 64], src[h])\
                        .then_inc(lru_w_loaded, 16)
            g.memset(s_half, -0.5).then_inc(rows_cleared, 1)
            pool.wait_ge(rows_cleared, 3)

            def inverse_root(n):
                pool.wait_ge(mean_square, n + 1)
                if n:
                    pool.wait_ge(xn_ready, n)
                g.tensor_tensor(out=s_rs, in0=s_ms, in1=s_half[:, 0:2], op=ALU.pow).then_inc(inverse_rms, 1)

            inverse_root(0)
            wait_taken(pool, ("bias", NE - 1))
            for i in range(2):
                rows = scratch.rearrange("q (h i) -> q h i", h=NE)[:, 4 * i:4 * i + 4, 0:BIAS_ROW]
                pool.dma_start(rows, ROWB[i]).then_inc(bias_saved, 16)
            pool.wait_ge(bias_saved, 32)
            pool.dma_start(BIAS[:, :, :], bass.AP(scratch.tensor, 127, [[W * NE - 1, P], [W, NE], [1, T]]))\
                .then_inc(bias_loaded, 16)
            inverse_root(1)
            pool.wait_ge(filled, PLAN.filled(("w_out", 1, 1)))
            pool.dma_start(GMOE, I["o_ln_ffn"][0].partition_broadcast(P)).then_inc(moe_gain_loaded, 16)
            for n in (2, 3):
                inverse_root(n)
            for l in range(DEPTH2):
                inverse_root(4 + l)

        @block.tensor
        def _(pe):
            mm = nc.tensor.matmul

            def norm(n, tag):
                pe.wait_ge(xn_ready, n + 1)
                for u in range(4):
                    b = fill(pe, (tag, "xT", u))
                    for k in range(2):
                        for m in range(TT):
                            d = 2 * u + k
                            last = nc.tensor.transpose(b[:, (2 * k + m) * P:(2 * k + m + 1) * P],
                                                       XN[:, m, d * P:(d + 1) * P], IDENT)
                    last.then_inc(filled, 1)
                wait_taken(pe, (tag, "xT", 2))
                wait_taken(pe, (tag, "xT", 3))

            def product(name, lhs, w, n, kt):
                b = fill(pe, name)
                for k in range(kt):
                    last = mm(b[:, 0:n], lhs(k), w[:, k, :], start=k == 0, stop=k == kt - 1)
                last.then_inc(filled, 1)

            def by_token(name, tile, n, src, kt=KD, base=0):
                w = wait_tile(pe, tile)[:, base:base + kt * n].rearrange("p (k n) -> p k n", k=kt)
                for m in range(TT):
                    product(name + (m,), lambda k: src[:, k, m * P:(m + 1) * P], w, n, kt)

            def to_channels(name, units, src):
                for u in range(units):
                    b = fill(pe, name + (u,))
                    for rows, at, a in src(u):
                        last = nc.tensor.transpose(b[0:rows, at:at + P], a, IDENT)
                    last.then_inc(filled, 1)

            order = [0]

            def attention(tag, steps, base, ready, lhs, rhs, src, pt, value, vd, halves=True):
                n_c = 1 if vd == P else 2

                def scores(i):
                    g, m = steps[i]
                    w = (m + 1) * P
                    b = fill(pe, (tag, "scores", i))
                    first = mm(b[:, 0:w], lhs(g, 0, m), rhs(g, 0, w), start=True, stop=True)
                    if halves:
                        order[0] += 1
                        first.then_inc(row_tile, 1)
                        pe.wait_ge(row_tile, order[0])
                    mm(b[:, T:T + w], lhs(g, 1, m), rhs(g, 1, w), start=True, stop=True).then_inc(filled, 1)

                scores(0)
                scores(1)
                for i, (g, m) in enumerate(steps):
                    b = fill(pe, (tag, "weightsT", i))
                    pe.wait_ge(ready, base + i + 1)
                    for c in range(n_c):
                        for k in range(m + 1):
                            last = nc.tensor.transpose(b[:, (2 * c + k) * P:(2 * c + k + 1) * P],
                                                       src(i % 2, c, k), IDENT)
                    last.then_inc(filled, 1)
                    if i + 2 < len(steps):
                        scores(i + 2)
                    b = fill(pe, (tag, "values", i))
                    wait_taken(pe, (tag, "weightsT", i))
                    for c in range(n_c):
                        for k in range(m + 1):
                            last = mm(b[:, c * vd:(c + 1) * vd], pt[:, i % 2, c, k, :], value(g, c, k),
                                      start=k == 0, stop=k == m)
                    last.then_inc(filled, 1)

            pe.wait_ge(const_loaded, 16)
            pe.wait_ge(rows_loaded, 16 * 2)
            b = fill(pe, "params")
            for half, n in enumerate(NROWS):
                last = nc.tensor.transpose(b[:, half * P:half * P + n], ROWS[0:n, half * P:half * P + P],
                                           IDENT[0:n, 0:n])
            last.then_inc(filled, 1)
            def mods(first, end):
                for i in range(first, end):
                    w = wait_tile(pe, ("ada", i)).rearrange("p (k n) -> p k n", k=KD)
                    b = fill(pe, ("mod", i))
                    pe.wait_ge(c_silu, 1)
                    for j in range(4):
                        for k in range(KD):
                            last = mm(b[:, j:j + 1], w[:, k, j * P:(j + 1) * P], s_cc[:, k:k + 1],
                                      start=k == 0, stop=k == KD - 1)
                    last.then_inc(filled, 1)

            norm(0, "mix0")
            for u in range(CT_IN // 2):
                n = min(BANK, EVEN_IN - (u // 2) * BANK)
                w = wait_tile(pe, ("w_in", u // 2))[:, 0:KD * n].rearrange("p (k n) -> p k n", k=KD)
                b = fill(pe, ("w_in", u))
                for j in range(2):
                    c0 = (2 * (u % 2) + j) * P
                    for k in range(KD):
                        last = mm(b[:, j * T:(j + 1) * T], w[:, k, c0:c0 + P], XT[:, k, :],
                                  start=k == 0, stop=k == KD - 1)
                last.then_inc(filled, 1)
            pe.wait_ge(lru_w_loaded, 16 * 4)
            pe.wait_ge(conv_ready, 1)
            for u in range(4):
                w = (GAW, GXW)[u // 2]
                b = fill(pe, ("lru_gate", u))
                for j in range(2):
                    c = 2 * (u % 2) + j
                    last = mm(b[:, j * T:(j + 1) * T], w[:, c, :], XC[:, c, :], start=True, stop=True)
                last.then_inc(filled, 1)
            pe.wait_ge(lora_in, 2)
            for u in range(4):
                rows = slice(0, 64) if u < 2 else slice(64, 128)
                src = TWX[0:64, :] if u < 2 else PS[64:128, 12, :]
                b = fill(pe, ("lora", u))
                for j in range(2):
                    c = 2 * (u % 2) + j
                    last = mm(b[:, j * T:(j + 1) * T], WLA[rows, c * P:(c + 1) * P], src, start=True, stop=True)
                last.then_inc(filled, 1)
            for u in range(2):
                b = fill(pe, ("gate_g", u))
                for j in range(2):
                    c = 2 * u + j
                    last = mm(b[:, j * T:(j + 1) * T], WG2[:, c * P:(c + 1) * P], SXG, start=True, stop=True)
                last.then_inc(filled, 1)
            mods(*MOD_AT["gate_g"])
            for name, n in (("key_norm", 1), ("bonus", 2)):
                pe.wait_ge(key_squares, n)
                for u in range(2):
                    b = fill(pe, (name, u))
                    for j in range(2):
                        last = mm(b[:, j * T:(j + 1) * T], cst("same_head"), TMP[:, 2 * u + j, :],
                                  start=True, stop=True)
                    last.then_inc(filled, 1)
                mods(*MOD_AT[name])
            pe.wait_ge(chunk_ops, 1)
            for u in range(6):
                src = (KB, KT, PS[:, 8:12, :])[u // 2]
                b = fill(pe, ("by_token", u))
                for c in range(4):
                    last = nc.tensor.transpose(b[:, c * P:(c + 1) * P],
                                               src[:, c, (u % 2) * P:(u % 2 + 1) * P], IDENT)
                last.then_inc(filled, 1)
            for u in range(8):
                tt, h = u // 4, u // 2 % 2
                r = slice(64 * h, 64 * h + 64)
                for name, src in (("AB", KB), ("CB", KT)):
                    b = fill(pe, (name, u))
                    for j in range(2):
                        c = 2 * (u % 2) + j
                        last = mm(b[:, j * T:(j + 1) * T], src[r, c, tt * P:(tt + 1) * P],
                                  QR[r, c, :, tt * P:(tt + 1) * P], start=True, stop=True)
                    last.then_inc(filled, 1)
            for u in range(4):
                b = fill(pe, ("A", u))
                for i in range(4):
                    tt, c, r = u // 2, i, slice(64 * (u % 2), 64 * (u % 2) + 64)
                    last = mm(b[:, i * P:(i + 1) * P], QR[r, c, 0, tt * P:(tt + 1) * P],
                              KB[r, c, tt * P:(tt + 1) * P], start=True, stop=True)
                last.then_inc(filled, 1)
            for n, s in enumerate(LEVELS):
                for gr in range(4):
                    pe.wait_ge(inverse_in, 4 * n + gr + 1)
                    b = fill(pe, ("U", s, gr))
                    for i in range(4):
                        last = mm(b[:, i * P:(i + 1) * P], AM[:, 4 * gr + i, :], YI[:, 4 * gr + i, :],
                                  start=True, stop=True)
                    last.then_inc(filled, 1)
                for gr in range(4):
                    wait_taken(pe, ("U", s, gr))
                    for name in ("dY", "dX"):
                        if name == "dX" and s == LEVELS[-1]:
                            continue
                        b = fill(pe, (name, s, gr))
                        for i in range(4):
                            k = 4 * gr + i
                            lhs, rhs = (XI, UU) if name == "dY" else (UU, XI)
                            last = mm(b[:, i * P:(i + 1) * P], lhs[:, k, :], rhs[:, k, :],
                                      start=True, stop=True)
                        last.then_inc(filled, 1)
            pe.wait_ge(small_loaded, 16 * N_SMALL)
            for h in range(NE):
                b = fill(pe, ("bias", h))
                mm(b[:, 0:BIAS_ROW], s_relb[0:32, h:h + 1].broadcast_to([32, P]), BUCK[0:32, :],
                   start=True, stop=True).then_inc(filled, 1)

            wait_taken(pe, ("dY", LEVELS[-1], 3))
            for c in range(4):
                tt, r = c // 2, slice(64 * (c % 2), 64 * (c % 2) + 64)
                t0 = slice(tt * P, (tt + 1) * P)

                def group(name, parts):
                    b = fill(pe, name)
                    for i, (c0, n, lhs, rhs) in enumerate(parts):
                        last = mm(b[:, c0:c0 + n], lhs, rhs, start=i == 0, stop=i == len(parts) - 1,
                                  skip_group_check=True)
                    last.then_inc(filled, 1)

                state = lambda w: [(p * P, P, QR[:, p, w, t0], ST[c % 2][:, p, :]) for p in range(4)] if c else []
                if c:
                    pe.wait_ge(state_ready, c)
                group(("Z", c), state(0) + [(h * 64, 64, CB2[r, at_head(tt, h), 0:P], TMV[r, tt, h * 64:h * 64 + 64])
                                            for h in range(8)])
                wait_taken(pe, ("Z", c))
                group(("SA", c), [(h * 64, 64, YI[r, at_head(tt, h), :], ZS[r, h * 64:h * 64 + 64])
                                  for h in range(8)])
                wait_taken(pe, ("SA", c))
                if c < 3:
                    group(("dS", c), [(p * P, P, a[r, tt, p * P:(p + 1) * P], b_[r, p * P:(p + 1) * P])
                                      for p in range(4) for a, b_ in ((TMK, SAN), (TMT, TMV[:, tt, :]))])
                group(("O", c), state(1)
                      + [(h * 64, 64, B1T[r, at_head(tt, h), :], SAN[r, h * 64:h * 64 + 64]) for h in range(8)]
                      + [(h * 64, 64, CB2[r, at_head(tt, h), P:2 * P], TMV[r, tt, h * 64:h * 64 + 64])
                         for h in range(8)])
                mods(*MOD_AT[c])
            pe.wait_ge(gn_ready, 1)
            to_channels(("OT",), 2, lambda u: [(P, (2 * j + m) * P, OO[:, m, (2 * u + j) * P:(2 * u + j + 1) * P])
                                               for j in range(2) for m in range(TT)])
            pe.wait_ge(yT_ready, 1)
            for c in range(2):
                by_token(("w_out", c), ("w_out", c), BANK, YT)

            norm(1, "ffn")
            for i, step in enumerate(FFN_STEPS + [None]):
                if step is not None:
                    c, w, m = step
                    for kind in ("G", "Up"):
                        wt = wait_tile(pe, (kind, c))[:, 0:KD * w].rearrange("p (k n) -> p k n", k=KD)
                        product((kind, c, m), lambda k: XT[:, k, m * P:(m + 1) * P], wt, w, KD)
                if i:
                    c, w, m = FFN_STEPS[i - 1]
                    b = fill(pe, ("hT", c, m))
                    wait_taken(pe, ("Up", c, m))
                    for k in range(w // P):
                        last = nc.tensor.transpose(b[:, k * P:(k + 1) * P],
                                                   HH[:, (i - 1) % 2, k * P:(k + 1) * P], IDENT)
                    last.then_inc(filled, 1)
                    wd = wait_tile(pe, ("Dn", c))[:, 0:(w // P) * D].rearrange("p (k n) -> p k n", n=D)
                    wait_taken(pe, ("hT", c, m))
                    for n in range(2):
                        product(("Dn", c, m, n), lambda k: HT[:, (i - 1) % 2, k, :],
                                wd[:, :, n * BANK:(n + 1) * BANK], BANK, w // P)

            norm(2, "mix1")
            for c in range(QKV // BANK):
                by_token(("qkv", c), ("qkv", c), BANK, XT)
            pe.wait_ge(qk_ready, 1)
            to_channels(("qkT",), 8, lambda u: [(P, (2 * j + m) * P, QKVB[:, m, (2 * u + j) * P:(2 * u + j + 1) * P])
                                                for j in range(2) for m in range(TT)])
            wait_taken(pe, ("qkT", 6))
            wait_taken(pe, ("qkT", 7))
            attention("diff", DIFF_STEPS, 0, weights,
                      lambda h, c, m: QKT[64 * c:64 * c + 64, h, m * P:(m + 1) * P],
                      lambda h, c, w: QKT[64 * c:64 * c + 64, 8 + h, 0:w],
                      lambda b, c, k: AT[:, b, k * P:(k + 1) * P], PT,
                      lambda h, c, k: QKVB[:, k, 2048 + h * P:2048 + (h + 1) * P], P)
            pe.wait_ge(o_ready, 1)
            to_channels(("oT",), 4, lambda u: [(P, (2 * j + m) * P, OA[:, m, (2 * u + j) * P:(2 * u + j + 1) * P])
                                               for j in range(2) for m in range(TT)])
            wait_taken(pe, ("oT", 2))
            wait_taken(pe, ("oT", 3))
            for c in range(2):
                by_token(("w_o", c), ("w_o", c), BANK, XT)

            pe.wait_ge(filled, PLAN.filled(("w_o", 1, 1)))
            pe.sem_inc(m_filled, E_N)
            norm(3, "moe")
            b = fill(pe, "router")
            for m in range(TT):
                for k in range(KD):
                    last = mm(b[:, m * NE:(m + 1) * NE], XT[:, k, m * P:(m + 1) * P], ROUTER[:, k, :],
                              start=k == 0, stop=k == KD - 1)
            last.then_inc(filled, 1)
            b = fill(pe, "places")
            pe.wait_ge(choices, 1)
            for at, parts in ((0, (("before", 0),)), (NE, (("ones", 0), ("before", 1))),
                              (2 * NE, (("ones", 0), ("ones", 1)))):
                for i, (a, m) in enumerate(parts):
                    last = mm(b[:, at:at + NE], cst(a), s_mask[:, m, :], start=i == 0, stop=i == len(parts) - 1)
            last.then_inc(filled, 1)
            pe.wait_ge(items_ready, 1)
            wait_taken(pe, "places")
            wait_taken(pe, ("moe", "xT", 2))
            pe.wait_ge(moe_in, 1)
            with pe.Fori(0, pe.value_load(ITEM[0:1, 12:13], min_val=NE, max_val=ITEMS)) as it:
                for u in range(2):
                    b = e_fill(pe, it, ("XG", u))
                    if u == 0:
                        pe.wait_ge(m_places, it * TT + TT)
                    for k in range(4):
                        d = 4 * u + k
                        for m in range(TT):
                            last = mm(b[:, k * P:(k + 1) * P], XN[:, m, d * P:(d + 1) * P], PSEL[:, m, :],
                                      start=m == 0, stop=m == TT - 1)
                    last.then_inc(m_filled, 1)
                b = e_fill(pe, it, "PCT")
                pe.wait_ge(m_combs, it * TT + TT)
                for m in range(TT):
                    last = nc.tensor.transpose(b[:, m * P:(m + 1) * P], PCMB[:, m, :], IDENT)
                last.then_inc(m_filled, 1)

                def expert_product(kind, c):
                    b = e_fill(pe, it, (kind, c))
                    if c == 0 and kind == "G":
                        e_wait_taken(pe, it, ("XG", 1))
                    for k in range(KD):
                        g = SPLIT.index((kind, c, k // 4))
                        if k % 4 == 0:
                            e_split_done(pe, it, g)
                        high, low = (part[g % E_SPLITS][:, k % 4 * BANK:(k % 4 + 1) * BANK] for part in (WH, WL))
                        mm(b, XGH[:, k, :], high, start=k == 0, stop=False)
                        mm(b, XGL[:, k, :], high, start=False, stop=False)
                        last = mm(b, XGH[:, k, :], low, start=False, stop=k == KD - 1)
                    last.then_inc(m_filled, 1)

                for c in range(EC + 1):
                    if c < EC:
                        expert_product("G", c)
                    if c:
                        b = e_fill(pe, it, ("hT", c - 1))
                        e_wait_taken(pe, it, ("Up", c - 1))
                        for k in range(4):
                            last = nc.tensor.transpose(b[:, k * P:(k + 1) * P],
                                                       HH[:, (c - 1) % 2, k * P:(k + 1) * P], IDENT)
                        last.then_inc(m_filled, 1)
                    if c < EC:
                        expert_product("Up", c)
                    if c:
                        for n in range(2):
                            b = e_fill(pe, it, ("Dn", c - 1, n))
                            w = e_tile(pe, it, ("Dn", c - 1, n)).rearrange("p (k n) -> p k n", k=4)
                            if n == 0:
                                e_wait_taken(pe, it, ("hT", c - 1))
                            for k in range(4):
                                last = mm(b, HT[:, (c - 1) % 2, k, :], w[:, k, :], start=k == 0, stop=k == 3)
                            last.then_inc(m_filled, 1)
                for m in range(TT):
                    for n in range(2):
                        b = e_fill(pe, it, ("Y", m, n))
                        e_wait_taken(pe, it, ("Dn", EC - 1, n))
                        mm(b, PCT[:, m, :], YE[:, n * BANK:(n + 1) * BANK], start=True, stop=True)\
                            .then_inc(m_filled, 1)
            wait_x(pe, 4)

            for l in range(DEPTH2):
                for n in range(2):
                    b = fill(pe, ("mod_gate", l, n))
                    for j in range(4):
                        col = s_mod[:, 24 * l + 16 + 4 * n + j:24 * l + 17 + 4 * n + j]
                        last = mm(b[:, j * P:(j + 1) * P], col.broadcast_to([P, P]), IDENT, start=True, stop=True)
                    last.then_inc(filled, 1)
                norm(4 + l, ("h", l))
                for c in range(6):
                    by_token(("z", l, c), ("z", l, c), HEAD0 if c == 0 else BANK, XT)
                pe.wait_ge(qk_ready, 1 + 3 * l + 1)
                to_channels(("cT", l), 2, lambda u: [(P, (2 * j + m) * P, CN[:, m, (2 * u + j) * P:(2 * u + j + 1) * P])
                                                     for j in range(2 - u) for m in range(TT)])
                wait_taken(pe, ("cT", l, 1))
                w = wait_tile(pe, ("up", l))
                wq = w[:, 0:1536].rearrange("p (k n) -> p k n", k=2)
                for c, (n0, n) in enumerate(((0, 512), (512, 256))):
                    for m in range(TT):
                        product(("up", l, c, m), lambda k: CT[:, k, m * P:(m + 1) * P],
                                wq[:, :, n0:n0 + n], n, 2)
                for c in range(2):
                    for m in range(TT):
                        product(("up", l, 2 + c, m), lambda k: CT3[:, m * P:(m + 1) * P],
                                w[:, 1536 + c * BANK:1536 + (c + 1) * BANK].unsqueeze(1), BANK, 1)
                pe.wait_ge(qk_ready, 1 + 3 * l + 2)
                to_channels(("mlaT", l), 8, lambda u: [(96, (2 * j + m) * P, QK[:, m, (2 * u + j) * 96:(2 * u + j + 1) * 96])
                                                       for j in range(2) for m in range(TT)])
                wait_taken(pe, ("mlaT", l, 6))
                wait_taken(pe, ("mlaT", l, 7))
                attention(("mla", l), PAIR_STEPS, 16 + 16 * l, exps,
                          lambda g, c, m: QKT2[0:96, 2 * g + c, m * P:(m + 1) * P],
                          lambda g, c, w_: QKT2[0:96, 8 + 2 * g + c, 0:w_],
                          lambda b_, c, k: EE2[:, b_, c, k * P:(k + 1) * P], PT2,
                          lambda g, c, k: KV[:, k, (2 * g + c) * P + 64:(2 * g + c + 1) * P], 64, halves=False)
                pe.wait_ge(qk_ready, 1 + 3 * l + 3)
                to_channels(("mobaT", l), 4, lambda u: [
                    (P, (2 * j + m) * P, ZB[:, m, ZQ + (2 * u + j) * P:ZQ + (2 * u + j + 1) * P])
                    for j in range(2) for m in range(TT)])
                wait_taken(pe, ("mobaT", l, 2))
                wait_taken(pe, ("mobaT", l, 3))
                attention(("moba", l), PAIR_STEPS, 24 + 16 * l, exps,
                          lambda g, c, m: QKT2[64 * c:64 * c + 64, g, m * P:(m + 1) * P],
                          lambda g, c, w_: QKT2[64 * c:64 * c + 64, 4 + g, 0:w_],
                          lambda b_, c, k: EE2[:, b_, c, k * P:(k + 1) * P], PT2,
                          lambda g, c, k: ZB[:, k, ZV + (2 * g + c) * 64:ZV + (2 * g + c + 1) * 64], 64)
                pe.wait_ge(o_ready, 2 + l)
                to_channels(("yT", l), 4, lambda u: [(P, (2 * j + m) * P, O2[:, m, (2 * u + j) * P:(2 * u + j + 1) * P])
                                                     for j in range(2) for m in range(TT)])
                wait_taken(pe, ("yT", l, 2))
                wait_taken(pe, ("yT", l, 3))
                for c in range(2):
                    by_token(("w_out", l, c), ("wo2", l, c), BANK, XT)

        @block.vector
        def _(v):
            V = Chain(v, v_done)
            d = nc.vector
            ev = emptied["v"]
            tt_, ts, stt = d.tensor_tensor, d.tensor_scalar, d.scalar_tensor_tensor
            MUL, ADD, SUB = ALU.mult, ALU.add, ALU.subtract

            def bc(a, axis, shape):
                return a.unsqueeze(axis).broadcast_to(shape)

            def norm(n, tag, gain=None, shift=None):
                v.wait_ge(squares, n + 1)
                V(ts(s_ms, s_ss, 1.0 / D, 1e-6, MUL, ADD), mean_square)
                v.wait_ge(inverse_rms, n + 1)
                V(ts(XN[:, 0, :], X[:, 0, :], s_rs[:, 0:1], None, MUL))
                V(ts(XN[:, 1, :], X[:, 1, :], s_rs[:, 1:2], None, MUL), xn_ready)

            def norm_out(tag, gain, shift=None):
                for u in (1, 3):
                    b = take(v, (tag, "xT", u))
                    for k in range(2):
                        src, dst = b[:, k * T:(k + 1) * T], XT[:, 2 * u + k, :]
                        to = ev if k else None
                        if shift is None:
                            V(ts(dst, src, gain(2 * u + k), None, MUL), to)
                        else:
                            V(ts(dst, src, gain(2 * u + k), shift(2 * u + k), MUL, ADD), to)

            def add_rows(name):
                for c in range(2):
                    for m in range(TT):
                        b = take(v, name + (c, m))
                        x = X[:, m, c * BANK:(c + 1) * BANK]
                        V(tt_(x, x, b, ADD), ev)

            def head_norm(n, ss, x, gain, groups, width):
                v.wait_ge(qk_squares, n)
                V(d.reduce_sum(s_qk[:, 0:groups], ss, AX))
                V(ts(s_qk[:, 0:groups], s_qk[:, 0:groups], 1.0 / width, 1e-6, MUL, ADD), qk_sums)
                v.wait_ge(qk_roots, n)
                V(d.reciprocal(s_qk[:, 0:groups], s_qk[:, 0:groups]))
                g2 = groups // TT
                for m in range(TT):
                    xm = x(m)
                    flat = xm.rearrange("p (g w) -> p g w", w=width)
                    V(tt_(flat, flat, bc(s_qk[:, m * g2:(m + 1) * g2], 2, [P, g2, width]), MUL))
                    two = xm.rearrange("p (q g w) -> p q g w", q=2, w=width)
                    V(tt_(two, two, bc(gain.rearrange("p (q w) -> p q w", q=2), 2, [P, 2, g2 // 2, width]), MUL))

            def rotate(x1, x2, sin, cos, tmp, g, w):
                t = [tmp[:, i, :].rearrange("p (m g w) -> p m g w", m=TT, w=w) for i in range(4)]
                shape = [P, TT, g, w]
                cs, sn = (bc(a.rearrange("p (m w) -> p m w", m=TT), 2, shape) for a in (cos, sin))
                V(tt_(t[0], x1, cs, MUL))
                V(tt_(t[1], x2, sn, MUL))
                V(tt_(t[2], x2, cs, MUL))
                V(tt_(t[3], x1, sn, MUL))
                V(tt_(x1, t[0], t[1], SUB))

            def attention(tag, steps, base, ss, ee, at, add, scale_in, scale_max):
                def masked(i):
                    g, m = steps[i]
                    w = (m + 1) * P
                    b = take(v, (tag, "scores", i)).rearrange("p (c k) -> p c k", c=2)[:, :, 0:w]
                    if i >= 2:
                        v.wait_ge(exps, base + i - 1)
                    x = ss[:, i % 2, :, 0:w]
                    if scale_in is None:
                        V(tt_(x, b, add(g, w), ADD), ev)
                    else:
                        V(stt(x, b, scale_in, add(g, w), MUL, ADD), ev)
                    V(d.tensor_reduce(s_nm[:, i % 2, :], x, AX, ALU.max, negate=True),
                      maxima if scale_max is None else None)
                    if scale_max is not None:
                        V(ts(s_nm[:, i % 2, :], s_nm[:, i % 2, :], scale_max, None, MUL), maxima)

                masked(0)
                for i, (g, m) in enumerate(steps):
                    if i + 1 < len(steps):
                        masked(i + 1)
                    w = (m + 1) * P
                    v.wait_ge(exps, base + i + 1)
                    if at is None:
                        if i >= 2:
                            wait_taken(v, (tag, "values", i - 2))
                        V(d.reciprocal(s_rcb[:, i % 2, :], s_sm[:, i % 2, :]), weights)
                        continue
                    V(d.reciprocal(s_rcb[:, i % 2, :], s_sm[:, i % 2, :]))
                    V(tt_(s_rcb[:, i % 2, 1:2], s_rcb[:, i % 2, 1:2], s_lam[:, 2:3], MUL))
                    if i >= 2:
                        v.wait_ge(filled, PLAN.filled((tag, "weightsT", i - 2)))
                    a = at[:, i % 2, 0:w]
                    V(ts(a, ee[:, i % 2, 0, 0:w], s_rcb[:, i % 2, 0:1], None, MUL))
                    V(stt(a, ee[:, i % 2, 1, 0:w], s_rcb[:, i % 2, 1:2], a, MUL, ADD), weights)

            b = take(v, "params")
            V(d.tensor_copy(PRM[:, 0:NROWS[0]], b[:, 0:NROWS[0]]))
            V(d.tensor_copy(PRM[:, P:P + NROWS[1]], b[:, P:P + NROWS[1]]), ev)
            PAR = PRM[:, :]

            def prms(name, n, i=0):
                return PAR[:, PARAM_AT[name] + i:PARAM_AT[name] + i + n]

            lam_ = prms("e_lru_lambda", 4)
            V(ts(s_l[0], lam_, -1.0, None, MUL))
            V(tt_(s_l[1], s_l[0], lam_, ALU.max), lam_abs)
            V(ts(s_omka, prms("e_k_a", 4), -1.0, 1.0, MUL, ADD))
            V(ts(s_subg, prm("o_subln"), 1.0 - LAMBDA_INIT, None, MUL))
            norm(0, "mix0")
            v.wait_ge(lam_exp, 1)
            V(ts(s_l[3], s_l[2], 2.0, None, ADD))
            V(d.reciprocal(s_l[3], s_l[3]))
            V(tt_(s_l[3], s_l[2], s_l[3], MUL))
            V(tt_(s_l[4], s_l[3], s_l[3], MUL))
            V(ts(s_l[5], s_l[4], 1.0 / 19, None, MUL))
            for k in (17, 15, 13, 11, 9, 7, 5, 3):
                V(stt(s_l[5], s_l[5], 1.0 / k, s_l[4], ADD, MUL))
            V(stt(s_l[5], s_l[5], 1.0, s_l[3], ADD, MUL))
            V(ts(s_l[0], s_l[0], 0.0, 8.0, ALU.max, MUL))
            V(stt(s_l[5], s_l[5], 16.0, s_l[0], MUL, ADD))
            v.wait_ge(small_loaded, 16 * N_SMALL)
            V(d.tensor_copy(s_posf, POS[:, :]))
            for i, (at, w, f) in enumerate(((0, 8, "freq1"), (8, 8, "freq1"), (16, 16, "freq2"), (32, 16, "freq2"))):
                V(ts(s_ang[:, at:at + w], cst(f), s_posf[:, i:i + 1], None, MUL))
            r, rc, k_ = s_ang[:, 0:48], s_ang[:, 48:96], s_turn
            V(ts(k_, r, 1.0 / TWO_PI, None, MUL))
            V(ts(k_, k_, 12582912.0, None, ADD))
            V(ts(k_, k_, 12582912.0, None, SUB))
            c1, c2 = 6.28125, 0.0019350051879882812
            for c in (c1, c2, TWO_PI - c1 - c2):
                V(stt(r, k_, -c, r, MUL, ADD))
            V(ts(rc, r, math.pi / 2, None, ADD))
            V(ts(k_, rc, math.pi, -TWO_PI, ALU.is_gt, MUL))
            V(tt_(rc, rc, k_, ADD))
            V(ts(s_ang, s_ang, 3.1415925, -3.1415925, ALU.min, ALU.max), angles)
            lams = G_LAM.rearrange("p (a b w) -> p a b w", a=2, b=2)
            prod = SXG[:, 0:128].rearrange("p (a w) -> p a w", a=2)
            V(tt_(prod, lams[:, :, 0, :], lams[:, :, 1, :], MUL))
            V(d.reduce_sum(s_lam[:, 0:2], prod, AX), lam_dots)
            v.wait_ge(lam_exps, 1)
            V(tt_(s_lam[:, 2:3], s_lam[:, 1:2], s_lam[:, 0:1], SUB))
            V(ts(s_lam[:, 2:3], s_lam[:, 2:3], -LAMBDA_INIT, None, ADD))
            norm_out("mix0", lambda i: prm("e_ln_mix", i))

            v.wait_ge(rows_cleared, 3)
            wait_taken(v, ("w_in", 1))
            for c in range(4):
                V(ts(XC[:, c, :], LX[:, c, 0:T], prm("e_conv_w", c), prm("e_conv_b", c), MUL, ADD))
                for j in range(1, CONV):
                    V(stt(XC[:, c, :], LX[:, c, j:j + T], prm("e_conv_w", 4 * j + c), XC[:, c, :], MUL, ADD),
                      conv_ready if (c, j) == (3, CONV - 1) else None)
            for u in range(4, CT_IN // 2, 2):
                b = take(v, ("w_in", u)).rearrange("p (c t) -> p c t", c=2)
                V(d.tensor_copy(RW[:, 2 * u - 8:2 * u - 6, 1:T + 1], b), ev)
            wait_taken(v, ("w_in", 9))
            V(tt_(PS, RW[:, :, 0:T], RW[:, :, 1:T + 1], SUB))
            for c in range(CT_RW):
                V(stt(PS[:, c, :], PS[:, c, :], prm("e_shift_mu", c), RW[:, c, 1:T + 1], MUL, ADD),
                  shifted if c == CT_RW - 1 else None)
            wait_taken(v, ("lru_gate", 3))
            for c in range(4):
                V(ts(T1[:, c, :], GA[:, c, :], s_l[5][:, c:c + 1], None, MUL), decay_arg if c == 3 else None)
            v.wait_ge(decay_ready, 1)
            V(ts(T1, T2, 1.0, None, ADD))
            V(d.reciprocal(T1, T1))
            V(stt(T2, T2, 2.0, T1, MUL, MUL), root_arg)
            v.wait_ge(root_ready, 1)
            V(tt_(T2, T2, GX, MUL))
            V(tt_(T2, T2, XC, MUL))
            for c in range(4):
                V(d.tensor_tensor_scan(T1[:, c, :], GA[:, c, :], T2[:, c, :], 0.0, MUL, ADD))
            V(tt_(YT[:, 0:4, :], T1, LG, MUL), lru_done)
            wait_taken(v, ("lora", 3))
            V(ts(TMP, TMP, -math.exp(-0.5), None, MUL))
            for c in range(4):
                V(d.tensor_tensor_scan(CW[:, c, :], cst("restart"), TMP[:, c, :], 0.0, MUL, ADD))
            V(tt_(EPX, CW, TMP, SUB), cum_ready)
            for u in range(2):
                b = take(v, ("gate_g", u)).rearrange("p (c t) -> p c t", c=2)
                V(d.tensor_copy(GG[:, 2 * u:2 * u + 2, :], b), ev)
            for c in range(4):
                V(ts(KK[:, c, :], PS[:, 4 + c, :], prm("e_k_k", c), None, MUL))
            V(tt_(TMP, KK, KK, MUL), key_squares)
            wait_taken(v, ("key_norm", 1))
            V(ts(GA, GA, 1e-12, None, ALU.max))
            V(d.reciprocal(GA, GA))
            V(tt_(KK, KK, GA, MUL))
            for c in range(4):
                V(ts(TMP[:, c, :], KB[:, c, :], prm("e_k_a", c), s_omka[:, c:c + 1], MUL, ADD))
            V(tt_(PS[:, 4:8, :], PS[:, 4:8, :], TMP, MUL))
            for c in range(4):
                V(stt(TMP[:, c, :], PS[:, c, :], prm("e_r_k", c), PS[:, 4 + c, :], MUL, MUL),
                  key_squares if c == 3 else None)
            v.wait_ge(exps_ready, 1)
            V(tt_(QR[:, :, 0, :], KK, EPX, MUL))
            V(tt_(QR[:, :, 1, :], PS[:, 0:4, :], EP, MUL))
            V(tt_(KB, KB, KK, MUL))
            V(tt_(KB, KB, EN, MUL))
            V(d.tensor_copy(s_pl, EP.rearrange("p c (k t) -> p c k t", t=HALF)[:, :, :, HALF - 1]))
            V(tt_(KT, PS[:, 4:8, :], EN, MUL), chunk_ops)
            for u in range(2):
                b = take(v, ("bonus", u)).rearrange("p (c t) -> p c t", c=2)
                V(tt_(BON[:, 2 * u:2 * u + 2, :], b, PS[:, 8 + 2 * u:10 + 2 * u, :], MUL), ev)
            for u in (1, 3, 5):
                V(d.tensor_copy((TMK, TMT, TMV)[u // 2][:, 1, :], take(v, ("by_token", u))), ev)
            pair = CST[:, WHERE["before_same"][0]:WHERE["before_same"][0] + T]
            for u in range(8):
                i = 2 * u
                b = take(v, ("AB", u)).rearrange("p (h w t) -> p h w t", h=2, w=2)
                V(tt_(YI[:, i:i + 2, :], b[:, :, 0, :], bc(cst("join1_up"), 1, [P, 2, P]), MUL))
                V(tt_(B1T[:, i:i + 2, :], b[:, :, 1, :], bc(cst("until_same"), 1, [P, 2, P]), MUL), ev)
                b = take(v, ("CB", u)).rearrange("p (h t) -> p h t", h=2)
                V(tt_(CB2[:, i:i + 2, :], b, bc(pair, 1, [P, 2, T]), MUL), ev)

            def join(s, gr):
                q = slice(4 * gr, 4 * gr + 4)
                V(tt_(AM[:, q, :], AL[:, q, :], bc(cst(f"join{s}"), 1, [P, 4, P]), MUL), inverse_in)

            for u in range(4):
                q = slice(4 * u, 4 * u + 4)
                b = take(v, ("A", u)).rearrange("p (h t) -> p h t", h=4)
                V(tt_(AL[:, q, :], b, bc(cst("after_same"), 1, [P, 4, P]), MUL), ev)
                V(tt_(XI[:, q, :], AL[:, q, :], bc(cst("join1"), 1, [P, 4, P]), MUL))
                V(tt_(XI[:, q, :], bc(IDENT, 1, [P, 4, P]), XI[:, q, :], SUB))
                V(tt_(YI[:, q, :], bc(IDENT, 1, [P, 4, P]), YI[:, q, :], SUB))
                join(LEVELS[0], u)
            for n, s in enumerate(LEVELS):
                for gr in range(4):
                    q = slice(4 * gr, 4 * gr + 4)
                    b = take(v, ("dY", s, gr)).rearrange("p (h t) -> p h t", h=4)
                    V(tt_(YI[:, q, :], YI[:, q, :], b, SUB), ev)
                    if s < LEVELS[-1]:
                        b = take(v, ("dX", s, gr)).rearrange("p (h t) -> p h t", h=4)
                        V(tt_(XI[:, q, :], XI[:, q, :], b, SUB), ev)
                        join(LEVELS[n + 1], gr)
            for c in range(4):
                r = slice(64 * (c % 2), 64 * (c % 2) + 64)
                V(d.tensor_copy(ZS[r, :], take(v, ("Z", c))[r, :]), ev)
                V(ts(SAN[r, :], take(v, ("SA", c))[r, :], -1.0, None, MUL), ev)
                if c < 3:
                    b = take(v, ("dS", c)).rearrange("p (h t) -> p h t", h=4)
                    V(tt_(DS, b, bc(cst("same_head"), 1, [P, 4, P]), MUL), ev)
                    if c:
                        V(tt_(DS, DS, ST[c % 2], ADD))
                    V(tt_(ST[(c + 1) % 2], DS, bc(s_pl[:, :, c], 2, [P, 4, P]), MUL), state_ready)
            wait_taken(v, ("O", 3))
            heads = OO.rearrange("p m (h w) -> p (m h) w", w=64)
            sq = GSQ.rearrange("p m (h w) -> p (m h) w", w=64)
            V(d.reduce_sum(s_mean, heads, AX))
            V(ts(s_mean, s_mean, 1.0 / 64, None, MUL))
            V(tt_(heads, heads, bc(s_mean, 2, [P, 16, 64]), SUB))
            V(tt_(sq, heads, heads, MUL))
            V(d.reduce_sum(s_var, sq, AX))
            V(ts(s_var, s_var, 1.0 / 64, 64e-5, MUL, ADD), gn_var)
            v.wait_ge(gn_root, 1)
            V(d.reciprocal(s_var, s_var))
            V(tt_(heads, heads, bc(s_var, 2, [P, 16, 64]), MUL), gn_ready)
            for u in range(2):
                b = take(v, ("OT", u))
                for j in range(2):
                    c = 2 * u + j
                    V(ts(YT[:, 4 + c, :], b[:, j * T:(j + 1) * T], prm("e_gn_w", c), prm("e_gn_b", c), MUL, ADD),
                      ev if j else None)
            V(tt_(YT[:, 4:8, :], YT[:, 4:8, :], BON, ADD))
            V(tt_(YT[:, 4:8, :], YT[:, 4:8, :], GG, MUL), yT_ready)
            add_rows(("w_out",))

            norm(1, "ffn")
            norm_out("ffn", lambda i: prm("e_ln_ffn", i))
            v.wait_ge(bias_loaded, 16)
            V(tt_(BIAS[:, :, :], BIAS[:, :, :], bc(cst("future"), 1, [P, NE, T]), ADD))
            for i, step in enumerate(FFN_STEPS + [None]):
                if step is not None:
                    c, w, m = step
                    b = take(v, ("Up", c, m))
                    wait_taken(v, ("G", c, m))
                    V(tt_(HH[:, i % 2, 0:w], SIL[:, i % 2, 0:w], b[:, 0:w], MUL), ev)
                if i:
                    c, w, m = FFN_STEPS[i - 1]
                    for n in range(2):
                        x = X[:, m, n * BANK:(n + 1) * BANK]
                        V(tt_(x, x, take(v, ("Dn", c, m, n)), ADD), ev)

            norm(2, "mix1")
            norm_out("mix1", lambda i: prm("o_ln_mix", i))
            for c in range(QKV // BANK):
                V(d.tensor_copy(QKVB[:, 1, c * BANK:(c + 1) * BANK], take(v, ("qkv", c, 1))), ev)
            head_norm(1, SQ.rearrange("p m (g w) -> p (m g) w", w=64), lambda m: QKVB[:, m, 0:2048], G_QK, 64, 64)
            v.wait_ge(sines, 1)
            qk4 = QKVB[:, :, 0:2048].rearrange("p m (g w) -> p m g w", w=64)
            rotate(qk4[:, :, :, 0:8], qk4[:, :, :, 8:16], s_ang[:, 0:16], s_ang[:, 48:64], ROT, 32, 8)
            t2, t3 = (ROT[:, i, :].rearrange("p (m g w) -> p m g w", m=TT, w=8) for i in (2, 3))
            V(tt_(qk4[:, :, :, 8:16], t2, t3, ADD), qk_ready)
            for u in range(1, 8, 2):
                b = take(v, ("qkT", u)).rearrange("p (g t) -> p g t", g=2)
                V(d.tensor_copy(QKT[:, 2 * u:2 * u + 2, :], b), ev)
            attention("diff", DIFF_STEPS, 0, SS, EE, AT,
                      lambda g, w: bc(cst("future")[:, T - w:T], 1, [P, 2, w]), None, 0.125)
            v.wait_ge(o_squares, 1)
            V(d.reduce_sum(s_mean, SQ[:, 0, :].rearrange("p (g w) -> p g w", w=P), AX))
            V(ts(s_mean, s_mean, 1.0 / P, 1e-6, MUL, ADD), o_sums)
            v.wait_ge(o_roots, 1)
            V(d.reciprocal(s_mean, s_mean))
            oh = OA.rearrange("p m (g w) -> p (m g) w", w=P)
            V(tt_(oh, oh, bc(s_mean, 2, [P, 16, P]), MUL), o_ready)
            for u in (1, 3):
                b = take(v, ("oT", u)).rearrange("p (g t) -> p g t", g=2)
                V(ts(XT[:, 2 * u:2 * u + 2, :], b, s_subg, None, MUL), ev)
            add_rows(("w_o",))

            norm(3, "moe")
            norm_out("moe", lambda i: prm("o_ln_ffn", i))
            v.wait_ge(moe_gain_loaded, 16)
            V(tt_(XN[:, :, :], XN[:, :, :], bc(GMOE, 1, [P, TT, D]), MUL), moe_in)
            b = take(v, "router")
            V(d.tensor_copy(s_lg, b[:, 0:TT * NE].rearrange("p (m e) -> p m e", m=TT)), ev)
            for m in range(TT):
                V(d.max(s_mx[:, m, :], s_lg[:, m, :]))
                V(d.max_index(IX[:, m, :], s_mx[:, m, :], s_lg[:, m, :]))
            V(d.tensor_copy(s_ixf, IX[:, :, :]))
            V(tt_(s_w[:, 0:TT], s_mx[:, :, 1], s_mx[:, :, 0], SUB), gap_ready)
            v.wait_ge(gap_exp, 1)
            V(ts(s_w[:, 0:TT], s_w[:, TT:2 * TT], 1.0, None, ADD))
            V(d.reciprocal(s_w[:, 0:TT], s_w[:, 0:TT]))
            V(tt_(s_w[:, TT:2 * TT], s_w[:, TT:2 * TT], s_w[:, 0:TT], MUL))
            for m in range(TT):
                for k in range(2):
                    V(ts(s_oh[:, k, m, :], cst("count8"), s_ixf[:, m, k:k + 1], None, ALU.is_equal))
            V(tt_(s_mask, s_oh[:, 0], s_oh[:, 1], ADD), choices)
            for m in range(TT):
                c8 = s_comb[:, m, 0:NE]
                V(ts(c8, s_oh[:, 0, m, :], s_w[:, m:m + 1], None, MUL))
                V(stt(c8, s_oh[:, 1, m, :], s_w[:, TT + m:TT + m + 1], c8, MUL, ADD))
            b = take(v, "places")
            p8 = s_place[:, :, 0:NE]
            V(ts(p8, b[:, 0:TT * NE].rearrange("p (m e) -> p m e", m=TT), 1.0, None, ADD))
            V(ts(s_over, b[:, 2 * NE:3 * NE], float(P), None, ALU.is_gt), ev)
            V(tt_(p8, p8, s_mask, MUL))
            V(ts(p8, p8, -1.0, None, ADD))
            V(d.tensor_tensor_scan(s_rank, cst("ones")[:, 0:NE], s_over, 0.0, MUL, ADD))
            V(d.memset(s_item, 0.0))
            V(d.tensor_copy(s_item[:, 0:NE], cst("count8")))
            V(ts(s_item[:, 12:13], s_rank[:, NE - 1:NE], float(NE), None, ADD))
            V(tt_(s_rank, s_rank, s_over, SUB))
            for j in range(ITEMS - NE):
                V(ts(s_pick, s_rank, float(j), None, ALU.is_equal))
                V(tt_(s_pick, s_pick, s_over, MUL))
                V(tt_(s_junk, s_pick, cst("count8"), MUL))
                V(d.reduce_sum(s_item[:, NE + j:NE + j + 1], s_junk, AX))
                for table in (s_place, s_comb):
                    V(tt_(s_lg, table[:, :, 0:NE], bc(s_pick, 1, [P, TT, NE]), MUL))
                    V(d.reduce_sum(table[:, :, NE + j], s_lg, AX))
                V(ts(s_place[:, :, NE + j], s_place[:, :, NE + j], float(-P), None, ADD))
            V(d.tensor_copy(ITEM[0:1, :], s_item[0:1, :]), items_ready)
            v.sem_inc(m_emptied["v"], E_BY["v"])
            v.sem_inc(w_low, N_SPLIT)
            me = m_emptied["v"]
            with v.Fori(0, v.value_load(ITEM[0:1, 12:13], min_val=NE, max_val=ITEMS)) as it:
                v.wait_ge(me, it * E_BY["v"] + E_BY["v"])
                for m in range(TT):
                    place, comb = s_place[:, m, bass.ds(it, 1)], s_comb[:, m, bass.ds(it, 1)]
                    ts(PCMB[:, m, :], cst("count128"), place, comb, ALU.is_equal, MUL).then_inc(m_combs, 1)
                    ts(PSEL[:, m, :], cst("count128"), place, None, ALU.is_equal).then_inc(m_places, 1)

                def low_parts(*halves):
                    for g in halves:
                        if g < N_SPLIT:
                            v.wait_ge(w_high, it * N_SPLIT + (g + 1))
                            tt_(WL[g % E_SPLITS], half(E_TILES.index(SPLIT[g]) % E_SLOTS),
                                WH[g % E_SPLITS].bitcast(F32), SUB).then_inc(w_low, 1)

                low_parts(0, 1)
                for u in range(2):
                    b = e_take(v, it, ("XG", u)).rearrange("p (k s) -> p k s", k=4)
                    v.wait_ge(xg_high, it * 2 + (u + 1))
                    k4 = slice(4 * u, 4 * u + 4)
                    tt_(XGL[:, k4, :], b, XGH[:, k4, :].bitcast(F32), SUB).then_inc(me, 1)
                low_parts(2, 3)
                for c in range(EC + 1):
                    if c < EC:
                        low_parts(4 * c + 4, 4 * c + 5)
                        b = e_take(v, it, ("Up", c))
                        e_wait_taken(v, it, ("G", c))
                        tt_(HH[:, c % 2, :], SIL[:, c % 2, :], b, MUL).then_inc(me, 1)
                        low_parts(4 * c + 6, 4 * c + 7)
                    if c:
                        for n in range(2):
                            y = YE[:, n * BANK:(n + 1) * BANK]
                            b = e_take(v, it, ("Dn", c - 1, n))
                            if c == 1:
                                d.tensor_copy(y, b).then_inc(me, 1)
                            else:
                                e_wait_taken(v, it, ("Dn", c - 2, n))
                                tt_(y, y, b, ADD).then_inc(me, 1)
                for m in range(TT):
                    for n in range(2):
                        x = X[:, m, n * BANK:(n + 1) * BANK]
                        tt_(x, x, e_take(v, it, ("Y", m, n)), ADD).then_inc(me, 1)
            V(d.memset(s_junk, 0.0), v_ended)
            v.sem_inc(x_ready, 1)

            for l in range(DEPTH2):
                norm(4 + l, ("h", l))
                V(stt(s_gs, s_mod[:, 24 * l + 8:24 * l + 16], 1.0, prms("norm_g_2", 8, 8 * l), ADD, MUL), mod_ready)
                for n in range(2):
                    V(d.tensor_copy(GATE[:, n * BANK:(n + 1) * BANK], take(v, ("mod_gate", l, n))), ev)
                norm_out(("h", l), lambda i: s_gs[:, i:i + 1], lambda i: s_mod[:, 24 * l + i:24 * l + i + 1])

                def z_out(c):
                    c0, n = (0, HEAD0) if c == 0 else (HEAD0 + (c - 1) * BANK, BANK)
                    V(d.tensor_copy(ZB[:, 1, c0:c0 + n], take(v, ("z", l, c, 1))[:, 0:n]), ev)

                z_out(0)
                v.wait_ge(qk_squares, 3 * l + 2)
                V(ts(s_qk[:, 0:2], s_qk[:, 0:2], 1.0 / 256, 1e-6, MUL, ADD))
                V(ts(s_qk[:, 2:4], s_qk[:, 2:4], 1.0 / 128, 1e-6, MUL, ADD), qk_sums)
                v.wait_ge(qk_roots, 3 * l + 2)
                V(d.reciprocal(s_qk[:, 0:4], s_qk[:, 0:4]))
                for m in range(TT):
                    V(ts(CN[:, m, 0:256], ZB[:, m, 0:256], s_qk[:, m:m + 1], None, MUL))
                    V(ts(CN[:, m, 256:384], ZB[:, m, ZC:ZC + 128], s_qk[:, 2 + m:3 + m], None, MUL),
                      qk_ready if m else None)
                for c in range(1, 6):
                    z_out(c)
                for c, (dst, n) in enumerate(((QK[:, 1, 0:512], 512), (QK[:, 1, 512:768], 256),
                                              (KV[:, 1, 0:512], 512), (KV[:, 1, 512:1024], 512))):
                    V(d.tensor_copy(dst, take(v, ("up", l, c, 1))[:, 0:n]), ev)
                wait_taken(v, ("up", l, 3, 0))
                keys = QK[:, :, 768:1536].rearrange("p m (h w) -> p m h w", w=96)
                V(d.tensor_copy(keys[:, :, :, 0:64], KV.rearrange("p m (h w) -> p m h w", w=P)[:, :, :, 0:64]))
                V(d.tensor_copy(keys[:, :, :, 64:96], bc(ZB[:, :, ZR:ZR + 32], 2, [P, TT, 8, 32])), qk_built)
                head_norm(3 * l + 3, SQ2.rearrange("p m (g w) -> p (m g) w", w=96), lambda m: QK[:, m, :],
                          G_MLA[l], 32, 96)
                q4 = QK.rearrange("p m (g w) -> p m g w", w=96)
                rotate(q4[:, :, :, 64:80], q4[:, :, :, 80:96], s_ang[:, 16:48], s_ang[:, 64:96], ROT2, 16, 16)
                t2, t3 = (ROT2[:, i, :].rearrange("p (m g w) -> p m g w", m=TT, w=16) for i in (2, 3))
                V(tt_(q4[:, :, :, 80:96], t2, t3, ADD), qk_ready)
                for u in range(1, 8, 2):
                    b = take(v, ("mlaT", l, u)).rearrange("p (g t) -> p g t", g=2)
                    V(d.tensor_copy(QKT2[0:96, 2 * u:2 * u + 2, :], b[0:96]), ev)
                attention(("mla", l), PAIR_STEPS, 16 + 16 * l, SS2, EE2, None,
                          lambda g, w: bc(cst("future")[:, T - w:T], 1, [P, 2, w]), None, 96 ** -0.5)
                head_norm(3 * l + 4, SQ2.rearrange("p a b -> p (a b)")[:, 0:2048].rearrange("p (g w) -> p g w", w=64),
                          lambda m: ZB[:, m, ZQ:ZQ + 1024], G_MOBA[l], 32, 64)
                V(d.memset(s_junk, 0.0), qk_ready)
                for u in (1, 3):
                    b = take(v, ("mobaT", l, u)).rearrange("p (g t) -> p g t", g=2)
                    V(d.tensor_copy(QKT2[:, 2 * u:2 * u + 2, :], b), ev)
                attention(("moba", l), PAIR_STEPS, 24 + 16 * l, SS2, EE2, None,
                          lambda g, w: BIAS[:, 2 * g:2 * g + 2, T - w:T], 0.125, None)
                v.wait_ge(gate_silu, l + 1)
                wait_taken(v, (("moba", l), "values", 7))
                V(tt_(O2[:, :, 0:512], O2[:, :, 0:512], ZB[:, :, ZG:ZG + 512], MUL))
                V(tt_(O2[:, :, 512:1024], O2[:, :, 512:1024], ZB[:, :, ZGB:ZGB + 512], MUL), o_ready)
                for u in (1, 3):
                    b = take(v, ("yT", l, u)).rearrange("p (g t) -> p g t", g=2)
                    V(d.tensor_copy(XT[:, 2 * u:2 * u + 2, :], b), ev)
                for c in range(2):
                    for m in range(TT):
                        tmp = SQ2[:, 0, 0:BANK]
                        V(tt_(tmp, GATE[:, c * BANK:(c + 1) * BANK], take(v, ("w_out", l, c, m)), MUL), ev)
                        x = X[:, m, c * BANK:(c + 1) * BANK]
                        V(tt_(x, x, tmp, ADD), x_ready if (c, m) == (1, 1) else None)

        @block.scalar
        def _(act):
            A = Chain(act, a_done)
            f = nc.scalar.activation
            ea = emptied["a"]

            def norm(n, tag, gain, shift=None, between=None):
                wait_x(act, n)
                if n:
                    act.wait_ge(mean_square, n)
                A(f(XN[:, 0, :], X[:, 0, :], ACT.Square, accum_out=s_ss[:, 0:1]))
                A(f(XN[:, 1, :], X[:, 1, :], ACT.Square, accum_out=s_ss[:, 1:2]), squares)
                if between:
                    between()
                for u in (0, 2):
                    b = take(act, (tag, "xT", u))
                    for k in range(2):
                        src, dst = b[:, k * T:(k + 1) * T], XT[:, 2 * u + k, :]
                        bias = 0.0 if shift is None else shift(2 * u + k)
                        A(f(dst, src, ACT.Copy if shift is None else ACT.Identity, bias=bias,
                            scale=gain(2 * u + k)), ea if k else None)

            def attention(tag, steps, base, ss, ee, pt, out, scale, vd):
                n_c = 1 if vd == P else 2

                def exponentials(i):
                    g, m = steps[i]
                    w = (m + 1) * P
                    act.wait_ge(maxima, base + i + 1)
                    if i >= 2:
                        act.wait_ge(weights, base + i - 1)
                        act.wait_ge(filled, PLAN.filled((tag, "weightsT", i - 2)))
                    for c in range(2):
                        A(f(ee[:, i % 2, c, 0:w], ss[:, i % 2, c, 0:w], ACT.Exp, bias=s_nm[:, i % 2, c:c + 1],
                            scale=scale, accum_out=s_sm[:, i % 2, c:c + 1]), exps if c else None)

                exponentials(0)
                for i, (g, m) in enumerate(steps):
                    if i + 1 < len(steps):
                        exponentials(i + 1)
                    b = take(act, (tag, "weightsT", i))
                    if i >= 2:
                        act.wait_ge(filled, PLAN.filled((tag, "values", i - 2)))
                    src = b[:, 0:n_c * T].rearrange("p (c k q) -> p c k q", c=n_c, k=2)[:, :, 0:m + 1, :]
                    if n_c == 1:
                        A(f(pt[:, i % 2, 0, 0:m + 1, :], src[:, 0], ACT.Copy), ea)
                    else:
                        A(f(pt[:, i % 2, :, 0:m + 1, :], src, ACT.Copy), ea)
                    b = take(act, (tag, "values", i))
                    if n_c == 1:
                        A(f(out[:, m, g * P:(g + 1) * P], b[:, 0:P], ACT.Copy), ea)
                    else:
                        act.wait_ge(weights, base + i + 1)
                        for c in range(2):
                            A(f(out(m, 2 * g + c), b[:, c * 64:(c + 1) * 64], ACT.Copy,
                                scale=s_rcb[:, i % 2, c:c + 1]), ea if c else None)

            def halves(name, units, dst, rows=P):
                for u in range(0, units, 2):
                    b = take(act, name + (u,)).rearrange("p (g t) -> p g t", g=2)
                    A(f(dst[0:rows, 2 * u:2 * u + 2, :], b[0:rows], ACT.Copy), ea)

            def root(n, ready, to, a):
                act.wait_ge(ready, n)
                A(f(a, a, ACT.Sqrt), to)

            def start():
                act.wait_ge(lam_abs, 1)
                A(f(s_l[2], s_l[1], ACT.Exp, scale=-1.0), lam_exp)
                A(f(s_cc, PRM[:, PARAM_AT["c_2"]:PARAM_AT["c_2"] + KD], ACT.Silu), c_silu)
                act.wait_ge(lam_dots, 1)
                A(f(s_lam[:, 0:2], s_lam[:, 0:2], ACT.Exp), lam_exps)
                act.wait_ge(angles, 1)
                A(f(s_ang, s_ang, ACT.Sin), sines)

            def mods(first, end):
                for i in range(first, end):
                    b = take(act, ("mod", i))
                    for j in range(4):
                        A(f(s_mod[:, 4 * i + j:4 * i + j + 1], b[:, j:j + 1], ACT.Identity,
                            bias=prm("b_ada_2", 4 * i + j)), ea if j == 3 else None)

            norm(0, "mix0", lambda i: prm("e_ln_mix", i), between=start)
            act.wait_ge(rows_cleared, 3)
            for u in (0, 1, 2, 3, 5, 7, 9):
                b = take(act, ("w_in", u)).rearrange("p (c t) -> p c t", c=2)
                if u < 2:
                    A(f(LX[:, 2 * u:2 * u + 2, CONV - 1:CONV - 1 + T], b, ACT.Copy), ea)
                elif u < 4:
                    A(f(LG[:, 2 * u - 4:2 * u - 2, :], b, ACT.Gelu_apprx_tanh), ea)
                else:
                    A(f(RW[:, 2 * u - 8:2 * u - 6, 1:T + 1], b, ACT.Copy), ea)
            for u in range(4):
                b = take(act, ("lru_gate", u))
                for j in range(2):
                    c = 2 * (u % 2) + j
                    dst, bias = ((GA, "e_gate_a_b"), (GX, "e_gate_x_b"))[u // 2]
                    A(f(dst[:, c, :], b[:, j * T:(j + 1) * T], ACT.Sigmoid, bias=prm(bias, c)), ea if j else None)
            act.wait_ge(shifted, 1)
            A(f(TWX[0:64, :], PS[0:64, 12, :], ACT.Tanh), lora_in)
            A(f(SXG, PS[:, 13, :], ACT.Sigmoid), lora_in)
            act.wait_ge(decay_arg, 1)
            A(f(T2, T1, ACT.Tanh))
            A(f(GA, T1, ACT.Exp, scale=-1.0), decay_ready)
            root(1, root_arg, root_ready, T2)
            act.wait_ge(lru_done, 1)
            for u in range(4):
                b = take(act, ("lora", u))
                for j in range(2):
                    c = 2 * (u % 2) + j
                    dst, bias = ((TMP, "e_w0"), (KB, "e_a0"))[u // 2]
                    A(f(dst[:, c, :], b[:, j * T:(j + 1) * T], ACT.Sigmoid, bias=prm(bias, c)), ea if j else None)
            mods(*MOD_AT["gate_g"])
            act.wait_ge(cum_ready, 1)
            A(f(EP, CW, ACT.Exp))
            A(f(EN, CW, ACT.Exp, scale=-1.0))
            A(f(EPX, EPX, ACT.Exp), exps_ready)
            for u in range(2):
                b = take(act, ("key_norm", u)).rearrange("p (c t) -> p c t", c=2)
                A(f(GA[:, 2 * u:2 * u + 2, :], b, ACT.Sqrt), ea)
            mods(*MOD_AT["key_norm"])
            mods(*MOD_AT["bonus"])
            for u in (0, 2, 4):
                A(f((TMK, TMT, TMV)[u // 2][:, 0, :], take(act, ("by_token", u)), ACT.Copy), ea)
            for s in LEVELS:
                for gr in range(4):
                    b = take(act, ("U", s, gr)).rearrange("p (h t) -> p h t", h=4)
                    A(f(UU[:, 4 * gr:4 * gr + 4, :], b, ACT.Copy), ea)
            for h in range(NE):
                A(f(ROWB[h // 4][:, h % 4, :], take(act, ("bias", h))[:, 0:BIAS_ROW], ACT.Copy),
                  ea)
            for c in range(4):
                r = slice(64 * (c % 2), 64 * (c % 2) + 64)
                A(f(OO[r, c // 2, :], take(act, ("O", c))[r, :], ACT.Copy), ea)
                mods(*MOD_AT[c])
            root(1, gn_var, gn_root, s_var)

            norm(1, "ffn", lambda i: prm("e_ln_ffn", i))
            act.wait_ge(bias_saved, 32)
            for i, step in enumerate(FFN_STEPS + [None]):
                if step is not None:
                    c, w, m = step
                    b = take(act, ("G", c, m))
                    if i >= 2:
                        wait_taken(act, ("Up", FFN_STEPS[i - 2][0], FFN_STEPS[i - 2][2]))
                    A(f(SIL[:, i % 2, 0:w], b[:, 0:w], ACT.Silu), ea)
                if i:
                    c, w, m = FFN_STEPS[i - 1]
                    b = take(act, ("hT", c, m))
                    if i >= 3:
                        c_, _, m_ = FFN_STEPS[i - 3]
                        act.wait_ge(filled, PLAN.filled(("Dn", c_, m_, 1)))
                    A(f(HT[:, (i - 1) % 2, 0:w // P, :], b[:, 0:w].rearrange("p (k s) -> p k s", s=P), ACT.Copy), ea)

            norm(2, "mix1", lambda i: prm("o_ln_mix", i))
            for c in range(QKV // BANK):
                A(f(QKVB[:, 0, c * BANK:(c + 1) * BANK], take(act, ("qkv", c, 0)), ACT.Copy), ea)
            wait_taken(act, ("qkv", 3, 1))
            A(f(SQ[:, 0, :], QKVB[:, 0, 0:2048], ACT.Square))
            A(f(SQ[:, 1, :], QKVB[:, 1, 0:2048], ACT.Square), qk_squares)
            root(1, qk_sums, qk_roots, s_qk)
            halves(("qkT",), 8, QKT)
            attention("diff", DIFF_STEPS, 0, SS, EE, PT, OA, 0.125, P)
            A(f(SQ[:, 0, :], OA.rearrange("p m c -> p (m c)"), ACT.Square), o_squares)
            root(1, o_sums, o_roots, s_mean)
            for u in (0, 2):
                b = take(act, ("oT", u)).rearrange("p (g t) -> p g t", g=2)
                A(f(XT[:, 2 * u:2 * u + 2, :], b, ACT.Copy, scale=s_subg), ea)

            norm(3, "moe", lambda i: prm("o_ln_ffn", i))
            act.wait_ge(gap_ready, 1)
            A(f(s_w[:, TT:2 * TT], s_w[:, 0:TT], ACT.Exp), gap_exp)
            act.wait_ge(items_ready, 1)
            act.sem_inc(m_emptied["a"], E_BY["a"])
            me = m_emptied["a"]
            with act.Fori(0, act.value_load(ITEM[0:1, 12:13], min_val=NE, max_val=ITEMS)) as it:
                def high_parts(*halves):
                    for g in halves:
                        if g < N_SPLIT:
                            kind, c_, _ = SPLIT[g - E_SPLITS]
                            n = E_PLAN.index[(kind, c_)] + 1
                            act.wait_ge(m_filled, it * E_N + (n + E_N if g >= E_SPLITS else n))
                            f(WH[g % E_SPLITS], e_tile(act, it, SPLIT[g]), ACT.Copy).then_inc(w_high, 1)

                high_parts(0, 1, 2, 3)
                for u in range(2):
                    b = e_take(act, it, ("XG", u)).rearrange("p (k s) -> p k s", k=4)
                    f(XGH[:, 4 * u:4 * u + 4, :], b, ACT.Copy).then_inc(xg_high, 1)
                b = e_take(act, it, "PCT")[:, 0:T].rearrange("p (m t) -> p m t", m=TT)
                f(PCT, b, ACT.Copy).then_inc(me, 1)
                for c in range(EC + 1):
                    if c < EC:
                        b = e_take(act, it, ("G", c))
                        if c >= 2:
                            e_wait_taken(act, it, ("Up", c - 2))
                        f(SIL[:, c % 2, :], b, ACT.Silu).then_inc(me, 1)
                    if c:
                        b = e_take(act, it, ("hT", c - 1)).rearrange("p (k s) -> p k s", k=4)
                        if c >= 3:
                            n = E_PLAN.index[("Dn", c - 3, 1)]
                            act.wait_ge(m_filled, it * E_N + (E_N + n + 1))
                        f(HT[:, (c - 1) % 2], b, ACT.Copy).then_inc(me, 1)
                    high_parts(*range(4 * c + 4, 4 * c + 8))

            for l in range(DEPTH2):
                norm(4 + l, ("h", l), lambda i: s_gs[:, i:i + 1], lambda i: s_mod[:, 24 * l + i:24 * l + i + 1],
                     between=lambda: act.wait_ge(mod_ready, l + 1))

                def z_out(c):
                    c0, n = (0, HEAD0) if c == 0 else (HEAD0 + (c - 1) * BANK, BANK)
                    A(f(ZB[:, 0, c0:c0 + n], take(act, ("z", l, c, 0))[:, 0:n], ACT.Copy), ea)

                z_out(0)
                wait_taken(act, ("z", l, 0, 1))
                for i, (c0, n, m) in enumerate(((0, 256, 0), (0, 256, 1), (ZC, 128, 0), (ZC, 128, 1))):
                    A(f(SQ2[:, 0, 0:n], ZB[:, m, c0:c0 + n], ACT.Square, accum_out=s_qk[:, i:i + 1]),
                      qk_squares if i == 3 else None)
                root(3 * l + 2, qk_sums, qk_roots, s_qk[:, 0:4])
                for c in range(1, 6):
                    z_out(c)
                b = take(act, ("cT", l, 0))
                for k in range(2):
                    A(f(CT[:, k, :], b[:, k * T:(k + 1) * T], ACT.Copy, scale=prm("mla_q_norm_g_2", 2 * l + k)),
                      ea if k else None)
                A(f(CT3, take(act, ("cT", l, 1))[:, 0:T], ACT.Copy, scale=prm("mla_kv_norm_g_2", l)), ea)
                for c, (dst, n) in enumerate(((QK[:, 0, 0:512], 512), (QK[:, 0, 512:768], 256),
                                              (KV[:, 0, 0:512], 512), (KV[:, 0, 512:1024], 512))):
                    A(f(dst, take(act, ("up", l, c, 0))[:, 0:n], ACT.Copy), ea)
                act.wait_ge(qk_built, l + 1)
                A(f(SQ2, QK, ACT.Square), qk_squares)
                root(3 * l + 3, qk_sums, qk_roots, s_qk[:, 0:32])
                halves(("mlaT", l), 8, QKT2, 96)
                attention(("mla", l), PAIR_STEPS, 16 + 16 * l, SS2, EE2, PT2,
                          lambda m, h: O2[:, m, h * 64:(h + 1) * 64], 96 ** -0.5, 64)
                act.wait_ge(qk_ready, 1 + 3 * l + 2)
                flat = SQ2.rearrange("p a b -> p (a b)")[:, 0:2048].rearrange("p (m c) -> p m c", m=TT)
                A(f(flat, ZB[:, :, ZQ:ZQ + 1024], ACT.Square), qk_squares)
                root(3 * l + 4, qk_sums, qk_roots, s_qk[:, 0:32])
                halves(("mobaT", l), 4, QKT2)
                attention(("moba", l), PAIR_STEPS, 24 + 16 * l, SS2, EE2, PT2,
                          lambda m, h: O2[:, m, 512 + h * 64:512 + (h + 1) * 64], 1.0, 64)
                for g0 in (ZG, ZGB):
                    A(f(ZB[:, :, g0:g0 + 512], ZB[:, :, g0:g0 + 512], ACT.Silu), gate_silu if g0 == ZGB else None)
                halves(("yT", l), 4, XT)


def packed(inputs):
    rows = []
    for part in (PARAM_ROWS, PARAM_ROWS_2):
        a = np.concatenate([np.asarray(inputs[n]).reshape(-1, P) for n, _ in part])
        rows.append(a)
    each = [inputs["o_q_norm"][0], inputs["o_k_norm"][0]]
    for l in range(DEPTH2):
        each += [inputs["mla_q_g_2"][l], inputs["mla_k_g_2"][l]]
    for l in range(DEPTH2):
        each += [inputs["moba_q_g_2"][l], inputs["moba_k_g_2"][l]]
    each += [inputs[n][0] for n in ("o_lambda_q1", "o_lambda_k1", "o_lambda_q2", "o_lambda_k2")]
    return [("rows0", rows[0]), ("rows1", rows[1]), ("gains", np.concatenate([np.asarray(a) for a in each])),
            ("lora", np.concatenate([np.asarray(inputs["e_w2"])[0], np.asarray(inputs["e_a2"])[0]])),
            ("pos", np.stack([np.asarray(inputs["positions"])[0], np.asarray(inputs["positions_2"])[0]])
             .reshape(2, TT, P))]


def kernel(**inputs):
    import concourse.bacc as bacc
    from concourse.bass_utils import run_bass_kernel_spmd

    nc = bacc.Bacc("TRN2", target_bir_lowering=False, num_devices=1)
    arrays, aps = {}, {}
    given = [(n, np.ascontiguousarray(inputs[n])) for n in NAMES] + packed(inputs)
    for name, a in given + [("const_table", CONSTS), ("bucket_table", bucket_table())]:
        arrays[f"in_{name}"] = a
        aps[name] = nc.dram_tensor(f"in_{name}", a.shape, mybir.dt.from_np(a.dtype), kind="ExternalInput").ap()
    out = nc.dram_tensor("out_0", (1, T, D), F32, kind="ExternalOutput").ap()
    build(nc, aps, aps["const_table"], aps["bucket_table"], out)
    r = run_bass_kernel_spmd(nc, [arrays], core_ids=[0])
    return r.results[0]["out_0"]
```

```python
import math
from contextlib import ExitStack

import numpy as np

import concourse.bass as bass
from concourse import mybir

F32 = mybir.dt.float32
F32R = mybir.dt.float32r
I32 = mybir.dt.int32
U32 = mybir.dt.uint32
ALU = mybir.AluOpType
ACT = mybir.ActivationFunctionType
AX = mybir.AxisListType.X

P = 128
T = 256
TT = T // P
D = 1024
KD = D // P
BANK = 512
W = 512
NC4 = W // P
HALF = 64
EVEN_IN = 2816
CT_IN = EVEN_IN // P
CT_RW = CT_IN - 2 * NC4
FFN = 2816
NE = 8
EF = 3584
EC = EF // BANK
ITEMS = NE + 3
QKV = 3072
DIN2 = 2976
HEAD0 = 416
CONV = 4
HALF_TILE = 2048
RAW = 2
PAIRS = 2
E_SLOTS = 7
E_SPLITS = 3
E_BANKS = 6
LAMBDA_INIT = 0.8 - 0.6 * math.exp(-0.3)
MASKED = -1e30
TWO_PI = 2.0 * math.pi
DEPTH2 = 2


def const_tables():
    j = np.arange(P)[:, None]
    t = np.arange(P)[None, :]
    same = (j // HALF) == (t // HALF)
    parts = {
        "ident": (j == t),
        "same_head": same,
        "before_same": same & (j < t),
        "until_same": same & (j <= t),
        "after_same": same & (j > t),
        "before": (j < t),
        "ones": np.ones((P, P)),
    }
    for s in (1, 2, 4, 8, 16, 32):
        parts[f"join{s}"] = (j // (2 * s) == t // (2 * s)) & (j % (2 * s) >= s) & (t % (2 * s) < s)
    parts["join1_up"] = parts["join1"].T
    parts["future"] = np.concatenate([np.zeros((P, P)), np.where(t > j, MASKED, 0.0)], 1)
    parts["restart"] = np.broadcast_to((np.arange(T) % HALF != 0)[None, :], (P, T))
    parts["count128"] = np.broadcast_to(t, (P, P))
    parts["count8"] = np.broadcast_to(np.arange(8)[None, :], (P, 8))
    f1 = 500000.0 ** (-np.arange(0, 16, 2, dtype=np.float32) / np.float32(16))
    f2 = 10000.0 ** (-np.arange(0, 16, dtype=np.float32) / np.float32(16))
    parts["freq1"] = np.broadcast_to(f1[None, :], (P, 8))
    parts["freq2"] = np.broadcast_to(f2[None, :], (P, 16))
    at, where = 0, {}
    for name, a in parts.items():
        where[name] = (at, a.shape[1])
        at += a.shape[1]
    table = np.concatenate([np.asarray(a, np.float32) for a in parts.values()], 1)
    return np.ascontiguousarray(table), where


BIAS_ROW = 384


def bucket_table():
    dist = np.arange(T)
    nf = np.maximum(dist, 1).astype(np.float32)
    large = 16 + (np.log(nf / np.float32(16)) / np.float32(math.log(4096 / 16))
                  * np.float32(16)).astype(np.int32)
    bucket = np.where(dist < 16, dist, np.minimum(large, 31))
    out = np.zeros((32, BIAS_ROW), np.float32)
    for i in range(BIAS_ROW):
        d = 255 - i
        if d >= 0:
            out[bucket[d], i] = 1.0
    return out


CONSTS, WHERE = const_tables()
NCONST = CONSTS.shape[1]


class Plan:

    def __init__(self):
        self.by = []
        self.index = {}

    def add(self, name, who):
        self.index[name] = len(self.by)
        self.by.append(who)

    def emptied_before(self, i):
        if i < 8:
            return None
        who = self.by[i - 8]
        return who, sum(w == who for w in self.by[:i - 7])

    def filled(self, name):
        return self.index[name] + 1


def attention_fills(plan, tag, steps):
    plan.add((tag, "scores", 0), "v")
    plan.add((tag, "scores", 1), "v")
    for i in range(steps + 1):
        if i + 2 < steps:
            plan.add((tag, "scores", i + 2), "v")
        if i < steps:
            plan.add((tag, "weightsT", i), "a")
        if i:
            plan.add((tag, "values", i - 1), "a")


FFN_CHUNKS = [(c, min(BANK, FFN - c * BANK)) for c in range(-(-FFN // BANK))]
LEVELS = (2, 4, 8, 16, 32)


ADA = 12


def make_plan():
    plan = Plan()
    add = plan.add

    def norm(tag):
        for u in range(4):
            add((tag, "xT", u), "v")

    def rows(tag, n):
        for c in range(n):
            for m in range(TT):
                add((tag, c, m), "v")

    add("params", "v")
    norm("mix0")
    for u in range(CT_IN // 2):
        add(("w_in", u), "a" if u < 4 or u % 2 else "v")
    for u in range(4):
        add(("lru_gate", u), "a")
    for u in range(4):
        add(("lora", u), "a")
    for u in range(2):
        add(("gate_g", u), "v")
    for u in range(2):
        add(("key_norm", u), "a")
    for u in range(2):
        add(("bonus", u), "v")
    for u in range(6):
        add(("by_token", u), "av"[u % 2])
    for u in range(8):
        add(("AB", u), "v")
        add(("CB", u), "v")
    for u in range(4):
        add(("A", u), "v")
    for s in LEVELS:
        for g in range(4):
            add(("U", s, g), "a")
        for g in range(4):
            add(("dY", s, g), "v")
            if s < LEVELS[-1]:
                add(("dX", s, g), "v")
    for h in range(NE):
        add(("bias", h), "a")
    for tt in range(TT):
        add(("ZV", tt), "a")
        add(("OV", tt), "a")
    for c in range(4):
        if c:
            add(("Z", c), "v")
        add(("SA", c), "v")
        if c < 3:
            add(("dS", c), "v")
        add(("O", c), "a")
    for u in range(2):
        add(("OT", u), "v")
    rows("w_out", 2)
    norm("ffn")
    for c in range(len(FFN_CHUNKS) + 1):
        more = c < len(FFN_CHUNKS)
        for m in range(TT if more else 0):
            add(("G", c, m), "a")
        for m in range(TT if c else 0):
            add(("hT", c - 1, m), "v")
        for i in range(2 if c else 0):
            add(("mod", 2 * (c - 1) + i), "a")
        for m in range(TT if more else 0):
            add(("Up", c, m), "v")
        for n in range(2 if c else 0):
            for m in range(TT):
                add(("Dn", c - 1, n, m), "v")
    norm("mix1")
    for c in range(QKV // BANK):
        for m in range(TT):
            add(("qkv", c, m), "av"[m])
    for u in range(8):
        add(("qkT", u), "av"[u % 2])
    attention_fills(plan, "diff", 16)
    for u in range(4):
        add(("oT", u), "v")
    rows("w_o", 2)
    for u in range(4):
        add(("moe", "xT", u), "av"[u % 2])
    add("router", "v")
    add("places", "v")
    for l in range(DEPTH2):
        for u in range(2):
            add(("mod_gate", l, u), "v")
        for u in range(4):
            add((("h", l), "xT", u), "v")
        for c in range(6):
            for m in range(TT):
                add(("z", l, c, m), "av"[m])
        for u in range(2):
            add(("cT", l, u), "a")
        for c in range(4):
            for m in range(TT):
                add(("up", l, c, m), "av"[m])
        for u in range(4):
            add(("mobaT", l, u), "av"[u % 2])
        attention_fills(plan, ("moba", l), 8)
        for u in range(8):
            add(("mlaT", l, u), "av"[u % 2])
        attention_fills(plan, ("mla", l), 8)
        for u in range(4):
            add(("yT", l, u), "v")
        for c in range(2):
            for m in range(TT):
                add(("w_out", l, c, m), "v")
    return plan


PLAN = make_plan()


class Halves:

    def __init__(self):
        self.rows = []
        self.index = {}
        self.split = []
        self.used = {}
        self.firsts = 0

    def add(self, name, dims, src, fill, split=True):
        self.index[name] = len(self.rows)
        self.rows.append((name, dims, src, fill if not split else None))
        if split:
            self.split.append(name)
            if fill is None:
                self.firsts += 1
            self.used[name] = ("fill", fill) if fill is not None else ("half", self.firsts)

    def over_k(self, name, w, c0, n, fill):
        for j in range(2):
            src = w[j * W:(j + 1) * W, c0:c0 + n].rearrange("(k p) n -> p k n", p=P)
            self.add(name + (j,), [KD // 2, n], src, fill if j else None)


def make_halves(I):
    halves = Halves()
    for c in range(6):
        n = min(BANK, EVEN_IN - c * BANK)
        halves.over_k(("w_in", c), I["e_w_in"][0], c * BANK, n, ("w_in", (c * BANK + n) // 256 - 1))
    for c in range(2):
        halves.over_k(("w_out", c), I["e_w_out"][0], c * BANK, BANK, ("w_out", c, TT - 1))
    for c in range(len(FFN_CHUNKS) + 1):
        if c < len(FFN_CHUNKS):
            for kind, src in (("G", "e_ffn_gate"), ("Up", "e_ffn_up")):
                halves.over_k((kind, c), I[src][0], c * BANK, FFN_CHUNKS[c][1], (kind, c, TT - 1))
        for n in range(2 if c else 0):
            pc, pw = FFN_CHUNKS[c - 1]
            src = I["e_ffn_down"][0][pc * BANK:pc * BANK + pw, n * BANK:(n + 1) * BANK]
            halves.add(("Dn", pc, n), [pw // P, BANK], src.rearrange("(k p) n -> p k n", p=P), ("Dn", pc, n, TT - 1))
    for c in range(QKV // BANK):
        halves.over_k(("qkv", c), I["o_w_qkv"][0], c * BANK, BANK, ("qkv", c, TT - 1))
    for c in range(2):
        halves.over_k(("w_o", c), I["o_w_o"][0], c * BANK, BANK, ("w_o", c, TT - 1))
    for l in range(DEPTH2):
        for c in range(6):
            c0, n = (0, HEAD0) if c == 0 else (HEAD0 + (c - 1) * BANK, BANK)
            halves.over_k(("z", l, c), I["w_in_2"][l], c0, n, ("z", l, c, TT - 1))
        halves.add(("up_q", l), [2, 768], I["mla_w_uq_2"][l].rearrange("(k p) n -> p k n", p=P),
                   ("up", l, 1, TT - 1), split=False)
        halves.add(("up_kv", l), [1, 1024], I["mla_w_ukv_2"][l].rearrange("(k p) n -> p k n", p=P),
                   ("up", l, 3, TT - 1), split=False)
        for c in range(2):
            halves.over_k(("wo2", l, c), I["w_out_2"][l], c * BANK, BANK, ("w_out", l, c, TT - 1))
    return halves


PARAM_ROWS = [("e_ln_mix", 8), ("e_ln_ffn", 8), ("o_ln_mix", 8), ("o_ln_ffn", 8), ("e_conv_w", 16),
              ("e_conv_b", 4), ("e_gate_a_b", 4), ("e_gate_x_b", 4), ("e_lru_lambda", 4),
              ("e_shift_mu", CT_RW), ("e_w0", 4), ("e_a0", 4), ("e_k_k", 4), ("e_k_a", 4),
              ("e_r_k", 4), ("e_gn_w", 4), ("e_gn_b", 4), ("o_subln", 1), ("norm_g_2", 16),
              ("mla_q_norm_g_2", 4)]
PARAM_ROWS_2 = [("mla_kv_norm_g_2", 2), ("c_2", 8), ("b_ada_2", 48)]
PARAM_AT = {}
for _half, _rows in enumerate((PARAM_ROWS, PARAM_ROWS_2)):
    _at = 0
    for _name, _n in _rows:
        PARAM_AT[_name] = _half * P + _at
        _at += _n
NROWS = [sum(n for _, n in r) for r in (PARAM_ROWS, PARAM_ROWS_2)]
NPARAM = P + NROWS[1]

NAMES = ["x", "positions", "e_ln_mix", "e_w_in", "e_conv_w", "e_conv_b", "e_gate_a_w", "e_gate_a_b",
         "e_gate_x_w", "e_gate_x_b", "e_lru_lambda", "e_shift_mu", "e_w0", "e_w2", "e_a0", "e_a2",
         "e_g2", "e_k_k", "e_k_a", "e_r_k", "e_gn_w", "e_gn_b", "e_w_out", "e_ln_ffn", "e_ffn_gate",
         "e_ffn_up", "e_ffn_down", "o_ln_mix", "o_w_qkv", "o_q_norm", "o_k_norm", "o_lambda_q1",
         "o_lambda_k1", "o_lambda_q2", "o_lambda_k2", "o_subln", "o_w_o", "o_ln_ffn", "o_router",
         "o_moe_gate", "o_moe_up", "o_moe_down", "c_2", "positions_2", "norm_g_2", "w_ada_2",
         "b_ada_2", "w_in_2", "mla_q_norm_g_2", "mla_w_uq_2", "mla_kv_norm_g_2", "mla_w_ukv_2",
         "mla_q_g_2", "mla_k_g_2", "moba_q_g_2", "moba_k_g_2", "w_out_2", "rel_bias_2"]


N_SMALL = 7
DIFF_STEPS = [(h, m) for h in range(8) for m in range(TT)]
PAIR_STEPS = [(g, m) for g in range(4) for m in range(TT)]
ZC, ZR, ZG = 256, 384, HEAD0
ZQ = HEAD0 + 512
ZV = ZQ + 1024
ZGB = ZV + 512


class Chain:

    def __init__(self, eng, own):
        self.eng, self.own, self.made = eng, own, {}

    def __call__(self, instruction, to=None):
        sem = self.own if to is None else to
        self.made[sem.num] = self.made.get(sem.num, 0) + 1
        instruction.then_inc(sem, 1)
        self.eng.wait_ge(sem, self.made[sem.num])


def build(nc, I, consts, buckets, out):
    halves = make_halves(I)
    scratch = nc.dram_tensor("bias_rows", (P, W * NE), F32, kind="Internal").ap()
    ctx = ExitStack()
    with ctx:
        def sb(name, shape, dt=F32):
            return ctx.enter_context(nc.sbuf_tensor(name, shape, dt))

        def sem(name):
            return ctx.enter_context(nc.semaphore(name))

        X = sb("X", [P, TT, D])
        xn_base = -(-nc.sbuf_base // 32) * 32
        XN = sb("XN", [P, TT, D])
        xt_base = -(-nc.sbuf_base // 32) * 32
        XT = sb("XT", [P, KD, T])
        YT = sb("YT", [P, KD, T])
        CST = sb("CST", [P, NCONST])
        BIAS = sb("BIAS", [P, NE, T])
        big_base = -(-nc.sbuf_base // 32) * 32
        assert (RAW + 2 * PAIRS) * HALF_TILE == 12288
        BIG = sb("BIG", [P, 12288 + 25930])

        PRM = sb("PRM", [P, NPARAM])
        GAINS = sb("GAINS", [P, 1024])
        ROUTER = sb("ROUTER", [P, KD, NE])
        POS = sb("POS", [P, 2 * TT], I32)
        SM = sb("SM", [P, 720])
        IX = sb("IX", [P, TT, 8], U32)
        ITEM = sb("ITEM", [1, 16], I32)
        banks = [ctx.enter_context(nc.psum_tensor(f"bank{i}", [P, BANK], F32)) for i in range(8)]

        def R(at, n):
            assert at + n <= 25930
            return BIG[:, 12288 + at:12288 + at + n]

        def cst(name):
            at, n = WHERE[name]
            return CST[:, at:at + n]

        def prm(name, i=0):
            at = PARAM_AT[name] + i
            return PRM[:, at:at + 1]

        small_at = [0]

        def small(n):
            small_at[0] += n
            assert small_at[0] <= 720
            return SM[:, small_at[0] - n:small_at[0]]

        IDENT = cst("ident")

        filled = sem("bank_filled")
        emptied = {"a": sem("bank_emptied_by_scalar"), "v": sem("bank_emptied_by_vector")}
        raw_loaded = [sem(f"raw_half{i}_loaded") for i in range(RAW)]
        high_ready = sem("weight_half_high_ready")
        low_ready = sem("weight_half_low_ready")
        first_half_used = sem("first_weight_half_used")
        x_high = sem("x_high_ready")
        y_low = sem("mixer_result_low_ready")
        ada_loaded = [sem(f"ada_slot{i}_loaded") for i in range(2)]
        ada_sums = sem("ada_sums_ready")
        row_tile = sem("row_tile_done")
        v_done = sem("vector_done")
        a_done = sem("scalar_done")
        x_loaded = sem("x_loaded")
        const_loaded = sem("consts_loaded")
        rows_loaded = sem("param_rows_loaded")
        rows_cleared = sem("rows_cleared")
        lru_w_cleared = sem("lru_gate_weights_cleared")
        lru_w_loaded = sem("lru_gate_weights_loaded")
        small_loaded = sem("small_inputs_loaded")
        bias_saved = sem("bias_rows_saved")
        bias_loaded = sem("bias_loaded")
        moe_gain_loaded = sem("moe_gain_loaded")
        squares = sem("squares_ready")
        mean_square = sem("mean_square_ready")
        inverse_rms = sem("inverse_rms_ready")
        xn_ready = sem("xn_ready")
        x_ready = sem("x_ready")
        conv_ready = sem("conv_ready")
        lru_done = sem("lru_done")
        qk_built = sem("mla_keys_built")
        diff_squares = sem("diff_squares_ready")
        diff_scales = sem("diff_inverse_norms_ready")
        diff_ready = sem("diff_second_tile_ready")
        mla_scales = sem("mla_inverse_norms_ready")
        mla_ready = sem("mla_queries_and_keys_ready")
        g_done = sem("gpsimd_done")
        lam_abs = sem("lambda_abs_ready")
        lam_exp = sem("lambda_exp_ready")
        decay_arg = sem("lru_decay_arg_ready")
        decay_ready = sem("lru_decay_ready")
        root_arg = sem("lru_root_arg_ready")
        root_ready = sem("lru_root_ready")
        shifted = sem("shifted_ready")
        lora_in = sem("lora_inputs_ready")
        cum_ready = sem("cumulated_decay_ready")
        exps_ready = sem("decay_exps_ready")
        key_squares = sem("key_squares_ready")
        chunk_ops = sem("chunk_operands_ready")
        inverse_in = sem("inverse_operands_ready")
        state_ready = sem("state_ready")
        gn_ready = sem("group_norm_ready")
        gn_var = sem("group_variance_ready")
        gn_root = sem("group_root_ready")
        yT_ready = sem("mixer_result_ready")
        angles = sem("angles_ready")
        sines = sem("sines_ready")
        lam_dots = sem("lambda_dots_ready")
        lam_exps = sem("lambda_exps_ready")
        qk_sums = sem("qk_sums_ready")
        qk_squares = sem("qk_squares_ready")
        qk_roots = sem("qk_roots_ready")
        qk_ready = sem("qk_ready")
        maxima = sem("score_maxima_ready")
        exps = sem("score_exps_ready")
        weights = sem("weights_ready")
        o_squares = sem("o_squares_ready")
        o_sums = sem("o_sums_ready")
        o_roots = sem("o_roots_ready")
        o_ready = sem("o_ready")
        moe_in = sem("moe_input_ready")
        gap_ready = sem("router_gap_ready")
        gap_exp = sem("router_exp_ready")
        choices = sem("choices_ready")
        items_ready = sem("items_ready")
        m_filled = sem("expert_bank_filled")
        m_emptied = {"a": sem("expert_bank_emptied_by_scalar"),
                     "v": sem("expert_bank_emptied_by_vector")}
        m_places = sem("expert_places_ready")
        m_combs = sem("expert_weights_ready")
        v_ended = sem("vector_past_experts")
        m_loaded = [sem(f"expert_slot{i}_loaded") for i in range(E_SLOTS)]
        m_first = sem("expert_first_half_used")
        down_done = sem("expert_down_half_used")
        ye_ready = {"a": sem("expert_result_low_columns_ready"), "v": sem("expert_result_high_columns_ready")}
        xh_high = sem("expert_hidden_high_ready")
        w_high = sem("expert_weights_high_ready")
        w_low = sem("expert_weights_low_ready")
        xg_high = sem("expert_x_high_ready")
        c_silu = sem("condition_silu_ready")
        mod_ready = sem("modulation_ready")
        gate_silu = sem("output_gates_ready")
        out_saved = sem("out_saved")

        block = ctx.enter_context(nc.Block())

        def fill(pe, name):
            i = PLAN.index[name]
            before = PLAN.emptied_before(i)
            if before is not None:
                pe.wait_ge(emptied[before[0]], before[1])
            return banks[i % 8][:, :]

        def take(eng, name):
            eng.wait_ge(filled, PLAN.filled(name))
            return banks[PLAN.index[name] % 8][:, :]

        def wait_taken(eng, name):
            i = PLAN.index[name]
            who = PLAN.by[i]
            eng.wait_ge(emptied[who], sum(w == who for w in PLAN.by[:i + 1]))

        def raw(eng, name):
            i = halves.index[name]
            eng.wait_ge(raw_loaded[i % RAW], 16 * (i // RAW + 1))
            n = halves.rows[i][1][0] * halves.rows[i][1][1]
            return BIG[:, i % RAW * HALF_TILE:i % RAW * HALF_TILE + n]

        def wait_used(eng, name):
            how, what = halves.used[name]
            if how == "fill":
                eng.wait_ge(filled, PLAN.filled(what))
            else:
                eng.wait_ge(first_half_used, what)

        def split_half(pe, name):
            g = halves.split.index(name)
            pe.wait_ge(low_ready, g + 1)
            k, n = halves.rows[halves.index[name]][1]
            return [part[g % PAIRS][:, 0:k * n].rearrange("p (k n) -> p k n", k=k) for part in (WHM, WLM)]

        def at_head(tt, h):
            return tt * 8 + h % 2 * 4 + h // 2

        def v3(ap, n):
            return ap.rearrange("p (a b) -> p a b", a=n)

        PS = v3(R(0, CT_RW * T), CT_RW)
        GG = v3(R(3584, 1024), 4)
        BON = v3(R(4608, 1024), 4)
        KB = v3(R(5632, 1024), 4)
        KT = v3(R(6656, 1024), 4)
        QR = R(7680, 2048).rearrange("p (c w t) -> p c w t", c=4, w=2)
        TMK = v3(R(9728, 1024), TT)
        TMT = v3(R(10752, 1024), TT)
        TMV = v3(R(11776, 1024), TT)
        CW = v3(R(12800, 1024), 4)
        KK = v3(R(13824, 1024), 4)
        EP = v3(R(14848, 1024), 4)
        EPX = v3(R(15872, 1024), 4)
        EN = v3(R(16896, 1024), 4)
        TMP = v3(R(17920, 1024), 4)
        WLA = R(18944, 512)
        WG2 = R(19456, 512)
        RW = v3(R(20000, CT_RW * (T + 1)), CT_RW)
        TWX = R(23600, 256)
        SXG = R(23856, 256)
        GAW = v3(R(24112, 512), 4)
        GXW = v3(R(24624, 512), 4)
        LX = v3(R(7680, 4 * (T + CONV - 1)), 4)
        KN = v3(R(9728, 1024), 4)
        XC, LG = BIAS[:, 0:4, :], BIAS[:, 4:8, :]
        GA, GX = XT[:, 0:4, :], XT[:, 4:8, :]
        T1, T2 = (v3(XN[:, i, :], 4) for i in range(2))
        B1T = v3(R(12800, 2048), 16)
        CB2 = v3(R(14848, 4096), 16)
        AL = v3(R(18944, 2048), 16)
        YI = v3(R(20992, 2048), 16)
        XI = v3(R(23040, 2048), 16)
        AM = v3(R(0, 2048), 16)
        UU = XN[:, :, :].rearrange("p a b -> p (a b)").rearrange("p (a b) -> p a b", a=16)
        ST = [v3(R(2048, 512), 4), v3(R(5632, 512), 4)]
        ZS = R(2560, 512)
        ZVAL, OVAL = v3(R(0, 1024), TT), v3(R(1024, 1024), TT)
        SAN = R(3072, 512)
        OO = v3(R(6656, 1024), TT)
        GSQ = v3(R(9728, 1024), TT)
        DS = v3(R(6144, 512), 4)
        ROWB = [v3(R(18944, 4 * BIAS_ROW), 4), v3(R(23040, 4 * BIAS_ROW), 4)]
        BUCK = R(25500, BIAS_ROW)
        ROWS = R(3968, 2 * P)
        SIL = v3(R(18432, 1024), 2)
        HH = v3(R(19456, 1024), 2)
        ADAW = [v3(R(4096 * i, 4096), KD) for i in range(2)]
        ADAS = [R(8192 + 512 * i, 512) for i in range(4)]
        ADAJ = R(10240, P)
        PSEL = v3(R(23552, 256), TT)
        PCMB = v3(R(23808, 256), TT)
        PCT = v3(R(24064, 256), TT)
        YE = R(24320, 1024)

        def split_part(name, at, n, base=big_base):
            return nc.alloc_sbuf_tensor_at(name, [P, n], F32R, offset=base + 4 * at)[:, :]

        XGH = v3(split_part("expert_x_high", 12288 + 16384, 1024), KD)
        XGL = v3(split_part("expert_x_low", 12288 + 17408, 1024), KD)
        WH, WL = ([split_part(f"expert_weights_{part}{i}", E_SLOTS * HALF_TILE + (2 * i + j) * HALF_TILE, HALF_TILE)
                   for i in range(E_SPLITS)] for j, part in enumerate(("high", "low")))
        WHM, WLM = ([split_part(f"weights_{part}{i}", (RAW + 2 * i + j) * HALF_TILE, HALF_TILE)
                     for i in range(PAIRS)] for j, part in enumerate(("high", "low")))
        HTH, HTL = (split_part(f"hidden_{part}", 12288 + 20480 + 1024 * j, 1024)
                    .rearrange("p (m k s) -> p m k s", m=TT, k=4) for j, part in enumerate(("high", "low")))
        XTH = v3(split_part("x_high", 0, 2048, xn_base), KD)
        XTL = v3(split_part("x_low", 0, 2048, xt_base), KD)
        GMOE = YT[:, 0:4, :].rearrange("p a b -> p (a b)")
        QKVB = v3(R(0, 6144), TT)
        SQ = v3(R(6144, 4096), TT)
        QKT = v3(R(10240, 4096), 16)
        SS = R(14336, 1024).rearrange("p (b c k) -> p b c k", b=2, c=2)
        EE = R(15360, 1024).rearrange("p (b c k) -> p b c k", b=2, c=2)
        AT = R(16384, 512).rearrange("p (b k) -> p b k", b=2)
        PT = R(16896, 1024).rearrange("p (b c k q) -> p b c k q", b=2, c=2, k=2)
        OA = v3(R(17920, 2048), TT)
        ROT = R(19968, 2048).rearrange("p (a b) -> p a b", a=4)
        ZB = v3(R(0, TT * DIN2), TT)
        QK = v3(R(5952, 3072), TT)
        KV = v3(R(9024, 2048), TT)
        SQ2 = v3(R(11072, 3072), TT)
        QKT2 = v3(R(14144, 4096), 16)
        SS2 = R(18240, 1024).rearrange("p (b c k) -> p b c k", b=2, c=2)
        EE2 = R(19264, 1024).rearrange("p (b c k) -> p b c k", b=2, c=2)
        PT2 = R(20288, 1024).rearrange("p (b c k q) -> p b c k q", b=2, c=2, k=2)
        O2 = v3(R(21312, 2048), TT)
        GATE = R(23360, 1024)
        CN = v3(R(14144, 768), TT)
        CT = v3(R(25408, 0 + 512), 2)
        CT3 = XN[:, 0, 0:256]
        MSQ = SQ2.rearrange("p a b -> p (a b)")[:, 0:2048].rearrange("p (m c) -> p m c", m=TT)
        ROT2 = SQ2.rearrange("p a b -> p (a b)")[:, 0:2048].rearrange("p (a b) -> p a b", a=4)
        G_QK = GAINS[:, 0:128]
        G_MLA = [GAINS[:, 128 + 192 * l:320 + 192 * l] for l in range(DEPTH2)]
        G_MOBA = [GAINS[:, 512 + 128 * l:640 + 128 * l] for l in range(DEPTH2)]
        G_LAM = GAINS[:, 768:1024]
        s_ss = small(2)
        s_ms = small(2)
        s_rs = small(2)
        s_half = small(4)
        s_l = [small(4) for _ in range(6)]
        s_omka = small(4)
        s_pl = small(16).rearrange("p (c k) -> p c k", c=4)
        s_mean = small(16)
        s_var = small(16)
        s_qk = small(64)
        s_ang = small(96)
        s_turn = small(48)
        s_posf = small(4)
        s_subg = small(1)
        s_rcb = small(4).rearrange("p (b c) -> p b c", b=2)
        s_lg = small(16).rearrange("p (m e) -> p m e", m=TT)
        s_nm = small(4).rearrange("p (b c) -> p b c", b=2)
        s_sm = small(4).rearrange("p (b c) -> p b c", b=2)
        s_lam = small(4)
        s_relb = small(8)
        s_mx = small(16).rearrange("p (m e) -> p m e", m=TT)
        s_ixf = small(16).rearrange("p (m e) -> p m e", m=TT)
        s_w = small(2 * TT)
        s_oh = small(2 * TT * NE).rearrange("p (k m e) -> p k m e", k=2, m=TT)
        s_mask = small(TT * NE).rearrange("p (m e) -> p m e", m=TT)
        s_comb = small(TT * ITEMS).rearrange("p (m e) -> p m e", m=TT)
        s_place = small(TT * ITEMS).rearrange("p (m e) -> p m e", m=TT)
        s_cnt = small(NE)
        s_over = small(NE)
        s_rank = small(NE)
        s_pick = small(NE)
        s_junk = small(NE)
        s_item = small(16)
        s_cc = small(KD)
        s_mod = small(48)
        s_gs = small(KD)
        gate_d = I["o_moe_gate"].rearrange("l e (k p) f -> p (l e) k f", p=P)
        up_d = I["o_moe_up"].rearrange("l e (k p) f -> p (l e) k f", p=P)
        down_d = I["o_moe_down"].rearrange("l e (k p) d -> p (l e) k d", p=P)
        E_TILES = []
        for c in range(EC + 1):
            for kind, c_ in (("G", c), ("Up", c), ("Dn", c - 1)):
                if 0 <= c_ < EC:
                    E_TILES += [(kind, c_, 0), (kind, c_, 1)]
        TURNS = len(E_TILES) // E_SLOTS
        N_SPLIT = len(E_TILES)
        assert N_SPLIT % E_SLOTS == 0 and N_SPLIT % E_SPLITS == 0

        E_PLAN = Plan()
        for u in range(2):
            E_PLAN.add(("XG", u), "v")
        E_PLAN.add("PCT", "a")
        for c in range(EC + 1):
            if c < EC:
                E_PLAN.add(("G", c), "a")
            if c:
                E_PLAN.add(("hT", c - 1), "v")
            if c < EC:
                E_PLAN.add(("Up", c), "v")
        for m in range(TT):
            for n in range(2):
                E_PLAN.add(("Y", m, n), "v")
        E_N = len(E_PLAN.by)
        E_BY = {w: sum(b == w for b in E_PLAN.by) for w in "av"}

        def e_count(it, who, i):
            n = sum(w == who for w in E_PLAN.by[:(i + E_N if i < 0 else i) + 1])
            return it * E_BY[who] + (n if i < 0 else n + E_BY[who])

        def e_fill(pe, it, name):
            i = E_PLAN.index[name]
            k = i - E_BANKS if i >= E_BANKS else max(k for k in range(E_N) if k % E_BANKS == i % E_BANKS) - E_N
            who = E_PLAN.by[k if k >= 0 else k + E_N]
            pe.wait_ge(m_emptied[who], e_count(it, who, k))
            return banks[i % E_BANKS][:, :]

        def e_take(eng, it, name):
            eng.wait_ge(m_filled, it * E_N + (E_N + E_PLAN.index[name] + 1))
            return banks[E_PLAN.index[name] % E_BANKS][:, :]

        def e_wait_taken(eng, it, name):
            i = E_PLAN.index[name]
            eng.wait_ge(m_emptied[E_PLAN.by[i]], e_count(it, E_PLAN.by[i], i))

        def e_split_done(eng, it, g, ahead=1):
            eng.wait_ge(w_low, it * N_SPLIT + (ahead * N_SPLIT + g + 1))

        def expert_loads(sp):
            sp.wait_ge(items_ready, 1)
            with sp.Fori(0, sp.value_load(ITEM[0:1, 12:13], min_val=NE, max_val=ITEMS)) as it:
                expert = sp.value_load(ITEM[0:1, bass.ds(it, 1)], min_val=0, max_val=NE - 1)
                for q, (kind, c, j) in enumerate(E_TILES):
                    before = E_TILES[q - E_SLOTS]
                    ahead = 1 if q >= E_SLOTS else 0
                    e_split_done(sp, it, E_TILES.index(before), ahead)
                    if kind == "Dn":
                        src = down_d[:, bass.ds(expert, 1), 4 * c:4 * c + 4, j * BANK:(j + 1) * BANK]
                    else:
                        w = gate_d if kind == "G" else up_d
                        src = w[:, bass.ds(expert, 1), 4 * j:4 * j + 4, c * BANK:(c + 1) * BANK]
                    dst = half(q % E_SLOTS).rearrange("p (l k n) -> p l k n", l=1, k=4)
                    sp.dma_start(dst, src).then_inc(m_loaded[q % E_SLOTS], 16)

        def half(i):
            return BIG[:, i * HALF_TILE:(i + 1) * HALF_TILE]

        def e_tile(eng, it, name):
            q = E_TILES.index(name)
            eng.wait_ge(m_loaded[q % E_SLOTS], it * (16 * TURNS) + 16 * (q // E_SLOTS + 1))
            return half(q % E_SLOTS)

        def bc(a, axis, shape):
            return a.unsqueeze(axis).broadcast_to(shape)

        def head_scale(C, tt_, xm, m, gain, groups, width):
            g2 = groups // TT
            flat = xm.rearrange("p (g w) -> p g w", w=width)
            C(tt_(flat, flat, bc(s_qk[:, m * g2:(m + 1) * g2], 2, [P, g2, width]), ALU.mult))
            two = xm.rearrange("p (q g w) -> p q g w", q=2, w=width)
            C(tt_(two, two, bc(gain.rearrange("p (q w) -> p q w", q=2), 2, [P, 2, g2 // 2, width]), ALU.mult))

        def rotate(C, tt_, x1, x2, sin, cos, tmp, g, w, to, tiles=TT):
            t = [tmp[:, i, :].rearrange("p (m g w) -> p m g w", m=tiles, w=w) for i in range(4)]
            shape = [P, tiles, g, w]
            cs, sn = (bc(a.rearrange("p (m w) -> p m w", m=tiles), 2, shape) for a in (cos, sin))
            C(tt_(t[0], x1, cs, ALU.mult))
            C(tt_(t[1], x2, sn, ALU.mult))
            C(tt_(t[2], x2, cs, ALU.mult))
            C(tt_(t[3], x1, sn, ALU.mult))
            C(tt_(x1, t[0], t[1], ALU.subtract))
            C(tt_(x2, t[2], t[3], ALU.add), to)

        def diff_heads(C, tt_, m, to):
            head_scale(C, tt_, QKVB[:, m, 0:2048], m, G_QK, 64, 64)
            C.eng.wait_ge(sines, 1)
            x = QKVB[:, m:m + 1, 0:2048].rearrange("p m (g w) -> p m g w", w=64)
            rotate(C, tt_, x[:, :, :, 0:8], x[:, :, :, 8:16], s_ang[:, 8 * m:8 * m + 8],
                   s_ang[:, 48 + 8 * m:56 + 8 * m], ROT[:, :, 256 * m:256 * m + 256], 32, 8, to, tiles=1)

        def wait_x(eng, n):
            if n == 0:
                eng.wait_ge(x_loaded, 16)
            elif n < 4:
                wait_taken(eng, [("w_out", 1, 1), ("Dn", len(FFN_CHUNKS) - 1, 1, 1), ("w_o", 1, 1)][n - 1])
            else:
                eng.wait_ge(x_ready, n - 3)

        @block.sync
        def _(sp):
            sp.dma_start(X[:, :, :], I["x"][0].rearrange("(m p) d -> p m d", p=P)).then_inc(x_loaded, 16)
            sp.dma_start(CST[:, :], consts).then_inc(const_loaded, 16)
            for i, (name, dims, src, fill_after) in enumerate(halves.rows):
                if name == ("z", 0, 0, 0):
                    expert_loads(sp)
                    sp.wait_ge(x_ready, 1)
                elif i >= RAW:
                    before = halves.rows[i - RAW]
                    if before[3] is not None:
                        sp.wait_ge(filled, PLAN.filled(before[3]))
                    else:
                        sp.wait_ge(low_ready, halves.split.index(before[0]) + 1)
                at = i % RAW * HALF_TILE
                dst = BIG[:, at:at + dims[0] * dims[1]].rearrange("p (k n) -> p k n", k=dims[0])
                sp.dma_start(dst, src).then_inc(raw_loaded[i % RAW], 16)
            wait_x(sp, 6)
            sp.dma_start(out[0].rearrange("(m p) d -> p m d", p=P), X[:, :, :]).then_inc(out_saved, 16)
            sp.wait_ge(out_saved, 16)

        @block.gpsimd
        def _(pool):
            g = nc.gpsimd
            for half, n in enumerate(NROWS):
                pool.dma_start(ROWS[0:n, half * P:half * P + P], I[f"rows{half}"]).then_inc(rows_loaded, 16)
            loads = [(POS[:, 0:2 * TT], I["pos"].rearrange("s m p -> p (s m)")),
                     (GAINS[:, :], I["gains"].partition_broadcast(P)), (WLA, I["lora"]), (WG2, I["e_g2"][0]),
                     (s_relb[0:32, :], I["rel_bias_2"]), (BUCK[0:32, :], buckets),
                     (ROUTER[:, :, :], I["o_router"][0].rearrange("(k p) e -> p k e", p=P))]
            for dst, src in loads:
                pool.dma_start(dst, src, allow_slow_non_contiguous=True).then_inc(small_loaded, 16)
            assert len(loads) == N_SMALL
            g.memset(R(24112, 1024), 0.0).then_inc(lru_w_cleared, 1)
            g.memset(LX[:, :, 0:CONV - 1], 0.0).then_inc(rows_cleared, 1)
            g.memset(RW[:, :, 0:1], 0.0).then_inc(rows_cleared, 1)
            pool.wait_ge(lru_w_cleared, 1)
            for dst, name in ((GAW, "e_gate_a_w"), (GXW, "e_gate_x_w")):
                src = I[name][0].rearrange("(c h) i j -> h i c j", h=2)
                for h in range(2):
                    pool.dma_start(dst[64 * h:64 * h + 64, :, 64 * h:64 * h + 64], src[h])\
                        .then_inc(lru_w_loaded, 16)
            g.memset(s_half, -0.5).then_inc(rows_cleared, 1)
            pool.wait_ge(rows_cleared, 3)

            def inverse_root(n):
                pool.wait_ge(mean_square, n + 1)
                if n:
                    pool.wait_ge(xn_ready, n)
                g.tensor_tensor(out=s_rs, in0=s_ms, in1=s_half[:, 0:2], op=ALU.pow).then_inc(inverse_rms, 1)

            inverse_root(0)
            wait_taken(pool, ("bias", NE - 1))
            for i in range(2):
                rows = scratch.rearrange("q (h i) -> q h i", h=NE)[:, 4 * i:4 * i + 4, 0:BIAS_ROW]
                pool.dma_start(rows, ROWB[i]).then_inc(bias_saved, 16)
            pool.wait_ge(bias_saved, 32)
            pool.wait_ge(lru_done, 1)
            pool.dma_start(BIAS[:, :, :], bass.AP(scratch.tensor, 127, [[W * NE - 1, P], [W, NE], [1, T]]))\
                .then_inc(bias_loaded, 16)
            inverse_root(1)
            pool.wait_ge(yT_ready, 1)
            for i in range(ADA):
                if i >= 2:
                    pool.wait_ge(ada_sums, i - 1)
                src = I["w_ada_2"][i // 6][:, i % 6 * BANK:(i % 6 + 1) * BANK].rearrange("(k p) n -> p k n", p=P)
                pool.dma_start(ADAW[i % 2], src).then_inc(ada_loaded[i % 2], 16)
            pool.wait_ge(filled, PLAN.filled(("w_out", 1, 1)))
            pool.dma_start(GMOE, I["o_ln_ffn"][0].partition_broadcast(P)).then_inc(moe_gain_loaded, 16)
            inverse_root(2)
            G = Chain(pool, g_done)
            pool.wait_ge(diff_scales, 1)
            diff_heads(G, g.tensor_tensor, 1, diff_ready)
            inverse_root(3)
            for l in range(DEPTH2):
                inverse_root(4 + l)
                pool.wait_ge(mla_scales, l + 1)
                for m in range(TT):
                    head_scale(G, g.tensor_tensor, QK[:, m, :], m, G_MLA[l], 32, 96)
                q4 = QK.rearrange("p m (g w) -> p m g w", w=96)
                rotate(G, g.tensor_tensor, q4[:, :, :, 64:80], q4[:, :, :, 80:96], s_ang[:, 16:48], s_ang[:, 64:96],
                       ROT2, 16, 16, mla_ready)

        @block.tensor
        def _(pe):
            mm = nc.tensor.matmul

            def norm(n, tag):
                pe.wait_ge(xn_ready, n + 1)
                for u in range(4):
                    b = fill(pe, (tag, "xT", u))
                    for k in range(2):
                        for m in range(TT):
                            d = 2 * u + k
                            last = nc.tensor.transpose(b[:, (2 * k + m) * P:(2 * k + m + 1) * P],
                                                       XN[:, m, d * P:(d + 1) * P], IDENT)
                    last.then_inc(filled, 1)

            def product(name, lhs, w, n, kt):
                b = fill(pe, name)
                for k in range(kt):
                    last = mm(b[:, 0:n], lhs(k), w[:, k, :], start=k == 0, stop=k == kt - 1)
                last.then_inc(filled, 1)

            def three_passes(b, high_l, high_r, low_l, low_r, start, stop, signal=None, check=True):
                mm(b, high_l, high_r, start=start, stop=False, skip_group_check=not check)
                mm(b, low_l, high_r, start=False, stop=False, skip_group_check=not check)
                last = mm(b, high_l, low_r, start=False, stop=stop, skip_group_check=not check)
                if signal is not None:
                    last.then_inc(signal, 1)

            def by_token(name, tile, n, ready=None):
                b = [fill(pe, name + (m,))[:, 0:n] for m in range(TT)]
                for j in range(2):
                    if ready is not None:
                        ready(j)
                    high, low = split_half(pe, tile + (j,))
                    for m in range(TT):
                        t = slice(m * P, (m + 1) * P)
                        for k in range(4):
                            x = 4 * j + k
                            signal = (filled if j else first_half_used if m else None) if k == 3 else None
                            three_passes(b[m], XTH[:, x, t], high[:, k, :], XTL[:, x, t], low[:, k, :],
                                         x == 0, x == KD - 1, signal)

            def transposed(tag):
                return lambda j: wait_taken(pe, tag + (2 * j + 1,))

            def to_channels(name, units, src):
                for u in range(units):
                    b = fill(pe, name + (u,))
                    for rows, at, a in src(u):
                        last = nc.tensor.transpose(b[0:rows, at:at + P], a, IDENT)
                    last.then_inc(filled, 1)

            order = [0]

            def attention(tag, steps, base, ready, lhs, rhs, src, pt, value, vd, halves=True):
                n_c = 1 if vd == P else 2

                def scores(i):
                    g, m = steps[i]
                    w = (m + 1) * P
                    b = fill(pe, (tag, "scores", i))
                    first = mm(b[:, 0:w], lhs(g, 0, m), rhs(g, 0, w), start=True, stop=True)
                    if halves:
                        order[0] += 1
                        first.then_inc(row_tile, 1)
                        pe.wait_ge(row_tile, order[0])
                    mm(b[:, T:T + w], lhs(g, 1, m), rhs(g, 1, w), start=True, stop=True).then_inc(filled, 1)

                def transposes(i):
                    g, m = steps[i]
                    b = fill(pe, (tag, "weightsT", i))
                    pe.wait_ge(ready, base + i + 1)
                    for c in range(n_c):
                        for k in range(m + 1):
                            last = nc.tensor.transpose(b[:, (2 * c + k) * P:(2 * c + k + 1) * P],
                                                       src(i % 2, c, k), IDENT)
                    last.then_inc(filled, 1)

                def values(i):
                    g, m = steps[i]
                    b = fill(pe, (tag, "values", i))
                    wait_taken(pe, (tag, "weightsT", i))
                    for c in range(n_c):
                        for k in range(m + 1):
                            last = mm(b[:, c * vd:(c + 1) * vd], pt[:, i % 2, c, k, :], value(g, c, k),
                                      start=k == 0, stop=k == m)
                    last.then_inc(filled, 1)

                scores(0)
                scores(1)
                for i in range(len(steps) + 1):
                    if i + 2 < len(steps):
                        scores(i + 2)
                    if i < len(steps):
                        transposes(i)
                    if i:
                        values(i - 1)

            pe.wait_ge(const_loaded, 16)
            pe.wait_ge(rows_loaded, 16 * 2)
            b = fill(pe, "params")
            for half, n in enumerate(NROWS):
                last = nc.tensor.transpose(b[:, half * P:half * P + n], ROWS[0:n, half * P:half * P + P],
                                           IDENT[0:n, 0:n])
            last.then_inc(filled, 1)
            norm(0, "mix0")
            for c in range(6):
                units = [u for u in (2 * c, 2 * c + 1) if u < CT_IN // 2]
                b = {u: fill(pe, ("w_in", u)) for u in units}
                for j in range(2):
                    wait_taken(pe, ("mix0", "xT", 2 * j + 1))
                    high, low = split_half(pe, ("w_in", c, j))
                    for u in units:
                        for i in range(2):
                            w = slice((2 * (u % 2) + i) * P, (2 * (u % 2) + i + 1) * P)
                            for k in range(4):
                                x = 4 * j + k
                                end = k == 3 and i == 1
                                signal = (filled if j else first_half_used if u == units[-1] else None) if end else None
                                three_passes(b[u][:, i * T:(i + 1) * T], high[:, k, w], XTH[:, x, :],
                                             low[:, k, w], XTL[:, x, :], x == 0 and i == 0, end and j == 1,
                                             signal, check=False)
            pe.wait_ge(lru_w_loaded, 16 * 4)
            pe.wait_ge(conv_ready, 1)
            for u in range(4):
                w = (GAW, GXW)[u // 2]
                b = fill(pe, ("lru_gate", u))
                for j in range(2):
                    c = 2 * (u % 2) + j
                    last = mm(b[:, j * T:(j + 1) * T], w[:, c, :], XC[:, c, :], start=True, stop=True)
                last.then_inc(filled, 1)
            pe.wait_ge(lora_in, 2)
            for u in range(4):
                rows = slice(0, 64) if u < 2 else slice(64, 128)
                src = TWX[0:64, :] if u < 2 else PS[64:128, 12, :]
                b = fill(pe, ("lora", u))
                for j in range(2):
                    c = 2 * (u % 2) + j
                    last = mm(b[:, j * T:(j + 1) * T], WLA[rows, c * P:(c + 1) * P], src, start=True, stop=True)
                last.then_inc(filled, 1)
            for u in range(2):
                b = fill(pe, ("gate_g", u))
                for j in range(2):
                    c = 2 * u + j
                    last = mm(b[:, j * T:(j + 1) * T], WG2[:, c * P:(c + 1) * P], SXG, start=True, stop=True)
                last.then_inc(filled, 1)
            for name, n in (("key_norm", 1), ("bonus", 2)):
                pe.wait_ge(key_squares, n)
                for u in range(2):
                    b = fill(pe, (name, u))
                    for j in range(2):
                        last = mm(b[:, j * T:(j + 1) * T], cst("same_head"), TMP[:, 2 * u + j, :],
                                  start=True, stop=True)
                    last.then_inc(filled, 1)
            pe.wait_ge(chunk_ops, 1)
            for u in range(6):
                src = (KB, KT, PS[:, 8:12, :])[u // 2]
                b = fill(pe, ("by_token", u))
                for c in range(4):
                    last = nc.tensor.transpose(b[:, c * P:(c + 1) * P],
                                               src[:, c, (u % 2) * P:(u % 2 + 1) * P], IDENT)
                last.then_inc(filled, 1)
            for u in range(8):
                tt, h = u // 4, u // 2 % 2
                r = slice(64 * h, 64 * h + 64)
                for name, src in (("AB", KB), ("CB", KT)):
                    b = fill(pe, (name, u))
                    for j in range(2):
                        c = 2 * (u % 2) + j
                        last = mm(b[:, j * T:(j + 1) * T], src[r, c, tt * P:(tt + 1) * P],
                                  QR[r, c, :, tt * P:(tt + 1) * P], start=True, stop=True)
                    last.then_inc(filled, 1)
            for u in range(4):
                b = fill(pe, ("A", u))
                for i in range(4):
                    tt, c, r = u // 2, i, slice(64 * (u % 2), 64 * (u % 2) + 64)
                    last = mm(b[:, i * P:(i + 1) * P], QR[r, c, 0, tt * P:(tt + 1) * P],
                              KB[r, c, tt * P:(tt + 1) * P], start=True, stop=True)
                last.then_inc(filled, 1)
            for n, s in enumerate(LEVELS):
                for gr in range(4):
                    pe.wait_ge(inverse_in, 4 * n + gr + 1)
                    b = fill(pe, ("U", s, gr))
                    for i in range(4):
                        last = mm(b[:, i * P:(i + 1) * P], AM[:, 4 * gr + i, :], YI[:, 4 * gr + i, :],
                                  start=True, stop=True)
                    last.then_inc(filled, 1)
                for gr in range(4):
                    wait_taken(pe, ("U", s, gr))
                    for name in ("dY", "dX"):
                        if name == "dX" and s == LEVELS[-1]:
                            continue
                        b = fill(pe, (name, s, gr))
                        for i in range(4):
                            k = 4 * gr + i
                            lhs, rhs = (XI, UU) if name == "dY" else (UU, XI)
                            last = mm(b[:, i * P:(i + 1) * P], lhs[:, k, :], rhs[:, k, :],
                                      start=True, stop=True)
                        last.then_inc(filled, 1)
            pe.wait_ge(small_loaded, 16 * N_SMALL)
            for h in range(NE):
                b = fill(pe, ("bias", h))
                mm(b[:, 0:BIAS_ROW], s_relb[0:32, h:h + 1].broadcast_to([32, P]), BUCK[0:32, :],
                   start=True, stop=True).then_inc(filled, 1)

            for tt in range(TT):
                for name, w in (("ZV", 0), ("OV", 1)):
                    b = fill(pe, (name, tt))
                    for h in range(8):
                        last = mm(b[:, h * 64:(h + 1) * 64], CB2[:, at_head(tt, h), w * P:(w + 1) * P],
                                  TMV[:, tt, h * 64:(h + 1) * 64], start=True, stop=True)
                    last.then_inc(filled, 1)
            wait_taken(pe, ("dY", LEVELS[-1], 3))
            for c in range(4):
                tt, r = c // 2, slice(64 * (c % 2), 64 * (c % 2) + 64)
                t0 = slice(tt * P, (tt + 1) * P)

                def group(name, parts):
                    b = fill(pe, name)
                    for i, (c0, n, lhs, rhs) in enumerate(parts):
                        last = mm(b[:, c0:c0 + n], lhs, rhs, start=i == 0, stop=i == len(parts) - 1,
                                  skip_group_check=True)
                    last.then_inc(filled, 1)

                state = lambda w: [(p * P, P, QR[:, p, w, t0], ST[c % 2][:, p, :]) for p in range(4)] if c else []
                if c:
                    pe.wait_ge(state_ready, c)
                    group(("Z", c), state(0))
                    wait_taken(pe, ("Z", c))
                else:
                    wait_taken(pe, ("ZV", 0))
                z = ZS if c else ZVAL[:, 0, :]
                group(("SA", c), [(h * 64, 64, YI[r, at_head(tt, h), :], z[r, h * 64:h * 64 + 64])
                                  for h in range(8)])
                wait_taken(pe, ("SA", c))
                if c < 3:
                    group(("dS", c), [(p * P, P, a[r, tt, p * P:(p + 1) * P], b_[r, p * P:(p + 1) * P])
                                      for p in range(4) for a, b_ in ((TMK, SAN), (TMT, TMV[:, tt, :]))])
                group(("O", c), state(1)
                      + [(h * 64, 64, B1T[r, at_head(tt, h), :], SAN[r, h * 64:h * 64 + 64]) for h in range(8)])
            pe.wait_ge(gn_ready, 1)
            to_channels(("OT",), 2, lambda u: [(P, (2 * j + m) * P, OO[:, m, (2 * u + j) * P:(2 * u + j + 1) * P])
                                               for j in range(2) for m in range(TT)])
            for c in range(2):
                by_token(("w_out", c), ("w_out", c), BANK, None if c else lambda j: pe.wait_ge(y_low, j + 1))

            norm(1, "ffn")
            for c in range(len(FFN_CHUNKS) + 1):
                w = FFN_CHUNKS[c][1] if c < len(FFN_CHUNKS) else 0
                if w:
                    by_token(("G", c), ("G", c), w, None if c else transposed(("ffn", "xT")))
                if c:
                    pw = FFN_CHUNKS[c - 1][1]
                    for m in range(TT):
                        b = fill(pe, ("hT", c - 1, m))
                        wait_taken(pe, ("Up", c - 1, m))
                        for k in range(pw // P):
                            last = nc.tensor.transpose(b[:, k * P:(k + 1) * P], HH[:, m, k * P:(k + 1) * P], IDENT)
                        last.then_inc(filled, 1)
                    for i in (2 * c - 2, 2 * c - 1):
                        pe.wait_ge(ada_sums, i + 1)
                        b = fill(pe, ("mod", i))
                        for j in range(4):
                            last = nc.tensor.transpose(b[:, j * P:(j + 1) * P], ADAS[i % 4][:, j * P:(j + 1) * P], IDENT)
                        last.then_inc(filled, 1)
                if w:
                    by_token(("Up", c), ("Up", c), w)
                for n in range(2 if c else 0):
                    b = [fill(pe, ("Dn", c - 1, n, m)) for m in range(TT)]
                    wait_taken(pe, ("hT", c - 1, 1))
                    high, low = split_half(pe, ("Dn", c - 1, n))
                    for m in range(TT):
                        for k in range(pw // P):
                            three_passes(b[m], HTH[:, m, k, :], high[:, k, :], HTL[:, m, k, :], low[:, k, :],
                                         k == 0, k == pw // P - 1, filled if k == pw // P - 1 else None)

            norm(2, "mix1")
            for c in range(QKV // BANK):
                by_token(("qkv", c), ("qkv", c), BANK, None if c else transposed(("mix1", "xT")))
            pe.wait_ge(qk_ready, 1)
            pe.wait_ge(diff_ready, 1)
            to_channels(("qkT",), 8, lambda u: [(P, (2 * j + m) * P, QKVB[:, m, (2 * u + j) * P:(2 * u + j + 1) * P])
                                                for j in range(2) for m in range(TT)])
            wait_taken(pe, ("qkT", 6))
            wait_taken(pe, ("qkT", 7))
            attention("diff", DIFF_STEPS, 0, weights,
                      lambda h, c, m: QKT[64 * c:64 * c + 64, h, m * P:(m + 1) * P],
                      lambda h, c, w: QKT[64 * c:64 * c + 64, 8 + h, 0:w],
                      lambda b, c, k: AT[:, b, k * P:(k + 1) * P], PT,
                      lambda h, c, k: QKVB[:, k, 2048 + h * P:2048 + (h + 1) * P], P)
            pe.wait_ge(o_ready, 1)
            to_channels(("oT",), 4, lambda u: [(P, (2 * j + m) * P, OA[:, m, (2 * u + j) * P:(2 * u + j + 1) * P])
                                               for j in range(2) for m in range(TT)])
            for c in range(2):
                by_token(("w_o", c), ("w_o", c), BANK, None if c else transposed(("oT",)))

            pe.wait_ge(filled, PLAN.filled(("w_o", 1, 1)))
            pe.sem_inc(m_filled, E_N)
            pe.sem_inc(down_done, 2 * EC)
            norm(3, "moe")
            wait_taken(pe, ("moe", "xT", 2))
            wait_taken(pe, ("moe", "xT", 3))
            b = fill(pe, "router")
            for m in range(TT):
                for k in range(KD):
                    last = mm(b[:, m * NE:(m + 1) * NE], XT[:, k, m * P:(m + 1) * P], ROUTER[:, k, :],
                              start=k == 0, stop=k == KD - 1)
            last.then_inc(filled, 1)
            b = fill(pe, "places")
            pe.wait_ge(choices, 1)
            for at, parts in ((0, (("before", 0),)), (NE, (("ones", 0), ("before", 1))),
                              (2 * NE, (("ones", 0), ("ones", 1)))):
                for i, (a, m) in enumerate(parts):
                    last = mm(b[:, at:at + NE], cst(a), s_mask[:, m, :], start=i == 0, stop=i == len(parts) - 1)
            last.then_inc(filled, 1)
            pe.wait_ge(items_ready, 1)
            wait_taken(pe, "places")
            wait_taken(pe, ("moe", "xT", 2))
            pe.wait_ge(moe_in, 1)
            with pe.Fori(0, pe.value_load(ITEM[0:1, 12:13], min_val=NE, max_val=ITEMS)) as it:
                for u in range(2):
                    b = e_fill(pe, it, ("XG", u))
                    if u == 0:
                        pe.wait_ge(m_places, it * TT + TT)
                    for k in range(4):
                        d = 4 * u + k
                        for m in range(TT):
                            last = mm(b[:, k * P:(k + 1) * P], XN[:, m, d * P:(d + 1) * P], PSEL[:, m, :],
                                      start=m == 0, stop=m == TT - 1)
                    last.then_inc(m_filled, 1)
                b = e_fill(pe, it, "PCT")
                pe.wait_ge(m_combs, it * TT + TT)
                for m in range(TT):
                    last = nc.tensor.transpose(b[:, m * P:(m + 1) * P], PCMB[:, m, :], IDENT)
                last.then_inc(m_filled, 1)

                def e_split_half(name):
                    q = E_TILES.index(name)
                    e_split_done(pe, it, q)
                    return (part[q % E_SPLITS].rearrange("p (k n) -> p k n", k=4) for part in (WH, WL))

                def expert_product(kind, c):
                    b = e_fill(pe, it, (kind, c))
                    if c == 0 and kind == "G":
                        e_wait_taken(pe, it, ("XG", 1))
                    for j in range(2):
                        high, low = e_split_half((kind, c, j))
                        for k in range(4):
                            x = 4 * j + k
                            three_passes(b, XGH[:, x, :], high[:, k, :], XGL[:, x, :], low[:, k, :], x == 0,
                                         x == KD - 1, (m_filled if j else m_first) if k == 3 else None)

                for c in range(EC + 1):
                    if c < EC:
                        expert_product("G", c)
                    if c:
                        b = e_fill(pe, it, ("hT", c - 1))
                        e_wait_taken(pe, it, ("Up", c - 1))
                        for k in range(4):
                            last = nc.tensor.transpose(b[:, k * P:(k + 1) * P],
                                                       HH[:, (c - 1) % 2, k * P:(k + 1) * P], IDENT)
                        last.then_inc(m_filled, 1)
                    if c < EC:
                        expert_product("Up", c)
                    for n in range(2 if c else 0):
                        if n == 0:
                            e_wait_taken(pe, it, ("hT", c - 1))
                        high, low = e_split_half(("Dn", c - 1, n))
                        for k in range(4):
                            three_passes(banks[E_BANKS + n][:, :], HTH[:, (c - 1) % 2, k, :], high[:, k, :],
                                         HTL[:, (c - 1) % 2, k, :], low[:, k, :], (c, k) == (1, 0), (c, k) == (EC, 3),
                                         down_done if k == 3 else None)
                for m in range(TT):
                    for n in range(2):
                        b = e_fill(pe, it, ("Y", m, n))
                        pe.wait_ge(ye_ready["av"[n]], it + 1)
                        mm(b, PCT[:, m, :], YE[:, n * BANK:(n + 1) * BANK], start=True, stop=True)\
                            .then_inc(m_filled, 1)
            wait_x(pe, 4)

            for l in range(DEPTH2):
                for n in range(2):
                    b = fill(pe, ("mod_gate", l, n))
                    for j in range(4):
                        col = s_mod[:, 24 * l + 16 + 4 * n + j:24 * l + 17 + 4 * n + j]
                        last = mm(b[:, j * P:(j + 1) * P], col.broadcast_to([P, P]), IDENT, start=True, stop=True)
                    last.then_inc(filled, 1)
                norm(4 + l, ("h", l))
                for c in range(6):
                    by_token(("z", l, c), ("z", l, c), HEAD0 if c == 0 else BANK,
                             None if c else transposed((("h", l), "xT")))
                pe.wait_ge(qk_ready, 1 + 2 * l + 1)
                to_channels(("cT", l), 2, lambda u: [(P, (2 * j + m) * P, CN[:, m, (2 * u + j) * P:(2 * u + j + 1) * P])
                                                     for j in range(2 - u) for m in range(TT)])
                wait_taken(pe, ("cT", l, 1))
                wq = raw(pe, ("up_q", l)).rearrange("p (k n) -> p k n", k=2)
                for c, (n0, n) in enumerate(((0, 512), (512, 256))):
                    for m in range(TT):
                        product(("up", l, c, m), lambda k: CT[:, k, m * P:(m + 1) * P],
                                wq[:, :, n0:n0 + n], n, 2)
                w = raw(pe, ("up_kv", l))
                for c in range(2):
                    for m in range(TT):
                        product(("up", l, 2 + c, m), lambda k: CT3[:, m * P:(m + 1) * P],
                                w[:, c * BANK:(c + 1) * BANK].unsqueeze(1), BANK, 1)
                pe.wait_ge(qk_ready, 1 + 2 * l + 2)
                to_channels(("mobaT", l), 4, lambda u: [
                    (P, (2 * j + m) * P, ZB[:, m, ZQ + (2 * u + j) * P:ZQ + (2 * u + j + 1) * P])
                    for j in range(2) for m in range(TT)])
                wait_taken(pe, ("mobaT", l, 2))
                wait_taken(pe, ("mobaT", l, 3))
                attention(("moba", l), PAIR_STEPS, 16 + 16 * l, exps,
                          lambda g, c, m: QKT2[64 * c:64 * c + 64, g, m * P:(m + 1) * P],
                          lambda g, c, w_: QKT2[64 * c:64 * c + 64, 4 + g, 0:w_],
                          lambda b_, c, k: EE2[:, b_, c, k * P:(k + 1) * P], PT2,
                          lambda g, c, k: ZB[:, k, ZV + (2 * g + c) * 64:ZV + (2 * g + c + 1) * 64], 64)
                pe.wait_ge(mla_ready, l + 1)
                to_channels(("mlaT", l), 8, lambda u: [(96, (2 * j + m) * P, QK[:, m, (2 * u + j) * 96:(2 * u + j + 1) * 96])
                                                       for j in range(2) for m in range(TT)])
                wait_taken(pe, ("mlaT", l, 6))
                wait_taken(pe, ("mlaT", l, 7))
                attention(("mla", l), PAIR_STEPS, 24 + 16 * l, exps,
                          lambda g, c, m: QKT2[0:96, 2 * g + c, m * P:(m + 1) * P],
                          lambda g, c, w_: QKT2[0:96, 8 + 2 * g + c, 0:w_],
                          lambda b_, c, k: EE2[:, b_, c, k * P:(k + 1) * P], PT2,
                          lambda g, c, k: KV[:, k, (2 * g + c) * P + 64:(2 * g + c + 1) * P], 64, halves=False)
                pe.wait_ge(o_ready, 2 + l)
                to_channels(("yT", l), 4, lambda u: [(P, (2 * j + m) * P, O2[:, m, (2 * u + j) * P:(2 * u + j + 1) * P])
                                                     for j in range(2) for m in range(TT)])
                for c in range(2):
                    by_token(("w_out", l, c), ("wo2", l, c), BANK, None if c else transposed(("yT", l)))

        @block.vector
        def _(v):
            V = Chain(v, v_done)
            d = nc.vector
            ev = emptied["v"]
            tt_, ts, stt = d.tensor_tensor, d.tensor_scalar, d.scalar_tensor_tensor
            MUL, ADD, SUB = ALU.mult, ALU.add, ALU.subtract

            def norm(n, tag, gain=None, shift=None):
                v.wait_ge(squares, n + 1)
                V(ts(s_ms, s_ss, 1.0 / D, 1e-6, MUL, ADD), mean_square)
                v.wait_ge(inverse_rms, n + 1)
                V(ts(XN[:, 0, :], X[:, 0, :], s_rs[:, 0:1], None, MUL))
                V(ts(XN[:, 1, :], X[:, 1, :], s_rs[:, 1:2], None, MUL), xn_ready)

            lows, x_lows = [0], [0]

            def low(n=1):
                for g in range(lows[0], min(lows[0] + n, len(halves.split))):
                    whole = raw(v, halves.split[g])
                    n_ = whole.shape[1]
                    v.wait_ge(high_ready, g + 1)
                    V(tt_(WLM[g % PAIRS][:, 0:n_], whole, WHM[g % PAIRS][:, 0:n_].bitcast(F32), SUB), low_ready)
                    lows[0] = g + 1

            def gemm(tiles, evacuate, ahead=True):
                for c in range(tiles):
                    split = ahead or c < tiles - 1
                    if split:
                        low()
                    evacuate(c)
                    if split:
                        low()

            def x_out(tag, gain=None, shift=None):
                for u in range(4):
                    b = take(v, tag + (u,))
                    x_lows[0] += 1
                    v.wait_ge(x_high, x_lows[0])
                    if gain is None:
                        d2 = slice(2 * u, 2 * u + 2)
                        V(tt_(XTL[:, d2, :], b.rearrange("p (g t) -> p g t", g=2), XTH[:, d2, :].bitcast(F32), SUB), ev)
                        continue
                    for k in range(2):
                        i = 2 * u + k
                        src = b[:, k * T:(k + 1) * T]
                        to = ev if k else None
                        if shift is None:
                            V(stt(XTL[:, i, :], src, gain(i), XTH[:, i, :].bitcast(F32), MUL, SUB), to)
                        else:
                            V(ts(XT[:, i, :], src, gain(i), shift(i), MUL, ADD))
                            V(tt_(XTL[:, i, :], XT[:, i, :], XTH[:, i, :].bitcast(F32), SUB), to)

            def add_rows(name, ahead):
                def one(c):
                    for m in range(TT):
                        b = take(v, name + (c, m))
                        x = X[:, m, c * BANK:(c + 1) * BANK]
                        V(tt_(x, x, b, ADD), ev)
                gemm(2, one, ahead)

            def head_sums(l, step, ss, groups, width, to=None):
                v.wait_ge(qk_squares, 3 * l + step - 1)
                V(d.reduce_sum(s_qk[:, 0:groups], ss, AX))
                V(ts(s_qk[:, 0:groups], s_qk[:, 0:groups], 1.0 / width, 1e-6, MUL, ADD), qk_sums)
                v.wait_ge(qk_roots, 3 * l + step)
                V(d.reciprocal(s_qk[:, 0:groups], s_qk[:, 0:groups]), to)

            def attention(tag, steps, base, ss, ee, at, add, scale_in, scale_max, between=None):
                def masked(i):
                    g, m = steps[i]
                    w = (m + 1) * P
                    b = take(v, (tag, "scores", i)).rearrange("p (c k) -> p c k", c=2)[:, :, 0:w]
                    if i >= 2:
                        v.wait_ge(exps, base + i - 1)
                    x = ss[:, i % 2, :, 0:w]
                    if scale_in is None:
                        V(tt_(x, b, add(g, w), ADD), ev)
                    else:
                        V(stt(x, b, scale_in, add(g, w), MUL, ADD), ev)
                    V(d.tensor_reduce(s_nm[:, i % 2, :], x, AX, ALU.max, negate=True),
                      maxima if scale_max is None else None)
                    if scale_max is not None:
                        V(ts(s_nm[:, i % 2, :], s_nm[:, i % 2, :], scale_max, None, MUL), maxima)

                masked(0)
                for i, (g, m) in enumerate(steps):
                    if i + 1 < len(steps):
                        masked(i + 1)
                    w = (m + 1) * P
                    v.wait_ge(exps, base + i + 1)
                    if at is None:
                        if i >= 2:
                            wait_taken(v, (tag, "values", i - 2))
                        V(d.reciprocal(s_rcb[:, i % 2, :], s_sm[:, i % 2, :]), weights)
                        if between:
                            between(i)
                        continue
                    V(d.reciprocal(s_rcb[:, i % 2, :], s_sm[:, i % 2, :]))
                    V(tt_(s_rcb[:, i % 2, 1:2], s_rcb[:, i % 2, 1:2], s_lam[:, 2:3], MUL))
                    if i >= 2:
                        v.wait_ge(filled, PLAN.filled((tag, "weightsT", i - 2)))
                    a = at[:, i % 2, 0:w]
                    V(ts(a, ee[:, i % 2, 0, 0:w], s_rcb[:, i % 2, 0:1], None, MUL))
                    V(stt(a, ee[:, i % 2, 1, 0:w], s_rcb[:, i % 2, 1:2], a, MUL, ADD), weights)

            b = take(v, "params")
            V(d.tensor_copy(PRM[:, 0:NROWS[0]], b[:, 0:NROWS[0]]))
            V(d.tensor_copy(PRM[:, P:P + NROWS[1]], b[:, P:P + NROWS[1]]), ev)
            PAR = PRM[:, :]

            def prms(name, n, i=0):
                return PAR[:, PARAM_AT[name] + i:PARAM_AT[name] + i + n]

            lam_ = prms("e_lru_lambda", 4)
            V(ts(s_l[0], lam_, -1.0, None, MUL))
            V(tt_(s_l[1], s_l[0], lam_, ALU.max), lam_abs)
            V(ts(s_omka, prms("e_k_a", 4), -1.0, 1.0, MUL, ADD))
            V(ts(s_subg, prm("o_subln"), 1.0 - LAMBDA_INIT, None, MUL))
            norm(0, "mix0")
            low(PAIRS)
            x_out(("mix0", "xT"), lambda i: prm("e_ln_mix", i))

            def softplus():
                v.wait_ge(lam_exp, 1)
                V(ts(s_l[3], s_l[2], 2.0, None, ADD))
                V(d.reciprocal(s_l[3], s_l[3]))
                V(tt_(s_l[3], s_l[2], s_l[3], MUL))
                V(tt_(s_l[4], s_l[3], s_l[3], MUL))
                V(ts(s_l[5], s_l[4], 1.0 / 19, None, MUL))
                for k in (17, 15, 13, 11, 9, 7, 5, 3):
                    V(stt(s_l[5], s_l[5], 1.0 / k, s_l[4], ADD, MUL))
                V(stt(s_l[5], s_l[5], 1.0, s_l[3], ADD, MUL))
                V(ts(s_l[0], s_l[0], 0.0, 8.0, ALU.max, MUL))
                V(stt(s_l[5], s_l[5], 16.0, s_l[0], MUL, ADD))

            def rotations():
                v.wait_ge(small_loaded, 16 * N_SMALL)
                V(d.tensor_copy(s_posf, POS[:, :]))
                for i, (at, w, f) in enumerate(((0, 8, "freq1"), (8, 8, "freq1"), (16, 16, "freq2"), (32, 16, "freq2"))):
                    V(ts(s_ang[:, at:at + w], cst(f), s_posf[:, i:i + 1], None, MUL))
                r, rc, k_ = s_ang[:, 0:48], s_ang[:, 48:96], s_turn
                V(ts(k_, r, 1.0 / TWO_PI, None, MUL))
                V(ts(k_, k_, 12582912.0, None, ADD))
                V(ts(k_, k_, 12582912.0, None, SUB))
                c1, c2 = 6.28125, 0.0019350051879882812
                for c in (c1, c2, TWO_PI - c1 - c2):
                    V(stt(r, k_, -c, r, MUL, ADD))
                V(ts(rc, r, math.pi / 2, None, ADD))
                V(ts(k_, rc, math.pi, -TWO_PI, ALU.is_gt, MUL))
                V(tt_(rc, rc, k_, ADD))
                V(ts(s_ang, s_ang, 3.1415925, -3.1415925, ALU.min, ALU.max), angles)

            def lambdas():
                lams = G_LAM.rearrange("p (a b w) -> p a b w", a=2, b=2)
                prod = SXG[:, 0:128].rearrange("p (a w) -> p a w", a=2)
                V(tt_(prod, lams[:, :, 0, :], lams[:, :, 1, :], MUL))
                V(d.reduce_sum(s_lam[:, 0:2], prod, AX), lam_dots)

            def lambda_difference():
                v.wait_ge(lam_exps, 1)
                V(tt_(s_lam[:, 2:3], s_lam[:, 1:2], s_lam[:, 0:1], SUB))
                V(ts(s_lam[:, 2:3], s_lam[:, 2:3], -LAMBDA_INIT, None, ADD))

            def convolution(c):
                if c == 0:
                    v.wait_ge(rows_cleared, 3)
                    wait_taken(v, ("w_in", 1))
                V(ts(XC[:, c, :], LX[:, c, 0:T], prm("e_conv_w", c), prm("e_conv_b", c), MUL, ADD))
                for j in range(1, CONV):
                    V(stt(XC[:, c, :], LX[:, c, j:j + T], prm("e_conv_w", 4 * j + c), XC[:, c, :], MUL, ADD),
                      conv_ready if (c, j) == (3, CONV - 1) else None)

            def projections(c):
                if c >= 2:
                    b = take(v, ("w_in", 2 * c)).rearrange("p (c t) -> p c t", c=2)
                    V(d.tensor_copy(RW[:, 4 * c - 8:4 * c - 6, 1:T + 1], b), ev)
                if c == 0:
                    softplus()
                elif c == 1:
                    rotations()
                elif c == 2:
                    lambdas()
                elif c == 4:
                    lambda_difference()
                if 1 <= c <= 4:
                    convolution(c - 1)

            gemm(6, projections)
            wait_taken(v, ("w_in", 9))
            V(tt_(PS, RW[:, :, 0:T], RW[:, :, 1:T + 1], SUB))
            for c in range(CT_RW):
                V(stt(PS[:, c, :], PS[:, c, :], prm("e_shift_mu", c), RW[:, c, 1:T + 1], MUL, ADD),
                  shifted if c == CT_RW - 1 else None)
            def lru_decay():
                wait_taken(v, ("lru_gate", 3))
                v.wait_ge(filled, PLAN.filled(("dY", LEVELS[-1], 3)))
                for c in range(4):
                    V(ts(T1[:, c, :], GA[:, c, :], s_l[5][:, c:c + 1], None, MUL), decay_arg if c == 3 else None)

            def lru_reciprocal(i):
                V(d.reciprocal(T1[:, 2 * i:2 * i + 2, :], T1[:, 2 * i:2 * i + 2, :]))

            def lru_scan():
                v.wait_ge(root_ready, 1)
                V(tt_(T2, T2, GX, MUL))
                V(tt_(T2, T2, XC, MUL))
                for c in range(4):
                    V(d.tensor_tensor_scan(T1[:, c, :], GA[:, c, :], T2[:, c, :], 0.0, MUL, ADD))
                V(tt_(YT[:, 0:4, :], T1, LG, MUL), lru_done)

            wait_taken(v, ("lora", 3))
            V(ts(TMP, TMP, -math.exp(-0.5), None, MUL))
            for c in range(4):
                V(d.tensor_tensor_scan(CW[:, c, :], cst("restart"), TMP[:, c, :], 0.0, MUL, ADD))
            V(tt_(EPX, CW, TMP, SUB), cum_ready)
            for u in range(2):
                b = take(v, ("gate_g", u)).rearrange("p (c t) -> p c t", c=2)
                V(d.tensor_copy(GG[:, 2 * u:2 * u + 2, :], b), ev)
            for c in range(4):
                V(ts(KK[:, c, :], PS[:, 4 + c, :], prm("e_k_k", c), None, MUL))
            V(tt_(TMP, KK, KK, MUL), key_squares)
            wait_taken(v, ("key_norm", 1))
            V(ts(KN, KN, 1e-12, None, ALU.max))
            V(d.reciprocal(KN, KN))
            V(tt_(KK, KK, KN, MUL))
            for c in range(4):
                V(ts(TMP[:, c, :], KB[:, c, :], prm("e_k_a", c), s_omka[:, c:c + 1], MUL, ADD))
            V(tt_(PS[:, 4:8, :], PS[:, 4:8, :], TMP, MUL))
            for c in range(4):
                V(stt(TMP[:, c, :], PS[:, c, :], prm("e_r_k", c), PS[:, 4 + c, :], MUL, MUL),
                  key_squares if c == 3 else None)
            v.wait_ge(exps_ready, 1)
            V(tt_(QR[:, :, 0, :], KK, EPX, MUL))
            V(tt_(QR[:, :, 1, :], PS[:, 0:4, :], EP, MUL))
            V(tt_(KB, KB, KK, MUL))
            V(tt_(KB, KB, EN, MUL))
            V(d.tensor_copy(s_pl, EP.rearrange("p c (k t) -> p c k t", t=HALF)[:, :, :, HALF - 1]))
            V(tt_(KT, PS[:, 4:8, :], EN, MUL), chunk_ops)
            for u in range(2):
                b = take(v, ("bonus", u)).rearrange("p (c t) -> p c t", c=2)
                V(tt_(BON[:, 2 * u:2 * u + 2, :], b, PS[:, 8 + 2 * u:10 + 2 * u, :], MUL), ev)
            for u in (1, 3, 5):
                V(d.tensor_copy((TMK, TMT, TMV)[u // 2][:, 1, :], take(v, ("by_token", u))), ev)
            pair = CST[:, WHERE["before_same"][0]:WHERE["before_same"][0] + T]
            for u in range(8):
                i = 2 * u
                b = take(v, ("AB", u)).rearrange("p (h w t) -> p h w t", h=2, w=2)
                V(tt_(YI[:, i:i + 2, :], b[:, :, 0, :], bc(cst("join1_up"), 1, [P, 2, P]), MUL))
                V(tt_(B1T[:, i:i + 2, :], b[:, :, 1, :], bc(cst("until_same"), 1, [P, 2, P]), MUL), ev)
                b = take(v, ("CB", u)).rearrange("p (h t) -> p h t", h=2)
                V(tt_(CB2[:, i:i + 2, :], b, bc(pair, 1, [P, 2, T]), MUL), ev)

            def join(s, gr):
                q = slice(4 * gr, 4 * gr + 4)
                V(tt_(AM[:, q, :], AL[:, q, :], bc(cst(f"join{s}"), 1, [P, 4, P]), MUL), inverse_in)

            for u in range(4):
                q = slice(4 * u, 4 * u + 4)
                b = take(v, ("A", u)).rearrange("p (h t) -> p h t", h=4)
                V(tt_(AL[:, q, :], b, bc(cst("after_same"), 1, [P, 4, P]), MUL), ev)
                V(tt_(XI[:, q, :], AL[:, q, :], bc(cst("join1"), 1, [P, 4, P]), MUL))
                V(tt_(XI[:, q, :], bc(IDENT, 1, [P, 4, P]), XI[:, q, :], SUB))
                V(tt_(YI[:, q, :], bc(IDENT, 1, [P, 4, P]), YI[:, q, :], SUB))
                join(LEVELS[0], u)
            for n, s in enumerate(LEVELS):
                for gr in range(4):
                    q = slice(4 * gr, 4 * gr + 4)
                    b = take(v, ("dY", s, gr)).rearrange("p (h t) -> p h t", h=4)
                    V(tt_(YI[:, q, :], YI[:, q, :], b, SUB), ev)
                    if s < LEVELS[-1]:
                        b = take(v, ("dX", s, gr)).rearrange("p (h t) -> p h t", h=4)
                        V(tt_(XI[:, q, :], XI[:, q, :], b, SUB), ev)
                        join(LEVELS[n + 1], gr)
            lru_decay()
            for c in range(4):
                r = slice(64 * (c % 2), 64 * (c % 2) + 64)
                if c:
                    b = take(v, ("Z", c))
                    wait_taken(v, ("ZV", c // 2))
                    V(tt_(ZS[r, :], b[r, :], ZVAL[r, c // 2, :], ADD), ev)
                V(ts(SAN[r, :], take(v, ("SA", c))[r, :], -1.0, None, MUL), ev)
                if c < 3:
                    b = take(v, ("dS", c)).rearrange("p (h t) -> p h t", h=4)
                    V(tt_(DS, b, bc(cst("same_head"), 1, [P, 4, P]), MUL), ev)
                    if c:
                        V(tt_(DS, DS, ST[c % 2], ADD))
                    V(tt_(ST[(c + 1) % 2], DS, bc(s_pl[:, :, c], 2, [P, 4, P]), MUL), state_ready)
                if c == 0:
                    v.wait_ge(decay_ready, 1)
                    V(ts(T1, T2, 1.0, None, ADD))
                    lru_reciprocal(0)
                elif c == 1:
                    lru_reciprocal(1)
                    V(stt(T2, T2, 2.0, T1, MUL, MUL), root_arg)
                elif c == 2:
                    lru_scan()
            wait_taken(v, ("O", 3))
            V(tt_(OO, OO, OVAL, ADD))
            heads = OO.rearrange("p m (h w) -> p (m h) w", w=64)
            sq = GSQ.rearrange("p m (h w) -> p (m h) w", w=64)
            V(d.reduce_sum(s_mean, heads, AX))
            V(ts(s_mean, s_mean, 1.0 / 64, None, MUL))
            V(tt_(heads, heads, bc(s_mean, 2, [P, 16, 64]), SUB))
            V(tt_(sq, heads, heads, MUL))
            V(d.reduce_sum(s_var, sq, AX))
            V(ts(s_var, s_var, 1.0 / 64, 64e-5, MUL, ADD), gn_var)

            def y_lows(c):
                x_lows[0] += 1
                v.wait_ge(x_high, x_lows[0])
                V(tt_(XTL[:, c:c + 4, :], YT[:, c:c + 4, :], XTH[:, c:c + 4, :].bitcast(F32), SUB), y_low)

            y_lows(0)
            v.wait_ge(gn_root, 1)
            V(d.reciprocal(s_var, s_var))
            V(tt_(heads, heads, bc(s_var, 2, [P, 16, 64]), MUL), gn_ready)
            for u in range(2):
                b = take(v, ("OT", u))
                for j in range(2):
                    c = 2 * u + j
                    V(ts(YT[:, 4 + c, :], b[:, j * T:(j + 1) * T], prm("e_gn_w", c), prm("e_gn_b", c), MUL, ADD),
                      ev if j else None)
            V(tt_(YT[:, 4:8, :], YT[:, 4:8, :], BON, ADD))
            V(tt_(YT[:, 4:8, :], YT[:, 4:8, :], GG, MUL), yT_ready)
            y_lows(4)
            add_rows(("w_out",), True)

            norm(1, "ffn")
            x_out(("ffn", "xT"), lambda i: prm("e_ln_ffn", i))
            v.wait_ge(bias_loaded, 16)
            V(tt_(BIAS[:, :, :], BIAS[:, :, :], bc(cst("future"), 1, [P, NE, T]), ADD))
            ada_done = [0]

            def ada(n):
                for step in range(ada_done[0], min(ada_done[0] + n, ADA * KD)):
                    i, k = divmod(step, KD)
                    acc = ADAS[i % 4]
                    if k == 0:
                        v.wait_ge(ada_loaded[i % 2], 16 * (i // 2 + 1))
                        v.wait_ge(c_silu, 1)
                        if i >= 4:
                            v.wait_ge(filled, PLAN.filled(("mod", i - 4)))
                        V(ts(acc, ADAW[i % 2][:, 0, :], s_cc[:, 0:1], None, MUL))
                    else:
                        V(stt(acc, ADAW[i % 2][:, k, :], s_cc[:, k:k + 1], acc, MUL, ADD), ada_sums if k == KD - 1 else None)
                    ada_done[0] = step + 1

            for c in range(len(FFN_CHUNKS) + 1):
                w = FFN_CHUNKS[c][1] if c < len(FFN_CHUNKS) else 0
                if w:
                    for _ in range(2):
                        ada(4)
                        low()
                if c:
                    pw = FFN_CHUNKS[c - 1][1]
                    for m in range(TT):
                        b = take(v, ("hT", c - 1, m))[:, 0:pw].rearrange("p (k s) -> p k s", s=P)
                        x_lows[0] += 1
                        v.wait_ge(x_high, x_lows[0])
                        V(tt_(HTL[:, m, 0:pw // P, :], b, HTH[:, m, 0:pw // P, :].bitcast(F32), SUB), ev)
                if w:
                    ada(4)
                    low()
                    ada(4)
                    for m in range(TT):
                        b = take(v, ("Up", c, m))
                        wait_taken(v, ("G", c, m))
                        V(tt_(HH[:, m, 0:w], SIL[:, m, 0:w], b[:, 0:w], MUL), ev)
                    low()
                for n in range(2 if c else 0):
                    for m in range(TT):
                        x = X[:, m, n * BANK:(n + 1) * BANK]
                        V(tt_(x, x, take(v, ("Dn", c - 1, n, m)), ADD), ev)
                    low()
            wait_taken(v, ("mod", ADA - 1))
            V(tt_(s_mod, s_mod, prms("b_ada_2", 48), ADD))

            norm(2, "mix1")
            x_out(("mix1", "xT"), lambda i: prm("o_ln_mix", i))

            def qkv_step(c):
                V(d.tensor_copy(QKVB[:, 1, c * BANK:(c + 1) * BANK], take(v, ("qkv", c, 1))), ev)
                if c >= 4:
                    v.wait_ge(diff_squares, c - 3)
                    V(d.reduce_sum(s_qk[:, 32 * (c - 4):32 * (c - 3)], SQ[:, c - 4, :].rearrange("p (g w) -> p g w", w=64),
                                   AX))

            gemm(QKV // BANK, qkv_step)
            V(ts(s_qk, s_qk, 1.0 / 64, 1e-6, MUL, ADD), qk_sums)
            v.wait_ge(qk_roots, 1)
            V(d.reciprocal(s_qk, s_qk), diff_scales)
            diff_heads(V, tt_, 0, qk_ready)
            for u in range(1, 8, 2):
                b = take(v, ("qkT", u)).rearrange("p (g t) -> p g t", g=2)
                V(d.tensor_copy(QKT[:, 2 * u:2 * u + 2, :], b), ev)
            attention("diff", DIFF_STEPS, 0, SS, EE, AT,
                      lambda g, w: bc(cst("future")[:, T - w:T], 1, [P, 2, w]), None, 0.125)
            v.wait_ge(o_squares, 1)
            V(d.reduce_sum(s_mean, SQ[:, 0, :].rearrange("p (g w) -> p g w", w=P), AX))
            V(ts(s_mean, s_mean, 1.0 / P, 1e-6, MUL, ADD), o_sums)
            v.wait_ge(o_roots, 1)
            V(d.reciprocal(s_mean, s_mean))
            oh = OA.rearrange("p m (g w) -> p (m g) w", w=P)
            V(tt_(oh, oh, bc(s_mean, 2, [P, 16, P]), MUL), o_ready)
            x_out(("oT",), lambda i: s_subg)
            add_rows(("w_o",), False)

            norm(3, "moe")
            for u in (1, 3):
                b = take(v, ("moe", "xT", u))
                for k in range(2):
                    V(ts(XT[:, 2 * u + k, :], b[:, k * T:(k + 1) * T], prm("o_ln_ffn", 2 * u + k), None, MUL),
                      ev if k else None)
            v.wait_ge(moe_gain_loaded, 16)
            V(tt_(XN[:, :, :], XN[:, :, :], bc(GMOE, 1, [P, TT, D]), MUL), moe_in)
            b = take(v, "router")
            V(d.tensor_copy(s_lg, b[:, 0:TT * NE].rearrange("p (m e) -> p m e", m=TT)), ev)
            for m in range(TT):
                V(d.max(s_mx[:, m, :], s_lg[:, m, :]))
                V(d.max_index(IX[:, m, :], s_mx[:, m, :], s_lg[:, m, :]))
            V(d.tensor_copy(s_ixf, IX[:, :, :]))
            V(tt_(s_w[:, 0:TT], s_mx[:, :, 1], s_mx[:, :, 0], SUB), gap_ready)
            v.wait_ge(gap_exp, 1)
            V(ts(s_w[:, 0:TT], s_w[:, TT:2 * TT], 1.0, None, ADD))
            V(d.reciprocal(s_w[:, 0:TT], s_w[:, 0:TT]))
            V(tt_(s_w[:, TT:2 * TT], s_w[:, TT:2 * TT], s_w[:, 0:TT], MUL))
            for m in range(TT):
                for k in range(2):
                    V(ts(s_oh[:, k, m, :], cst("count8"), s_ixf[:, m, k:k + 1], None, ALU.is_equal))
            V(tt_(s_mask, s_oh[:, 0], s_oh[:, 1], ADD), choices)
            for m in range(TT):
                c8 = s_comb[:, m, 0:NE]
                V(ts(c8, s_oh[:, 0, m, :], s_w[:, m:m + 1], None, MUL))
                V(stt(c8, s_oh[:, 1, m, :], s_w[:, TT + m:TT + m + 1], c8, MUL, ADD))
            b = take(v, "places")
            p8 = s_place[:, :, 0:NE]
            V(ts(p8, b[:, 0:TT * NE].rearrange("p (m e) -> p m e", m=TT), 1.0, None, ADD))
            V(ts(s_over, b[:, 2 * NE:3 * NE], float(P), None, ALU.is_gt), ev)
            V(tt_(p8, p8, s_mask, MUL))
            V(ts(p8, p8, -1.0, None, ADD))
            V(d.tensor_tensor_scan(s_rank, cst("ones")[:, 0:NE], s_over, 0.0, MUL, ADD))
            V(d.memset(s_item, 0.0))
            V(d.tensor_copy(s_item[:, 0:NE], cst("count8")))
            V(ts(s_item[:, 12:13], s_rank[:, NE - 1:NE], float(NE), None, ADD))
            V(tt_(s_rank, s_rank, s_over, SUB))
            for j in range(ITEMS - NE):
                V(ts(s_pick, s_rank, float(j), None, ALU.is_equal))
                V(tt_(s_pick, s_pick, s_over, MUL))
                V(tt_(s_junk, s_pick, cst("count8"), MUL))
                V(d.reduce_sum(s_item[:, NE + j:NE + j + 1], s_junk, AX))
                for table in (s_place, s_comb):
                    V(tt_(s_lg, table[:, :, 0:NE], bc(s_pick, 1, [P, TT, NE]), MUL))
                    V(d.reduce_sum(table[:, :, NE + j], s_lg, AX))
                V(ts(s_place[:, :, NE + j], s_place[:, :, NE + j], float(-P), None, ADD))
            V(d.tensor_copy(ITEM[0:1, :], s_item[0:1, :]), items_ready)
            v.sem_inc(m_emptied["v"], E_BY["v"])
            v.sem_inc(w_low, N_SPLIT)
            me = m_emptied["v"]
            with v.Fori(0, v.value_load(ITEM[0:1, 12:13], min_val=NE, max_val=ITEMS)) as it:
                v.wait_ge(me, it * E_BY["v"] + E_BY["v"])
                for m in range(TT):
                    place, comb = s_place[:, m, bass.ds(it, 1)], s_comb[:, m, bass.ds(it, 1)]
                    ts(PCMB[:, m, :], cst("count128"), place, comb, ALU.is_equal, MUL).then_inc(m_combs, 1)
                    ts(PSEL[:, m, :], cst("count128"), place, None, ALU.is_equal).then_inc(m_places, 1)

                def low_parts(*halves):
                    for q in halves:
                        if q < N_SPLIT:
                            v.wait_ge(w_high, it * N_SPLIT + (q + 1))
                            tt_(WL[q % E_SPLITS], half(q % E_SLOTS), WH[q % E_SPLITS].bitcast(F32), SUB)\
                                .then_inc(w_low, 1)

                low_parts(0, 1)
                for u in range(2):
                    b = e_take(v, it, ("XG", u)).rearrange("p (k s) -> p k s", k=4)
                    v.wait_ge(xg_high, it * 2 + (u + 1))
                    k4 = slice(4 * u, 4 * u + 4)
                    tt_(XGL[:, k4, :], b, XGH[:, k4, :].bitcast(F32), SUB).then_inc(me, 1)
                low_parts(2)
                ahead = E_SPLITS
                for c in range(EC + 1):
                    if c < EC:
                        low_parts(ahead, ahead + 1)
                        ahead += 2
                    if c:
                        b = e_take(v, it, ("hT", c - 1)).rearrange("p (k s) -> p k s", k=4)
                        v.wait_ge(xh_high, it * EC + c)
                        tt_(HTL[:, (c - 1) % 2], b, HTH[:, (c - 1) % 2].bitcast(F32), SUB).then_inc(me, 1)
                    if c < EC:
                        low_parts(ahead)
                        b = e_take(v, it, ("Up", c))
                        e_wait_taken(v, it, ("G", c))
                        tt_(HH[:, c % 2, :], SIL[:, c % 2, :], b, MUL).then_inc(me, 1)
                        low_parts(ahead + 1)
                        ahead += 2
                    if c:
                        low_parts(ahead, ahead + 1)
                        ahead += 2
                v.wait_ge(down_done, it * (2 * EC) + 4 * EC)
                d.tensor_copy(YE[:, BANK:], banks[E_BANKS + 1][:, :]).then_inc(ye_ready["v"], 1)
                for m in range(TT):
                    for n in range(2):
                        x = X[:, m, n * BANK:(n + 1) * BANK]
                        tt_(x, x, e_take(v, it, ("Y", m, n)), ADD).then_inc(me, 1)
            V(d.memset(s_junk, 0.0), v_ended)
            v.sem_inc(x_ready, 1)

            for l in range(DEPTH2):
                norm(4 + l, ("h", l))
                V(stt(s_gs, s_mod[:, 24 * l + 8:24 * l + 16], 1.0, prms("norm_g_2", 8, 8 * l), ADD, MUL), mod_ready)
                for n in range(2):
                    V(d.tensor_copy(GATE[:, n * BANK:(n + 1) * BANK], take(v, ("mod_gate", l, n))), ev)
                if l == 0:
                    low(PAIRS)
                x_out((("h", l), "xT"), lambda i: s_gs[:, i:i + 1], lambda i: s_mod[:, 24 * l + i:24 * l + i + 1])

                def z_out(c):
                    c0, n = (0, HEAD0) if c == 0 else (HEAD0 + (c - 1) * BANK, BANK)
                    V(d.tensor_copy(ZB[:, 1, c0:c0 + n], take(v, ("z", l, c, 1))[:, 0:n]), ev)

                def z_step(c):
                    z_out(c)
                    if c >= 4:
                        if c == 4:
                            head_sums(l, 3, MSQ.rearrange("p m (g w) -> p (m g) w", w=64), 32, 64)
                        head_scale(V, tt_, ZB[:, c - 4, ZQ:ZQ + 1024], c - 4, G_MOBA[l], 32, 64)
                    if c != 1:
                        return
                    v.wait_ge(qk_squares, 3 * l + 1)
                    V(ts(s_qk[:, 0:2], s_qk[:, 0:2], 1.0 / 256, 1e-6, MUL, ADD))
                    V(ts(s_qk[:, 2:4], s_qk[:, 2:4], 1.0 / 128, 1e-6, MUL, ADD), qk_sums)
                    v.wait_ge(qk_roots, 3 * l + 2)
                    V(d.reciprocal(s_qk[:, 0:4], s_qk[:, 0:4]))
                    for m in range(TT):
                        V(ts(CN[:, m, 0:256], ZB[:, m, 0:256], s_qk[:, m:m + 1], None, MUL))
                        V(ts(CN[:, m, 256:384], ZB[:, m, ZC:ZC + 128], s_qk[:, 2 + m:3 + m], None, MUL),
                          qk_ready if m else None)

                gemm(6, z_step, ahead=False)
                V(d.memset(s_junk, 0.0), qk_ready)
                for c, (dst, n) in enumerate(((QK[:, 1, 0:512], 512), (QK[:, 1, 512:768], 256),
                                              (KV[:, 1, 0:512], 512), (KV[:, 1, 512:1024], 512))):
                    V(d.tensor_copy(dst, take(v, ("up", l, c, 1))[:, 0:n]), ev)

                def mla_keys(i):
                    if i == 0:
                        wait_taken(v, ("up", l, 3, 0))
                        keys = QK[:, :, 768:1536].rearrange("p m (h w) -> p m h w", w=96)
                        V(d.tensor_copy(keys[:, :, :, 0:64],
                                        KV.rearrange("p m (h w) -> p m h w", w=P)[:, :, :, 0:64]))
                        V(d.tensor_copy(keys[:, :, :, 64:96], bc(ZB[:, :, ZR:ZR + 32], 2, [P, TT, 8, 32])), qk_built)
                    elif i == 2:
                        head_sums(l, 4, SQ2.rearrange("p m (g w) -> p (m g) w", w=96), 32, 96, mla_scales)
                    elif i in (4, 5):
                        low()

                for u in (1, 3):
                    b = take(v, ("mobaT", l, u)).rearrange("p (g t) -> p g t", g=2)
                    V(d.tensor_copy(QKT2[:, 2 * u:2 * u + 2, :], b), ev)
                attention(("moba", l), PAIR_STEPS, 16 + 16 * l, SS2, EE2, None,
                          lambda g, w: BIAS[:, 2 * g:2 * g + 2, T - w:T], 0.125, None, mla_keys)
                for u in range(1, 8, 2):
                    b = take(v, ("mlaT", l, u)).rearrange("p (g t) -> p g t", g=2)
                    V(d.tensor_copy(QKT2[0:96, 2 * u:2 * u + 2, :], b[0:96]), ev)
                attention(("mla", l), PAIR_STEPS, 24 + 16 * l, SS2, EE2, None,
                          lambda g, w: bc(cst("future")[:, T - w:T], 1, [P, 2, w]), None, 96 ** -0.5)
                v.wait_ge(gate_silu, l + 1)
                wait_taken(v, (("mla", l), "values", 7))
                V(tt_(O2[:, :, 0:512], O2[:, :, 0:512], ZB[:, :, ZG:ZG + 512], MUL))
                V(tt_(O2[:, :, 512:1024], O2[:, :, 512:1024], ZB[:, :, ZGB:ZGB + 512], MUL), o_ready)
                x_out(("yT", l))

                def gated_sum(c):
                    for m in range(TT):
                        tmp = SQ2[:, 0, 0:BANK]
                        V(tt_(tmp, GATE[:, c * BANK:(c + 1) * BANK], take(v, ("w_out", l, c, m)), MUL), ev)
                        x = X[:, m, c * BANK:(c + 1) * BANK]
                        V(tt_(x, x, tmp, ADD), x_ready if (c, m) == (1, 1) else None)

                gemm(2, gated_sum)

        @block.scalar
        def _(act):
            A = Chain(act, a_done)
            f = nc.scalar.activation
            ea = emptied["a"]

            def norm(n, tag, gain, shift=None, between=None):
                wait_x(act, n)
                if n:
                    act.wait_ge(mean_square, n)
                A(f(XN[:, 0, :], X[:, 0, :], ACT.Square, accum_out=s_ss[:, 0:1]))
                A(f(XN[:, 1, :], X[:, 1, :], ACT.Square, accum_out=s_ss[:, 1:2]), squares)
                if between:
                    between()
                if tag != "moe":
                    act.wait_ge(filled, PLAN.filled((tag, "xT", 3)))
                    return x_out((tag, "xT"), gain, shift)
                for u in (0, 2):
                    b = take(act, (tag, "xT", u))
                    for k in range(2):
                        A(f(XT[:, 2 * u + k, :], b[:, k * T:(k + 1) * T], ACT.Copy, scale=gain(2 * u + k)),
                          ea if k else None)

            def x_out(tag, gain=None, shift=None):
                for u in range(4):
                    b = take(act, tag + (u,))
                    if gain is None:
                        A(f(XTH[:, 2 * u:2 * u + 2, :], b.rearrange("p (g t) -> p g t", g=2), ACT.Copy), x_high)
                        continue
                    for k in range(2):
                        i = 2 * u + k
                        A(f(XTH[:, i, :], b[:, k * T:(k + 1) * T], ACT.Copy if shift is None else ACT.Identity,
                            bias=0.0 if shift is None else shift(i), scale=gain(i)), x_high if k else None)

            highs = [0]

            def high(n=1):
                for g in range(highs[0], min(highs[0] + n, len(halves.split))):
                    whole = raw(act, halves.split[g])
                    if g >= PAIRS:
                        wait_used(act, halves.split[g - PAIRS])
                    A(f(WHM[g % PAIRS][:, 0:whole.shape[1]], whole, ACT.Copy), high_ready)
                    highs[0] = g + 1

            def gemm(tiles, evacuate=None, ahead=True):
                for c in range(tiles):
                    split = ahead or c < tiles - 1
                    if split:
                        high()
                    if evacuate:
                        evacuate(c)
                    if split:
                        high()

            def attention(tag, steps, base, ss, ee, pt, out, scale, vd, between=None):
                n_c = 1 if vd == P else 2

                def exponentials(i):
                    g, m = steps[i]
                    w = (m + 1) * P
                    act.wait_ge(maxima, base + i + 1)
                    if i >= 2:
                        act.wait_ge(weights, base + i - 1)
                        act.wait_ge(filled, PLAN.filled((tag, "weightsT", i - 2)))
                    for c in range(2):
                        A(f(ee[:, i % 2, c, 0:w], ss[:, i % 2, c, 0:w], ACT.Exp, bias=s_nm[:, i % 2, c:c + 1],
                            scale=scale, accum_out=s_sm[:, i % 2, c:c + 1]), exps if c else None)

                def transposes(i):
                    m = steps[i][1]
                    b = take(act, (tag, "weightsT", i))
                    if i >= 2:
                        act.wait_ge(filled, PLAN.filled((tag, "values", i - 2)))
                    src = b[:, 0:n_c * T].rearrange("p (c k q) -> p c k q", c=n_c, k=2)[:, :, 0:m + 1, :]
                    if n_c == 1:
                        A(f(pt[:, i % 2, 0, 0:m + 1, :], src[:, 0], ACT.Copy), ea)
                    else:
                        A(f(pt[:, i % 2, :, 0:m + 1, :], src, ACT.Copy), ea)

                def values(i):
                    g, m = steps[i]
                    b = take(act, (tag, "values", i))
                    if n_c == 1:
                        A(f(out[:, m, g * P:(g + 1) * P], b[:, 0:P], ACT.Copy), ea)
                    else:
                        act.wait_ge(weights, base + i + 1)
                        for c in range(2):
                            A(f(out(m, 2 * g + c), b[:, c * 64:(c + 1) * 64], ACT.Copy,
                                scale=s_rcb[:, i % 2, c:c + 1]), ea if c else None)

                exponentials(0)
                for i in range(len(steps) + 1):
                    if i + 1 < len(steps):
                        exponentials(i + 1)
                    if i < len(steps):
                        transposes(i)
                    if i:
                        values(i - 1)
                    if between:
                        between(i)

            def transposed(name, units, dst, rows=P):
                for u in range(0, units, 2):
                    b = take(act, name + (u,)).rearrange("p (g t) -> p g t", g=2)
                    A(f(dst[0:rows, 2 * u:2 * u + 2, :], b[0:rows], ACT.Copy), ea)

            def root(n, ready, to, a):
                act.wait_ge(ready, n)
                A(f(a, a, ACT.Sqrt), to)

            norm(0, "mix0", lambda i: prm("e_ln_mix", i), between=lambda: high(PAIRS))
            act.wait_ge(rows_cleared, 3)

            def projections(c):
                for u in {0: (0, 1), 1: (2, 3), 5: ()}.get(c, (2 * c + 1,)):
                    b = take(act, ("w_in", u)).rearrange("p (c t) -> p c t", c=2)
                    if u < 2:
                        A(f(LX[:, 2 * u:2 * u + 2, CONV - 1:CONV - 1 + T], b, ACT.Copy), ea)
                    elif u < 4:
                        A(f(LG[:, 2 * u - 4:2 * u - 2, :], b, ACT.Gelu_apprx_tanh), ea)
                    else:
                        A(f(RW[:, 2 * u - 8:2 * u - 6, 1:T + 1], b, ACT.Copy), ea)
                if c == 0:
                    act.wait_ge(lam_abs, 1)
                    A(f(s_l[2], s_l[1], ACT.Exp, scale=-1.0), lam_exp)
                elif c == 3:
                    A(f(s_cc, PRM[:, PARAM_AT["c_2"]:PARAM_AT["c_2"] + KD], ACT.Silu), c_silu)
                    act.wait_ge(lam_dots, 1)
                    A(f(s_lam[:, 0:2], s_lam[:, 0:2], ACT.Exp), lam_exps)
                    act.wait_ge(angles, 1)
                    A(f(s_ang, s_ang, ACT.Sin), sines)

            gemm(6, projections)
            for u in range(4):
                b = take(act, ("lru_gate", u))
                for j in range(2):
                    c = 2 * (u % 2) + j
                    dst, bias = ((GA, "e_gate_a_b"), (GX, "e_gate_x_b"))[u // 2]
                    A(f(dst[:, c, :], b[:, j * T:(j + 1) * T], ACT.Sigmoid, bias=prm(bias, c)), ea if j else None)
            act.wait_ge(shifted, 1)
            A(f(TWX[0:64, :], PS[0:64, 12, :], ACT.Tanh), lora_in)
            A(f(SXG, PS[:, 13, :], ACT.Sigmoid), lora_in)
            for u in range(4):
                b = take(act, ("lora", u))
                for j in range(2):
                    c = 2 * (u % 2) + j
                    dst, bias = ((TMP, "e_w0"), (KB, "e_a0"))[u // 2]
                    A(f(dst[:, c, :], b[:, j * T:(j + 1) * T], ACT.Sigmoid, bias=prm(bias, c)), ea if j else None)
            act.wait_ge(cum_ready, 1)
            A(f(EP, CW, ACT.Exp))
            A(f(EN, CW, ACT.Exp, scale=-1.0))
            A(f(EPX, EPX, ACT.Exp), exps_ready)
            for u in range(2):
                b = take(act, ("key_norm", u)).rearrange("p (c t) -> p c t", c=2)
                A(f(KN[:, 2 * u:2 * u + 2, :], b, ACT.Sqrt), ea)
            for u in (0, 2, 4):
                A(f((TMK, TMT, TMV)[u // 2][:, 0, :], take(act, ("by_token", u)), ACT.Copy), ea)
            for s in LEVELS:
                for gr in range(4):
                    b = take(act, ("U", s, gr)).rearrange("p (h t) -> p h t", h=4)
                    A(f(UU[:, 4 * gr:4 * gr + 4, :], b, ACT.Copy), ea)
            for h in range(NE):
                A(f(ROWB[h // 4][:, h % 4, :], take(act, ("bias", h))[:, 0:BIAS_ROW], ACT.Copy),
                  ea)
            for tt in range(TT):
                A(f(ZVAL[:, tt, :], take(act, ("ZV", tt)), ACT.Copy), ea)
                A(f(OVAL[:, tt, :], take(act, ("OV", tt)), ACT.Copy), ea)
            act.wait_ge(decay_arg, 1)
            A(f(T2, T1, ACT.Tanh))
            A(f(GA, T1, ACT.Exp, scale=-1.0), decay_ready)
            for c in range(4):
                r = slice(64 * (c % 2), 64 * (c % 2) + 64)
                A(f(OO[r, c // 2, :], take(act, ("O", c))[r, :], ACT.Copy), ea)
                if c == 1:
                    root(1, root_arg, root_ready, T2)
            act.wait_ge(lru_done, 1)
            A(f(XTH[:, 0:4, :], YT[:, 0:4, :], ACT.Copy), x_high)
            root(1, gn_var, gn_root, s_var)
            act.wait_ge(yT_ready, 1)
            A(f(XTH[:, 4:8, :], YT[:, 4:8, :], ACT.Copy), x_high)
            gemm(2)

            norm(1, "ffn", lambda i: prm("e_ln_ffn", i))
            act.wait_ge(bias_saved, 32)
            for c in range(len(FFN_CHUNKS) + 1):
                w = FFN_CHUNKS[c][1] if c < len(FFN_CHUNKS) else 0
                if w:
                    high(2)
                    for m in range(TT):
                        b = take(act, ("G", c, m))
                        if c:
                            wait_taken(act, ("Up", c - 1, m))
                        A(f(SIL[:, m, 0:w], b[:, 0:w], ACT.Silu), ea)
                if c:
                    pw = FFN_CHUNKS[c - 1][1]
                    for m in range(TT):
                        b = take(act, ("hT", c - 1, m))[:, 0:pw].rearrange("p (k s) -> p k s", s=P)
                        A(f(HTH[:, m, 0:pw // P, :], b, ACT.Copy), x_high)
                    for i in (2 * c - 2, 2 * c - 1):
                        b = take(act, ("mod", i))
                        for j in range(4):
                            A(f(ADAJ, b[:, j * P:(j + 1) * P], ACT.Copy, accum_out=s_mod[:, 4 * i + j:4 * i + j + 1]),
                              ea if j == 3 else None)
                high((2 if w else 0) + (2 if c else 0))

            norm(2, "mix1", lambda i: prm("o_ln_mix", i))

            def qkv_step(c):
                A(f(QKVB[:, 0, c * BANK:(c + 1) * BANK], take(act, ("qkv", c, 0)), ACT.Copy), ea)
                if c == 4:
                    wait_taken(act, ("qkv", 3, 1))
                if c >= 4:
                    A(f(SQ[:, c - 4, :], QKVB[:, c - 4, 0:2048], ACT.Square), diff_squares)

            gemm(QKV // BANK, qkv_step)
            root(1, qk_sums, qk_roots, s_qk)
            transposed(("qkT",), 8, QKT)
            attention("diff", DIFF_STEPS, 0, SS, EE, PT, OA, 0.125, P)
            A(f(SQ[:, 0, :], OA.rearrange("p m c -> p (m c)"), ACT.Square), o_squares)
            root(1, o_sums, o_roots, s_mean)
            x_out(("oT",), lambda i: s_subg)
            gemm(2, ahead=False)

            norm(3, "moe", lambda i: prm("o_ln_ffn", i))
            act.wait_ge(gap_ready, 1)
            A(f(s_w[:, TT:2 * TT], s_w[:, 0:TT], ACT.Exp), gap_exp)
            act.wait_ge(items_ready, 1)
            act.sem_inc(m_emptied["a"], E_BY["a"])
            me = m_emptied["a"]
            with act.Fori(0, act.value_load(ITEM[0:1, 12:13], min_val=NE, max_val=ITEMS)) as it:
                def high_parts(*halves):
                    for q in halves:
                        if q >= N_SPLIT:
                            continue
                        kind, c_, j = E_TILES[q - E_SPLITS]
                        ahead = 1 if q >= E_SPLITS else 0
                        if kind == "Dn":
                            act.wait_ge(down_done, it * (2 * EC) + (ahead * 2 * EC + 2 * c_ + j + 1))
                        elif j:
                            act.wait_ge(m_filled, it * E_N + (ahead * E_N + E_PLAN.index[(kind, c_)] + 1))
                        else:
                            n = sum(t[0] != "Dn" and t[2] == 0 for t in E_TILES[:q - E_SPLITS + 1])
                            act.wait_ge(m_first, it * (2 * EC) + n)
                        f(WH[q % E_SPLITS], e_tile(act, it, E_TILES[q]), ACT.Copy).then_inc(w_high, 1)

                high_parts(0, 1, 2)
                for u in range(2):
                    b = e_take(act, it, ("XG", u)).rearrange("p (k s) -> p k s", k=4)
                    f(XGH[:, 4 * u:4 * u + 4, :], b, ACT.Copy).then_inc(xg_high, 1)
                b = e_take(act, it, "PCT")[:, 0:T].rearrange("p (m t) -> p m t", m=TT)
                f(PCT, b, ACT.Copy).then_inc(me, 1)
                ahead = E_SPLITS
                for c in range(EC + 1):
                    if c < EC:
                        high_parts(ahead, ahead + 1)
                        ahead += 2
                        b = e_take(act, it, ("G", c))
                        if c >= 2:
                            e_wait_taken(act, it, ("Up", c - 2))
                        f(SIL[:, c % 2, :], b, ACT.Silu).then_inc(me, 1)
                    if c:
                        b = e_take(act, it, ("hT", c - 1)).rearrange("p (k s) -> p k s", k=4)
                        if c >= 3:
                            act.wait_ge(down_done, it * (2 * EC) + (2 * EC + 2 * (c - 2)))
                        f(HTH[:, (c - 1) % 2], b, ACT.Copy).then_inc(xh_high, 1)
                    if c < EC:
                        high_parts(ahead, ahead + 1)
                        ahead += 2
                    if c:
                        high_parts(ahead, ahead + 1)
                        ahead += 2
                act.wait_ge(down_done, it * (2 * EC) + 4 * EC)
                f(YE[:, 0:BANK], banks[E_BANKS][:, :], ACT.Copy).then_inc(ye_ready["a"], 1)

            for l in range(DEPTH2):
                norm(4 + l, ("h", l), lambda i: s_gs[:, i:i + 1], lambda i: s_mod[:, 24 * l + i:24 * l + i + 1],
                     between=lambda: (high(PAIRS) if l == 0 else None, act.wait_ge(mod_ready, l + 1)))

                def z_out(c):
                    c0, n = (0, HEAD0) if c == 0 else (HEAD0 + (c - 1) * BANK, BANK)
                    A(f(ZB[:, 0, c0:c0 + n], take(act, ("z", l, c, 0))[:, 0:n], ACT.Copy), ea)

                def z_step(c):
                    z_out(c)
                    if c == 4:
                        wait_taken(act, ("z", l, 3, 1))
                        A(f(MSQ, ZB[:, :, ZQ:ZQ + 1024], ACT.Square), qk_squares)
                        root(3 * l + 3, qk_sums, qk_roots, s_qk[:, 0:32])
                    if c != 1:
                        return
                    wait_taken(act, ("z", l, 0, 1))
                    for i, (c0, n, m) in enumerate(((0, 256, 0), (0, 256, 1), (ZC, 128, 0), (ZC, 128, 1))):
                        A(f(SQ2[:, 0, 0:n], ZB[:, m, c0:c0 + n], ACT.Square, accum_out=s_qk[:, i:i + 1]),
                          qk_squares if i == 3 else None)
                    root(3 * l + 2, qk_sums, qk_roots, s_qk[:, 0:4])

                gemm(6, z_step, ahead=False)
                b = take(act, ("cT", l, 0))
                for k in range(2):
                    A(f(CT[:, k, :], b[:, k * T:(k + 1) * T], ACT.Copy, scale=prm("mla_q_norm_g_2", 2 * l + k)),
                      ea if k else None)
                A(f(CT3, take(act, ("cT", l, 1))[:, 0:T], ACT.Copy, scale=prm("mla_kv_norm_g_2", l)), ea)
                for c, (dst, n) in enumerate(((QK[:, 0, 0:512], 512), (QK[:, 0, 512:768], 256),
                                              (KV[:, 0, 0:512], 512), (KV[:, 0, 512:1024], 512))):
                    A(f(dst, take(act, ("up", l, c, 0))[:, 0:n], ACT.Copy), ea)

                def mla_squares(i):
                    if i == 0:
                        act.wait_ge(qk_built, l + 1)
                        A(f(SQ2, QK, ACT.Square), qk_squares)
                    elif i == 2:
                        root(3 * l + 4, qk_sums, qk_roots, s_qk[:, 0:32])
                    elif i in (4, 5):
                        high()

                transposed(("mobaT", l), 4, QKT2)
                attention(("moba", l), PAIR_STEPS, 16 + 16 * l, SS2, EE2, PT2,
                          lambda m, h: O2[:, m, 512 + h * 64:512 + (h + 1) * 64], 1.0, 64, mla_squares)
                for g0 in (ZG, ZGB):
                    A(f(ZB[:, :, g0:g0 + 512], ZB[:, :, g0:g0 + 512], ACT.Silu), gate_silu if g0 == ZGB else None)
                transposed(("mlaT", l), 8, QKT2, 96)
                attention(("mla", l), PAIR_STEPS, 24 + 16 * l, SS2, EE2, PT2,
                          lambda m, h: O2[:, m, h * 64:(h + 1) * 64], 96 ** -0.5, 64)
                x_out(("yT", l))
                gemm(2)


def packed(inputs):
    rows = []
    for part in (PARAM_ROWS, PARAM_ROWS_2):
        a = np.concatenate([np.asarray(inputs[n]).reshape(-1, P) for n, _ in part])
        rows.append(a)
    each = [inputs["o_q_norm"][0], inputs["o_k_norm"][0]]
    for l in range(DEPTH2):
        each += [inputs["mla_q_g_2"][l], inputs["mla_k_g_2"][l]]
    for l in range(DEPTH2):
        each += [inputs["moba_q_g_2"][l], inputs["moba_k_g_2"][l]]
    each += [inputs[n][0] for n in ("o_lambda_q1", "o_lambda_k1", "o_lambda_q2", "o_lambda_k2")]
    return [("rows0", rows[0]), ("rows1", rows[1]), ("gains", np.concatenate([np.asarray(a) for a in each])),
            ("lora", np.concatenate([np.asarray(inputs["e_w2"])[0], np.asarray(inputs["e_a2"])[0]])),
            ("pos", np.stack([np.asarray(inputs["positions"])[0], np.asarray(inputs["positions_2"])[0]])
             .reshape(2, TT, P))]


def kernel(**inputs):
    import concourse.bacc as bacc
    from concourse.bass_utils import run_bass_kernel_spmd

    nc = bacc.Bacc("TRN2", target_bir_lowering=False, num_devices=1)
    arrays, aps = {}, {}
    given = [(n, np.ascontiguousarray(inputs[n])) for n in NAMES] + packed(inputs)
    for name, a in given + [("const_table", CONSTS), ("bucket_table", bucket_table())]:
        arrays[f"in_{name}"] = a
        aps[name] = nc.dram_tensor(f"in_{name}", a.shape, mybir.dt.from_np(a.dtype), kind="ExternalInput").ap()
    out = nc.dram_tensor("out_0", (1, T, D), F32, kind="ExternalOutput").ap()
    build(nc, aps, aps["const_table"], aps["bucket_table"], out)
    r = run_bass_kernel_spmd(nc, [arrays], core_ids=[0])
    return r.results[0]["out_0"]
```
